# Optimizing a Trainium2 kernel written in Bass

```python
import jax, jax.numpy as jnp
from jax import lax
import numpy as np
import math

D_MODEL = 2048
BATCH = 1
SEQ = 256
DEPTH = 1

GLA_HEADS = 4
GLA_KEY_DIM = D_MODEL // 2
GLA_VALUE_DIM = D_MODEL
GLA_HEAD_K = GLA_KEY_DIM // GLA_HEADS
GLA_HEAD_V = GLA_VALUE_DIM // GLA_HEADS
GK_RANK = 16
GATE_LOGIT_NORMALIZER = 16.0
CHUNK = 64
CONV_WIDTH = D_MODEL
CONV_K = 3
FFN_HIDDEN = ((8 * D_MODEL + 3 * 256 - 1) // (3 * 256)) * 256
EPS = 1e-6

IN_SPLITS = [
    GLA_KEY_DIM,
    GLA_KEY_DIM,
    GLA_VALUE_DIM,
    GLA_VALUE_DIM,
    GK_RANK,
    CONV_WIDTH,
    CONV_WIDTH,
    CONV_WIDTH,
    D_MODEL,
    D_MODEL,
]
IN_COLS = int(sum(IN_SPLITS))
SPLIT_IDX = [int(i) for i in np.cumsum(IN_SPLITS)[:-1]]


def rmsnorm(x, w):
    xf = x.astype(jnp.float32)
    y = xf * lax.rsqrt(jnp.mean(xf * xf, axis=-1, keepdims=True) + EPS)
    return (y * w.astype(jnp.float32)).astype(x.dtype)

def gla_chunked(q, k, v, log_g):
    b_, s, h, dk = q.shape
    dv = v.shape[-1]
    n = s // CHUNK
    f32 = jnp.float32

    def chunks(t):
        return t.astype(f32).reshape(b_, n, CHUNK, h, t.shape[-1]).transpose(1, 0, 3, 2, 4)

    qc = chunks(q) * (dk ** -0.5)
    kc = chunks(k)
    vc = chunks(v)
    gc = chunks(log_g)
    bcum = jnp.cumsum(gc, axis=3)
    b_last = bcum[..., -1:, :]
    q_dec = qc * jnp.exp(bcum)
    k_dec = kc * jnp.exp(-bcum)
    k_to_end = kc * jnp.exp(b_last - bcum)

    causal = jnp.tril(jnp.ones((CHUNK, CHUNK), dtype=bool))
    scores = jnp.einsum('nbhik,nbhjk->nbhij', q_dec, k_dec)
    scores = jnp.where(causal, scores, 0.0)
    o_intra = jnp.einsum('nbhij,nbhjv->nbhiv', scores, vc)

    def step(state, inp):
        q_d, k_e, v_n, decay = inp
        o_inter = jnp.einsum('bhik,bhkv->bhiv', q_d, state)
        state = state * decay[:, :, 0, :, None] + jnp.einsum('bhjk,bhjv->bhkv', k_e, v_n)
        return state, o_inter

    state0 = jnp.zeros((b_, h, dk, dv), f32)
    _, o_inter = lax.scan(step, state0, (q_dec, k_to_end, vc, jnp.exp(b_last)))
    o = o_intra + o_inter
    return o.transpose(1, 0, 3, 2, 4).reshape(b_, s, h, dv)

def causal_depthwise_conv(u, w):
    s = u.shape[1]
    up = jnp.pad(u, ((0, 0), (CONV_K - 1, 0), (0, 0)))
    return sum(up[:, j:j + s, :] * w[j] for j in range(CONV_K))

def hybrid_mixer(h, w_in, w_gk_up, b_gk_up, gla_norm_w, conv_w, w_out):
    b_, s, _ = h.shape
    proj = jnp.einsum('bsd,de->bse', h, w_in)
    (q, k, v, g_out, gk_low, gate_b, gate_c, xc, merge_a, merge_b) = jnp.split(proj, SPLIT_IDX, axis=-1)

    gk = jnp.einsum('bsr,rk->bsk', gk_low, w_gk_up) + b_gk_up
    log_g = jax.nn.log_sigmoid(gk.astype(jnp.float32)) / GATE_LOGIT_NORMALIZER
    o = gla_chunked(q.reshape(b_, s, GLA_HEADS, GLA_HEAD_K),
                    k.reshape(b_, s, GLA_HEADS, GLA_HEAD_K),
                    v.reshape(b_, s, GLA_HEADS, GLA_HEAD_V),
                    log_g.reshape(b_, s, GLA_HEADS, GLA_HEAD_K))
    o = rmsnorm(o, gla_norm_w).astype(h.dtype)
    y_a = (o * jax.nn.silu(g_out.reshape(b_, s, GLA_HEADS, GLA_HEAD_V))).reshape(b_, s, GLA_VALUE_DIM)

    y_b = gate_b * causal_depthwise_conv(gate_c * xc, conv_w)

    merged = jax.nn.sigmoid(merge_a) * y_a + jax.nn.sigmoid(merge_b) * y_b
    return jnp.einsum('bse,ed->bsd', merged, w_out)

def swiglu(h, w_gate_up, w_down):
    gu = jnp.einsum('bsd,df->bsf', h, w_gate_up)
    gate, up = jnp.split(gu, [FFN_HIDDEN], axis=-1)
    return jnp.einsum('bsf,fd->bsd', jax.nn.silu(gate) * up, w_down)

def first_inputs(seed: int = 0) -> dict:
    key = jax.random.key(seed)
    ks = jax.random.split(key, 12)
    f32 = jnp.float32
    nrm = lambda k, shape, scale: jax.random.normal(k, shape, f32) * scale
    return {
        "x": nrm(ks[0], (BATCH, SEQ, D_MODEL), 1.0),
        "mix_norm_w": 1.0 + nrm(ks[1], (DEPTH, D_MODEL), 0.02),
        "w_in": nrm(ks[2], (DEPTH, D_MODEL, IN_COLS), D_MODEL ** -0.5),
        "w_gk_up": nrm(ks[3], (DEPTH, GK_RANK, GLA_KEY_DIM), GK_RANK ** -0.5),
        "b_gk_up": nrm(ks[4], (DEPTH, GLA_KEY_DIM), 0.1),
        "gla_norm_w": 1.0 + nrm(ks[5], (DEPTH, GLA_HEAD_V), 0.02),
        "conv_w": nrm(ks[6], (DEPTH, CONV_K, CONV_WIDTH), CONV_K ** -0.5),
        "w_out": nrm(ks[7], (DEPTH, D_MODEL, D_MODEL), D_MODEL ** -0.5),
        "ffn_norm_w": 1.0 + nrm(ks[8], (DEPTH, D_MODEL), 0.02),
        "w_gate_up": nrm(ks[9], (DEPTH, D_MODEL, 2 * FFN_HIDDEN), D_MODEL ** -0.5),
        "w_down": nrm(ks[10], (DEPTH, FFN_HIDDEN, D_MODEL), FFN_HIDDEN ** -0.5),
        "final_norm_w": 1.0 + nrm(ks[11], (D_MODEL,), 0.02),
    }

def first_block(x, mix_norm_w, w_in, w_gk_up, b_gk_up, gla_norm_w, conv_w, w_out,
              ffn_norm_w, w_gate_up, w_down, final_norm_w):
    h = x
    for l in range(DEPTH):
        h = h + hybrid_mixer(rmsnorm(h, mix_norm_w[l]), w_in[l], w_gk_up[l], b_gk_up[l],
                             gla_norm_w[l], conv_w[l], w_out[l])
        h = h + swiglu(rmsnorm(h, ffn_norm_w[l]), w_gate_up[l], w_down[l])
    return rmsnorm(h, final_norm_w)


HYENA_WIDTH = 1024
CONV_WIDTH_2 = 3
FILTER_EMB_DIM = 33
FILTER_HIDDEN = 64
DECAY_TARGET = 1e-2
FAST_DECAY_PCT = 0.3
SLOW_DECAY_PCT = 1.5
DECAY_SHIFT = 0.05

N_HEADS = 8
QK_NOPE_DIM = 128
QK_ROPE_DIM = 64
V_HEAD_DIM = 128
Q_LORA_RANK = 512
KV_LORA_RANK = 256
ROPE_THETA = 10000.0
Q_BLOCK = 128

ATTN_WIDTH = N_HEADS * V_HEAD_DIM
MIX_WIDTH = HYENA_WIDTH + ATTN_WIDTH
IN_PROJ_WIDTH = 3 * HYENA_WIDTH + Q_LORA_RANK + KV_LORA_RANK + QK_ROPE_DIM

D_FF = 5632
NORM_EPS = 1e-6


def _rmsnorm(x, gain):
    xf = x.astype(jnp.float32)
    y = xf * lax.rsqrt(jnp.mean(xf * xf, axis=-1, keepdims=True) + NORM_EPS)
    return (y * gain.astype(jnp.float32)).astype(x.dtype)

def _dwconv_centred(x, w, b):
    k = w.shape[0]
    half = k // 2
    s = x.shape[1]
    xp = jnp.pad(x, ((0, 0), (half, half), (0, 0)))
    return sum(xp[:, j:j + s] * w[j] for j in range(k)) + b

def _position_features(L):
    t = jnp.linspace(0.0, 1.0, L, dtype=jnp.float32)[:, None]
    bands = (FILTER_EMB_DIM - 1) // 2
    w = 2.0 * math.pi * jnp.arange(L, dtype=jnp.float32) / L
    f = jnp.linspace(1e-4, bands - 1, bands, dtype=jnp.float32)
    ang = w[:, None] * f[None, :]
    return t, jnp.concatenate([t, jnp.cos(ang), -jnp.sin(ang)], axis=-1)

def _implicit_filters(t, z, w1, b1, fr1, w2, b2, fr2, w3):
    f32 = jnp.float32
    L = t.shape[0]
    h = jnp.sin(fr1.astype(f32) * (z @ w1.astype(f32) + b1.astype(f32)))
    h = jnp.sin(fr2.astype(f32) * (h @ w2.astype(f32) + b2.astype(f32)))
    h = h @ w3.astype(f32)
    max_decay = math.log(DECAY_TARGET) / FAST_DECAY_PCT
    min_decay = math.log(DECAY_TARGET) / SLOW_DECAY_PCT
    deltas = jnp.abs(jnp.linspace(min_decay, max_decay, HYENA_WIDTH, dtype=f32))
    window = jnp.exp(-t * deltas[None, :]) + DECAY_SHIFT
    h = h.reshape(L, 2, HYENA_WIDTH) * window[:, None, :]
    h_fwd, h_bwd = h[:, 0], h[:, 1]
    return jnp.concatenate([h_fwd, jnp.zeros((1, HYENA_WIDTH), f32), h_bwd[1:][::-1]], axis=0)

def _bidir_long_conv(u, k2, bias):
    L = u.shape[1]
    n = 2 * L
    uf = jnp.fft.rfft(u.astype(jnp.float32), n=n, axis=1)
    kf = jnp.fft.rfft(k2, n=n, axis=0)
    y = jnp.fft.irfft(uf * kf[None], n=n, axis=1)[:, :L]
    return (y + u.astype(jnp.float32) * bias.astype(jnp.float32)).astype(u.dtype)

def _rope(x, cos, sin):
    x1, x2 = jnp.split(x, 2, axis=-1)
    return x * cos + jnp.concatenate([-x2, x1], axis=-1) * sin

def _mla(c_q, c_kv, k_pe, q_norm_gain, w_uq, kv_norm_gain, w_ukv, cos, sin):
    B, S, _ = c_q.shape
    dqk = QK_NOPE_DIM + QK_ROPE_DIM
    q = (_rmsnorm(c_q, q_norm_gain) @ w_uq).reshape(B, S, N_HEADS, dqk)
    q_nope, q_pe = q[..., :QK_NOPE_DIM], q[..., QK_NOPE_DIM:]
    kv = (_rmsnorm(c_kv, kv_norm_gain) @ w_ukv).reshape(B, S, N_HEADS, QK_NOPE_DIM + V_HEAD_DIM)
    k_nope, v = kv[..., :QK_NOPE_DIM], kv[..., QK_NOPE_DIM:]
    q_pe = _rope(q_pe, cos[:, None, :], sin[:, None, :])
    k_pe = _rope(k_pe, cos, sin)
    q = jnp.concatenate([q_nope, q_pe], axis=-1)
    k = jnp.concatenate([k_nope, jnp.broadcast_to(k_pe[:, :, None, :], (B, S, N_HEADS, QK_ROPE_DIM))], axis=-1)
    scale = dqk ** -0.5
    nb = S // Q_BLOCK
    qb = q.reshape(B, nb, Q_BLOCK, N_HEADS, dqk).transpose(1, 0, 2, 3, 4)

    def attend(q_blk):
        s = jnp.einsum('bqhd,bkhd->bhqk', q_blk, k).astype(jnp.float32) * scale
        p = jax.nn.softmax(s, axis=-1).astype(v.dtype)
        return jnp.einsum('bhqk,bkhd->bqhd', p, v)

    o = lax.map(attend, qb)
    return o.transpose(1, 0, 2, 3, 4).reshape(B, S, ATTN_WIDTH)

def second_inputs(seed: int = 0) -> dict:
    key = jax.random.key(seed)
    ks = jax.random.split(key, 32)
    f32 = jnp.float32

    def nrm(k, shape, scale):
        return jax.random.normal(k, shape, f32) * scale

    def gain(k, n):
        return 1.0 + 0.05 * jax.random.normal(k, (DEPTH, n), f32)

    return {
        "x": nrm(ks[0], (BATCH, SEQ, D_MODEL), 1.0),
        "pre_mix_gain": gain(ks[1], D_MODEL),
        "w_in": nrm(ks[2], (DEPTH, D_MODEL, IN_PROJ_WIDTH), D_MODEL ** -0.5),
        "hyena_conv_w": nrm(ks[3], (DEPTH, CONV_WIDTH_2, 3 * HYENA_WIDTH), CONV_WIDTH_2 ** -0.5),
        "hyena_conv_b": nrm(ks[4], (DEPTH, 3 * HYENA_WIDTH), 0.02),
        "filt_w1": nrm(ks[5], (DEPTH, FILTER_EMB_DIM, FILTER_HIDDEN), FILTER_EMB_DIM ** -0.5),
        "filt_b1": nrm(ks[6], (DEPTH, FILTER_HIDDEN), 0.02),
        "filt_freq1": 1.0 + 0.1 * jax.random.normal(ks[7], (DEPTH, FILTER_HIDDEN), f32),
        "filt_w2": nrm(ks[8], (DEPTH, FILTER_HIDDEN, FILTER_HIDDEN), FILTER_HIDDEN ** -0.5),
        "filt_b2": nrm(ks[9], (DEPTH, FILTER_HIDDEN), 0.02),
        "filt_freq2": 1.0 + 0.1 * jax.random.normal(ks[10], (DEPTH, FILTER_HIDDEN), f32),
        "filt_w3": nrm(ks[11], (DEPTH, FILTER_HIDDEN, 2 * HYENA_WIDTH), FILTER_HIDDEN ** -0.5),
        "hyena_bias": nrm(ks[12], (DEPTH, HYENA_WIDTH), 0.5),
        "q_norm_gain": gain(ks[13], Q_LORA_RANK),
        "w_uq": nrm(ks[14], (DEPTH, Q_LORA_RANK, N_HEADS * (QK_NOPE_DIM + QK_ROPE_DIM)), Q_LORA_RANK ** -0.5),
        "kv_norm_gain": gain(ks[15], KV_LORA_RANK),
        "w_ukv": nrm(ks[16], (DEPTH, KV_LORA_RANK, N_HEADS * (QK_NOPE_DIM + V_HEAD_DIM)), KV_LORA_RANK ** -0.5),
        "hyena_out_gain": gain(ks[17], HYENA_WIDTH),
        "attn_out_gain": gain(ks[18], ATTN_WIDTH),
        "w_out": nrm(ks[19], (DEPTH, MIX_WIDTH, D_MODEL), MIX_WIDTH ** -0.5),
        "post_mix_gain": gain(ks[20], D_MODEL),
        "pre_ffn_gain": gain(ks[21], D_MODEL),
        "w_up": nrm(ks[22], (DEPTH, D_MODEL, 2 * D_FF), D_MODEL ** -0.5),
        "ffn_conv_w": nrm(ks[23], (DEPTH, CONV_WIDTH_2, D_FF), CONV_WIDTH_2 ** -0.5),
        "ffn_conv_b": nrm(ks[24], (DEPTH, D_FF), 0.02),
        "w_down": nrm(ks[25], (DEPTH, D_FF, D_MODEL), D_FF ** -0.5),
        "post_ffn_gain": gain(ks[26], D_MODEL),
    }

def second_block(x, pre_mix_gain, w_in, hyena_conv_w, hyena_conv_b, filt_w1, filt_b1, filt_freq1,
              filt_w2, filt_b2, filt_freq2, filt_w3, hyena_bias, q_norm_gain, w_uq, kv_norm_gain,
              w_ukv, hyena_out_gain, attn_out_gain, w_out, post_mix_gain, pre_ffn_gain, w_up,
              ffn_conv_w, ffn_conv_b, w_down, post_ffn_gain):
    B, S, _ = x.shape
    pos = jnp.arange(S, dtype=jnp.float32)
    inv_freq = 1.0 / (ROPE_THETA ** (jnp.arange(0, QK_ROPE_DIM, 2, dtype=jnp.float32) / QK_ROPE_DIM))
    ang = pos[:, None] * inv_freq[None, :]
    ang = jnp.concatenate([ang, ang], axis=-1)
    cos = jnp.cos(ang).astype(x.dtype)
    sin = jnp.sin(ang).astype(x.dtype)
    t, z = _position_features(S)

    h = x
    for l in range(DEPTH):
        xn = _rmsnorm(h, pre_mix_gain[l])
        proj = xn @ w_in[l]
        o1 = 3 * HYENA_WIDTH
        o2 = o1 + Q_LORA_RANK
        o3 = o2 + KV_LORA_RANK
        xh, c_q, c_kv, k_pe = proj[..., :o1], proj[..., o1:o2], proj[..., o2:o3], proj[..., o3:]

        xh = _dwconv_centred(xh, hyena_conv_w[l], hyena_conv_b[l])
        x0 = xh[..., :HYENA_WIDTH]
        x1 = xh[..., HYENA_WIDTH:2 * HYENA_WIDTH]
        v = xh[..., 2 * HYENA_WIDTH:]
        k2 = _implicit_filters(t, z, filt_w1[l], filt_b1[l], filt_freq1[l], filt_w2[l], filt_b2[l],
                               filt_freq2[l], filt_w3[l])
        y_hyena = x0 * _bidir_long_conv(x1 * v, k2, hyena_bias[l])

        y_attn = _mla(c_q, c_kv, k_pe, q_norm_gain[l], w_uq[l], kv_norm_gain[l], w_ukv[l], cos, sin)

        mixed = jnp.concatenate([_rmsnorm(y_hyena, hyena_out_gain[l]),
                                 _rmsnorm(y_attn, attn_out_gain[l])], axis=-1) @ w_out[l]
        h = h + _rmsnorm(mixed, post_mix_gain[l])

        hn = _rmsnorm(h, pre_ffn_gain[l])
        gu = hn @ w_up[l]
        g = _dwconv_centred(gu[..., :D_FF], ffn_conv_w[l], ffn_conv_b[l])
        u = gu[..., D_FF:]
        f = (jax.nn.gelu(g, approximate=True) * u) @ w_down[l]
        h = h + _rmsnorm(f, post_ffn_gain[l])
    return h


def setup_inputs(seed=0):
    out = dict(first_inputs(seed))
    for name, value in second_inputs(seed + 1).items():
        if name != "x":
            out[name + "_2"] = value
    return out


def reference(
    x, mix_norm_w, w_in, w_gk_up, b_gk_up, gla_norm_w, conv_w, w_out, ffn_norm_w, w_gate_up,
    w_down, final_norm_w, pre_mix_gain_2, w_in_2, hyena_conv_w_2, hyena_conv_b_2, filt_w1_2,
    filt_b1_2, filt_freq1_2, filt_w2_2, filt_b2_2, filt_freq2_2, filt_w3_2, hyena_bias_2,
    q_norm_gain_2, w_uq_2, kv_norm_gain_2, w_ukv_2, hyena_out_gain_2, attn_out_gain_2, w_out_2,
    post_mix_gain_2, pre_ffn_gain_2, w_up_2, ffn_conv_w_2, ffn_conv_b_2, w_down_2,
    post_ffn_gain_2,
):
    x = first_block(
        x, mix_norm_w, w_in, w_gk_up, b_gk_up, gla_norm_w, conv_w, w_out, ffn_norm_w, w_gate_up,
        w_down, final_norm_w,
    )
    return second_block(
        x, pre_mix_gain_2, w_in_2, hyena_conv_w_2, hyena_conv_b_2, filt_w1_2, filt_b1_2,
        filt_freq1_2, filt_w2_2, filt_b2_2, filt_freq2_2, filt_w3_2, hyena_bias_2,
        q_norm_gain_2, w_uq_2, kv_norm_gain_2, w_ukv_2, hyena_out_gain_2, attn_out_gain_2,
        w_out_2, post_mix_gain_2, pre_ffn_gain_2, w_up_2, ffn_conv_w_2, ffn_conv_b_2, w_down_2,
        post_ffn_gain_2,
    )


_drawn_inputs = setup_inputs


def setup_inputs(seed=0):
    import zlib

    import numpy as np

    out = dict(_drawn_inputs(seed))
    spreads = {}
    factors = {'b_gk_up': 2.764,
     'gla_norm_w': 5.776,
     'ffn_norm_w': 2.753,
     'hyena_conv_b_2': 2.846,
     'filt_b1_2': 3.19,
     'filt_b2_2': 2.746,
     'ffn_conv_b_2': 4.978}
    for name, (base, spread) in spreads.items():
        noise = np.random.default_rng([zlib.crc32(name.encode()), seed]).standard_normal(out[name].shape)
        drawn = base * np.exp(spread * noise) if base else spread * noise
        out[name] = __import__('jax').numpy.asarray(drawn.astype(out[name].dtype))
    for name, factor in factors.items():
        out[name] = (out[name] * factor).astype(out[name].dtype)
    return out
```

```python
from contextlib import ExitStack, contextmanager

import numpy as np

import concourse.bass as bass
from concourse import mybir

F32 = mybir.dt.float32
F32R = mybir.dt.float32r
ALU = mybir.AluOpType
ACT = mybir.ActivationFunctionType
AX = mybir.AxisListType

P = 128
D = 2048
S = 256
DT = D // P
EPS = 1e-6
FF = 5632
FT = FF // P
GROUPS = 2
GT = FT // GROUPS
KD = GT // 2
RAW = 4
SPLIT = 2
HEADS = 4
DK = 256
DV = 512
CH = 64
NCH = S // CH
RANK = 16

VEC = {}
_at = 0
for _name, _tiles in (
    ("mix_norm_w", 16), ("ffn_norm_w", 16), ("final_norm_w", 16), ("gla_norm_w", 4), ("b_gk_up", 8),
    ("conv_w", 48), ("pre_mix_gain", 16), ("hyena_conv_w", 72), ("hyena_conv_b", 24), ("hyena_bias", 8),
    ("q_norm_gain", 4), ("kv_norm_gain", 2), ("hyena_out_gain", 8), ("attn_out_gain", 8),
    ("post_mix_gain", 16), ("pre_ffn_gain", 16), ("ffn_conv_w", 132), ("ffn_conv_b", 44),
    ("post_ffn_gain", 16),
):
    VEC[_name] = _at
    _at += _tiles
NVEC = _at

U_QKV, N_QKV = 0, 33
U_CONV, N_CONV = 33, 64
U_OUT, N_OUT = 97, 32
U_WO = 129
U_FF1 = 145
FF_UNITS = 2 * GT + 2 * DT
T_FF1 = 145
FF_TILES = 2 * GT + DT


class Steps:

    def __init__(self, engine, sem):
        self.engine, self.sem, self.n, self.run = engine, sem, 0, 0

    def __call__(self, instruction):
        instruction.then_inc(self.sem, 1)
        self.n += 1
        return instruction

    def wait(self):
        self.engine.wait_ge(self.sem, self.n + self.run)

    @contextmanager
    def loop(self, count, per):
        with self.engine.Fori(0, count) as i:
            first, self.run = self.n, i * per
            yield i
            assert self.n - first == per, (self.n - first, per)
        self.n, self.run = first + count * per, 0


def k_blocks(u, run=0):
    if isinstance(run, int):
        u += run
    if u >= N_UNITS:
        return None
    if U_UK <= u < U_WO2:
        return 8
    inside = u - (U_FF2 if u >= U_FF2 else U_FF1)
    return KD if 0 <= inside < GROUPS * FF_UNITS and inside % FF_UNITS >= 2 * GT else DT


POOL_WO = 1 + 2 * DT
ROUNDER = 1.5 * 2.0 ** 23
TURN = (6.28125, float(np.float32(2 * np.pi - 6.28125)))
PI_BELOW = 3.1415925
GATE_NORM = 16.0
POOL_FF1 = POOL_WO + 2 + 4 * DT

HY = 1024
HT = HY // P
LQ, LKV = 512, 256
QT, KVT = LQ // P, LKV // P
NH = 8
ROPE = 64
QK_SCALE = (P + ROPE) ** -0.5
EMB, FILT = 33, 64
U_IN2 = U_FF1 + GROUPS * FF_UNITS
U_LAT = U_IN2 + 3 * HT
U_UQ = U_LAT + QT + KVT + 1
U_UK = U_UQ + 3
U_UV = U_UK + 2
U_WO2 = U_UV + 2
U_FF2 = U_WO2 + DT
N_UNITS = U_FF2 + GROUPS * FF_UNITS
T_IN2 = T_FF1 + GROUPS * FF_TILES
T_LAT = T_IN2 + 3 * HT
T_UQ = T_LAT + QT + KVT + 1
T_UK = T_UQ + 12
T_UV = T_UK + 8
T_WO2 = T_UV + 5
T_FF2 = T_WO2 + DT
V_IN2 = 3 * DT + FT
V_MIX = V_IN2 + DT
V_PRE = V_MIX + DT
V_FF2 = V_PRE + DT
G_FF2 = 2 * DT + 2 + FT
POOL_WO2 = POOL_FF1 + 1 + 2 * DT


def build_program(nc, d, out):
    ctx = ExitStack()
    with ctx:
        base = -(-nc.sbuf_base // 32) * 32
        used = {}

        def at(name, offset, shape, dt=F32):
            return nc.alloc_sbuf_tensor_at(name, shape, dt, offset=base + offset)

        KB = 1024
        raw = at("raw", 0, [P, RAW, 2048])
        w_hi = at("w_hi", 32 * KB, [P, SPLIT, 2048], F32R)
        w_lo = at("w_lo", 48 * KB, [P, SPLIT, 2048], F32R)
        h = at("h", 64 * KB, [P, DT, S])
        xa = at("xa", 80 * KB, [P, DT, 2 * S], F32R)
        misc = 112 * KB
        small = at("small", misc, [P, 2, S])
        tmp = at("tmp", misc + 2 * KB, [P, 4, S])
        rstd = at("rstd", misc + 6 * KB, [P, S])
        scale2 = at("scale2", misc + 7 * KB, [P, S])
        ssum = at("ssum", misc + 8 * KB, [P, S])
        vec = at("vec", misc + 9 * KB, [P, NVEC])
        ident = at("ident", misc + 11 * KB, [P, P])
        ones = at("ones", misc + 11 * KB + 512, [P, P])
        A = misc + 12 * KB
        qkv = at("qkv", A, [P, 32, S])
        q_s = at("q_s", A + 32 * KB, [P, 2, S])
        k_s = at("k_s", A + 34 * KB, [P, 2, S])
        ke_s = at("ke_s", A + 36 * KB, [P, 2, S])
        v_s = at("v_s", A + 38 * KB, [P, 4, S])
        v_tok = at("v_tok", A + 42 * KB, [CH, NCH, DV])
        ke_tok = at("ke_tok", A + 50 * KB, [CH, NCH, DK])
        state = at("state", A + 54 * KB, [P, 2, DV])
        sc = at("sc", A + 58 * KB, [CH, NCH, CH])
        e_b = at("e_b", A + 59 * KB, [P, 8, S])
        e_nb = at("e_nb", A + 67 * KB, [P, 8, S])
        e_end = at("e_end", A + 75 * KB, [P, 8, S])
        yb = qkv[:, 0:DT]
        xb = at("xb", A + 32 * KB, [P, DT, 2 * S], F32R)
        xf = at("xf", A + 32 * KB, [P, DT, S])
        sq = at("sq", A + 66 * KB, [P, S])
        ssum2 = at("ssum2", A + 65 * KB, [P, S])
        dec = at("dec", A + 83 * KB, [P, 2, NCH])
        sq_all = at("sq_all", A + 59 * KB, [P, DT, S])
        gkl = at("gkl", A + 59 * KB, [RANK, S])
        w_gk = at("w_gk", A + 75 * KB, [RANK, 8 * P])
        mask_s = at("mask_s", A + 83 * KB + 32, [CH, CH])
        reset = at("reset", A + 48 * KB, [P, S])
        hid = at("hid", A, [P, GT, 2 * S], F32R)
        xh = at("xh", A, [P, 3 * HT, S])
        q_n = at("q_n", A + 24 * KB, [P, NH, S])
        q_p = at("q_p", A + 32 * KB, [P, NH // 2, S])
        k_p = at("k_p", A + 44 * KB, [P, 1, S])
        k_n = at("k_n", A + 36 * KB, [P, NH, S])
        v2 = at("v2", A + 45 * KB, [P, 2, NH * P])
        cq_s = at("cq_s", A + 53 * KB, [P, QT, 2 * S], F32R)
        ckv_s = at("ckv_s", A + 61 * KB, [P, KVT, 2 * S], F32R)
        lat = at("lat", A + 65 * KB, [P, QT + KVT, S])
        rope = at("rope", A + 71 * KB, [P, 2, S])
        rot = at("rot", A + 73 * KB, [P, P])
        rstd1 = at("rstd1", A + 73 * KB + 512, [P, S])
        B = A + 74 * KB + 512
        qh = at("qh", B, [P, 2, S])
        kh = at("kh", B + 2 * KB, [P, 2, S])
        vh = at("vh", B + 4 * KB, [P, 2, 2 * P])
        qph = at("qph", B + 6 * KB, [P, S])
        peak = at("peak", B + 7 * KB, [P, 2, 2])
        rows = at("rows", B + 7 * KB + 32, [P, 2, 2])
        XA = 80 * KB
        prob = at("prob", XA + 16 * KB, [P, 2, 2, S])
        prob_t = at("prob_t", XA + 20 * KB, [P, 2, 2, S])
        w_f3 = at("w_f3", A + 53 * KB, [FILT, 2 * HY])
        window = at("window", A + 61 * KB, [P, 2, HY])
        f_in = at("f_in", XA + 16 * KB, [EMB, S])
        w_f1 = at("w_f1", XA + 17 * KB, [EMB, FILT])
        w_f2 = at("w_f2", XA + 17 * KB + 256, [FILT, FILT])
        f_col = at("f_col", XA + 17 * KB + 512, [P, 6])
        f_arg = at("f_arg", XA + 18 * KB, [FILT, S])
        f_turn = at("f_turn", XA + 19 * KB, [FILT, S])
        f_h = at("f_h", XA + 20 * KB, [FILT, 2, S])
        f_sum = at("f_sum", XA, [P, 2, HY])
        f_dif = at("f_dif", XA + 8 * KB, [P, 2, HY])
        u_tok = at("u_tok", XA + 16 * KB, [P, 2, HY])
        dft = at("dft", XA + 24 * KB, [P, 2, 2, S])
        idft = at("idft", XA + 28 * KB, [P, 2, 2, S])
        spec = at("spec", A + 53 * KB, [P, 2, 2, HY])
        k_spec = at("k_spec", B, [P, 2, 512])
        part = at("part", B + 4 * KB, [P, 2, 512])
        mix_f = at("mix_f", A + 53 * KB, [P, DT, S])
        pre_a = at("pre_a", A, [P, DT, S])
        pre_b = at("pre_b", A + 16 * KB, [P, DT, S])
        branch = at("branch", A + 60 * KB, [P, DT, S])
        r_post = at("r_post", A + 77 * KB, [P, S])
        mix_sq = at("mix_sq", B, [P, QT + KVT, S])
        mix_sq2 = at("mix_sq2", A + 32 * KB, [P, DT, S])
        late_sqs = at("late_sqs", A + 16 * KB, [P, DT, S])
        ff_out = at("ff_out", A + 44 * KB, [P, DT, S])
        sq2 = at("sq2", A + 76 * KB, [P, S])
        USED_TOP = A + 83 * KB + 288
        assert base + USED_TOP <= nc.sbuf_usable_end, (base + USED_TOP, nc.sbuf_usable_end)

        acc = ctx.enter_context(nc.psum_tensor("acc", [P, 4, 512], F32))
        aux = ctx.enter_context(nc.psum_tensor("aux", [P, 4, 512], F32))

        def sem(name):
            return ctx.enter_context(nc.semaphore(name))

        consts_loaded = sem("consts_loaded")
        x_loaded = [sem(f"x_loaded{g}") for g in range(4)]
        raw_loaded = [sem(f"raw_loaded{r}") for r in range(RAW)]
        hi_made = sem("hi_made")
        lo_made = sem("lo_made")
        hi_used = sem("hi_used")
        lo_used = sem("lo_used")
        small_made = sem("small_made")
        acc_free = sem("acc_free")
        op_f32 = sem("op_f32")
        op_hi = sem("op_hi")
        op_lo = sem("op_lo")
        gate_in = sem("gate_in")
        gate_out = sem("gate_out")
        sums_made = sem("sums_made")
        sums_done = sem("sums_done")
        var_made = sem("var_made")
        std_made = sem("std_made")
        dve_step = sem("dve_step")
        act_step = sem("act_step")
        pool_step = sem("pool_step")
        h_new = sem("h_new")
        staged = sem("staged")
        v_staged = sem("v_staged")
        turned = sem("turned")
        tok_made = sem("tok_made")
        scores_made = sem("scores_made")
        masked = sem("masked")
        delta_made = sem("delta_made")
        state_made = sem("state_made")
        o_made = sem("o_made")
        o_read = sem("o_read")
        o_squared = sem("o_squared")
        head_done = sem("head_done")
        act_settled = sem("act_settled")
        pe_settled = sem("pe_settled")
        gkl_made = sem("gkl_made")
        qkv_made = sem("qkv_made")
        gk_made = sem("gk_made")
        out_stored = sem("out_stored")

        (hy_ready, lat_f32, lat_squared, lat_summed, lat_norm, lat_hi, lat_lo, q_rope_in, rotated, roped, head_q, head_kv,
         attn_scores, attn_peak, attn_exp, attn_prob, attn_turned, attn_probt, attn_out, attn_read, filt_in, filt_arg, filt_sin, filt_made, filt_win, u_ready,
         u_turned, u_copied, spec_made, k_copied, spec_used, spec_ready, conv_made, conv_done, mix_squared, mix_summed, late_sq, late_sum, tables_loaded, filt_loaded, x1_made, fin_sum, stream_sq) = (sem(n) for n in (
            "hy_ready lat_f32 lat_squared lat_summed lat_norm lat_hi lat_lo q_rope_in rotated roped head_q head_kv attn_scores attn_peak attn_exp attn_prob attn_turned attn_probt attn_out attn_read filt_in filt_arg filt_sin filt_made filt_win u_ready u_turned u_copied spec_made k_copied spec_used spec_ready conv_made conv_done mix_squared mix_summed late_sq late_sum tables_loaded filt_loaded x1_made fin_sum stream_sq").split())

        def column(name, tile):
            return vec[:, bass.ds(VEC[name] + tile, 1)]

        def bank(t):
            return (t + 3) % 4

        block = ctx.enter_context(nc.Block())

        @block.sync
        def _(sp):
            sp.dma_start(vec[:], d["vec"]).then_inc(consts_loaded, 16)
            for g in range(4):
                sp.dma_start(h[:, 4 * g:4 * g + 4], d["x"][:, 4 * g:4 * g + 4]).then_inc(x_loaded[g], 16)

            def unit(u, run, src, index, width):
                if u >= RAW:
                    sp.wait_ge(lo_made, run + (u - (RAW - 1)))
                sp.dma_start(raw[:, u % RAW, 0:width], src[index]).then_inc(raw_loaded[u % RAW], 16)

            def load(u0, src, n, width):
                with sp.Fori(0, n // 4) as i:
                    for j in range(4):
                        unit(u0 + j, 4 * i, src, 4 * i + j, width)

            for u in range(5):
                unit(u, 0, d["w_in"], u, 2048)
            load(5, d["w_in"][5:], 124, 2048)
            load(U_WO, d["w_out"], 16, 2048)
            for g in range(GROUPS):
                load(U_FF1 + g * FF_UNITS, d["w_gate_up"][g], 2 * GT, 2048)
                load(U_FF1 + g * FF_UNITS + 2 * GT, d["w_down"][g], 2 * DT, KD * P)
            sp.wait_ge(op_lo, 2 * DT)
            sp.dma_start(rope[:], d["rope"]).then_inc(tables_loaded, 16)
            sp.dma_start(rot[:], d["rot"]).then_inc(tables_loaded, 16)
            load(U_IN2, d["w_in_2"], 3 * HT, 2048)
            for u in range(U_LAT, U_UQ):
                unit(u, 0, d["w_in_2"], u - U_IN2, 2048)
            for u in range(U_UQ, U_UK):
                unit(u, 0, d["w_uq"], u - U_UQ, 2048)
            for u in range(U_UK, U_WO2):
                unit(u, 0, d["w_ukv"], u - U_UK, 1024)
            sp.wait_ge(lo_used, U_UQ)
            sp.dma_start(dft[:], d["dft"]).then_inc(filt_loaded, 16)
            sp.dma_start(idft[:], d["idft"]).then_inc(filt_loaded, 16)
            for u in range(U_WO2, U_WO2 + 4):
                unit(u, 0, d["w_out_2"], u - U_WO2, 2048)
            sp.wait_ge(lo_used, U_WO2)
            sp.dma_start(w_f3[:], d["w_f3"]).then_inc(filt_loaded, 16)
            sp.dma_start(window[:], d["window"]).then_inc(filt_loaded, 16)
            sp.wait_ge(attn_read, NH + 1)
            sp.dma_start(f_in[:], d["f_in"]).then_inc(filt_loaded, 16)
            sp.dma_start(w_f1[:], d["w_f1"]).then_inc(filt_loaded, 16)
            sp.dma_start(w_f2[:], d["w_f2"]).then_inc(filt_loaded, 16)
            sp.dma_start(f_col[:], d["f_col"]).then_inc(filt_loaded, 16)
            load(U_WO2 + 4, d["w_out_2"][4:], 12, 2048)
            for g in range(GROUPS):
                load(U_FF2 + g * FF_UNITS, d["w_up"][g], 2 * GT, 2048)
                load(U_FF2 + g * FF_UNITS + 2 * GT, d["w_down_2"][g], 2 * DT, KD * P)
            for g in range(4):
                sp.wait_ge(fin_sum, g + 1)
                sp.dma_start(out[:, 4 * g:4 * g + 4], h[:, 4 * g:4 * g + 4]).then_inc(out_stored, 16)
            sp.wait_ge(out_stored, 64)

        @block.scalar
        def _(act):
            step = Steps(act, act_step)
            act.dma_start(ones[:], d["ones"]).then_inc(consts_loaded, 16)
            act.dma_start(ident[:], d["ident"]).then_inc(consts_loaded, 16)
            act.dma_start(w_gk[:], d["w_gk_up"]).then_inc(consts_loaded, 16)
            act.dma_start(mask_s[:], d["mask"]).then_inc(consts_loaded, 16)
            act.dma_start(reset[:], d["reset"]).then_inc(consts_loaded, 16)

            def settle():
                act.sem_inc(act_settled, 1)

            def split(u, run=0):
                if k_blocks(u, run) is None:
                    return
                kt = k_blocks(u, run)
                act.wait_ge(raw_loaded[u % RAW], run * 4 + 16 * (u // RAW + 1))
                if u >= SPLIT:
                    act.wait_ge(hi_used, run + (u - 1))
                    act.wait_ge(lo_made, run + (u - 1))
                act.activation(w_hi[:, u % SPLIT, 0:kt * P], raw[:, u % RAW, 0:kt * P], ACT.Copy).then_inc(hi_made, 1)

            def mixed(t, run, done, n=1):
                b = bank(t)
                act.wait_ge(lo_used, done)
                act.wait_ge(acc_free, run + (t + (3 if n == 1 else 4)))
                if n == 1:
                    act.activation(small[:, b % 2], acc[:, b, S:2 * S], ACT.Copy).then_inc(small_made, 1)
                else:
                    act.activation(small[:], acc[:, b:b + 2, S:2 * S], ACT.Copy).then_inc(small_made, 2)

            def root(number):
                act.wait_ge(var_made, number)
                act.activation(scale2[:], scale2[:], ACT.Sqrt).then_inc(std_made, 1)

            split(0)
            split(1)
            for g in range(4):
                act.wait_ge(x_loaded[g], 16)
                act.activation(sq_all[:, 4 * g:4 * g + 4], h[:, 4 * g:4 * g + 4], ACT.Square).then_inc(sums_made, 1)
                act.wait_ge(op_f32, 4 * g + 4)
                act.activation(xa[:, 4 * g:4 * g + 4, 0:S], xf[:, 4 * g:4 * g + 4], ACT.Copy).then_inc(op_hi, 4)
            root(1)

            def gates(piece):
                if piece == 3:
                    act.wait_ge(gate_in, 1)
                    step(act.activation(e_b[:], e_nb[:], ACT.Abs))
                if piece == 4:
                    step.wait()
                    step(act.activation(e_b[:], e_b[:], ACT.Exp, scale=-1.0))
                if piece == 5:
                    step.wait()
                    act.activation(e_b[:], e_b[:], ACT.Ln, bias=1.0).then_inc(gate_out, 1)
                if piece == 10:
                    act.wait_ge(gate_in, 2)
                    step(act.activation(e_b[:], e_nb[:], ACT.Exp, scale=1.0 / GATE_NORM))
                if piece == 11:
                    step(act.activation(e_end[:], e_end[:], ACT.Exp, scale=1.0 / GATE_NORM))
                if piece == 12:
                    step.wait()
                    act.activation(e_nb[:], e_nb[:], ACT.Exp, scale=-1.0 / GATE_NORM).then_inc(gate_out, 1)

            split(2)
            mixed(0, 0, 1)
            for j in range(1, 17):
                split(j + 2)
                mixed(j, 0, j + 1)
                gates(j)
            with act.Fori(4, 8) as i:
                for j in range(1, 5):
                    split(j + 2, 4 * i)
                    mixed(j, 4 * i, 4 * i + (j + 1))

            def stage_values(hd):
                settle()
                act.activation(v_s[:], qkv[:, bass.ds(hd * 4 + 16, 4)], ACT.Copy).then_inc(v_staged, 1)

            def head_part(hd, slot, last):
                if slot == 0:
                    act.wait_ge(turned, hd * 3 + 1)
                    act.activation(ke_tok[:], aux[0:CH, 0:2], ACT.Copy).then_inc(tok_made, 1)
                if slot < 2:
                    act.wait_ge(turned, hd * 3 + (slot + 2))
                    act.activation(v_tok[:, 2 * slot:2 * slot + 2], aux[0:CH, 2:4], ACT.Copy).then_inc(tok_made, 1)
                if 2 <= slot < 6:
                    n = slot - 2
                    act.wait_ge(o_made, hd * NCH + (n + 1))
                    settle()
                    act.activation(qkv[:, bass.ds(hd * 4 + 16, 4), n * CH:(n + 1) * CH],
                                   aux[:, 1 - n % 2, 0:4 * CH], ACT.Copy).then_inc(o_read, 1)
                if slot == 5:
                    act.wait_ge(o_read, hd * NCH + NCH)
                    settle()
                    act.activation(v_s[:], qkv[:, bass.ds(hd * 4 + 16, 4)], ACT.Square).then_inc(o_squared, 1)
                if slot == 6 and not last:
                    act.wait_ge(head_done, hd + 1)
                    stage_values(hd + 1)
                if slot == 7:
                    act.wait_ge(var_made, hd + 2)
                    act.activation(scale2[:], scale2[:], ACT.Sqrt).then_inc(std_made, 1)

            def head(hd, last):
                for p in range(8):
                    u = U_CONV + 2 * p
                    head_part(hd, p, last)
                    split(u + 2, 16 * hd)
                    split(u + 3, 16 * hd)
                    mixed(u, 16 * hd, 16 * hd + (u + 2), 2)
                    if p % 2:
                        act.wait_ge(gate_in, 4 * hd + (3 + p // 2))
                        act.activation(tmp[:, 3], tmp[:, 1], ACT.Sigmoid).then_inc(gate_out, 1)

            act.wait_ge(qkv_made, 1)
            stage_values(0)
            with act.Fori(0, HEADS - 1) as hd:
                head(hd, False)
            head(HEADS - 1, True)

            with act.Fori(0, DT // 2) as i:
                for p in range(2):
                    u = U_OUT + 2 * p
                    split(u + 2, 4 * i)
                    split(u + 3, 4 * i)
                    mixed(u, 4 * i, 4 * i + (u + 2), 2)
                    act.wait_ge(gate_in, 2 * i + (DT + 3 + p))
                    act.activation(tmp[:, 2:4], tmp[:, 0:2], ACT.Sigmoid).then_inc(gate_out, 1)
                    act.wait_ge(op_f32, 2 * i + (DT + 1 + p))
                    settle()
                    act.activation(xb[:, bass.ds(2 * i + p, 1), 0:S], yb[:, bass.ds(2 * i + p, 1)], ACT.Copy).then_inc(op_hi, 1)

            with act.Fori(0, DT // 4) as i:
                for j in range(4):
                    u = U_WO + j
                    split(u + 2, 4 * i)
                    mixed(u, 4 * i, 4 * i + (u + 1))
                    act.wait_ge(op_f32, 4 * i + (2 * DT + 1 + j))
                    settle()
                    act.activation(xa[:, bass.ds(4 * i + j, 1), 0:S], tmp[:, 2], ACT.Copy).then_inc(op_hi, 1)

            for g in range(GROUPS):
                u0, t0 = U_FF1 + g * FF_UNITS, T_FF1 + g * FF_TILES
                v0, g0 = 3 * DT + g * GT, 2 * DT + 2 + g * GT

                def gated(run, pairs):
                    for p in range(2):
                        u, t = u0 + 2 * p, t0 + 2 * p
                        split(u + 2, run)
                        split(u + 3, run)
                        mixed(t, run, run + (u + 2), 2)
                        if g == 0 and p == 0:
                            pass
                        act.wait_ge(gate_in, pairs + (g0 + 1 + p))
                        act.activation(tmp[:, 2], tmp[:, 0], ACT.Silu).then_inc(gate_out, 1)
                        act.wait_ge(op_f32, pairs + (v0 + 1 + p))
                        settle()
                        act.activation(hid[:, bass.ds(pairs + p, 1), 0:S], tmp[:, 3], ACT.Copy).then_inc(op_hi, 1)

                if g == 0:
                    root(HEADS + 2)
                with act.Fori(0, GT // 2 - 1) as i:
                    gated(4 * i, 2 * i)
                gated(2 * GT - 4, GT - 2)

                u1, t1 = u0 + 2 * GT, t0 + 2 * GT

                def down(run, tiles):
                    for j in range(4):
                        split(u1 + 2 * j + 2, run)
                        split(u1 + 2 * j + 3, run)
                        mixed(t1 + j, tiles, run + (u1 + 2 * j + 2))
                        if g == GROUPS - 1:
                            act.wait_ge(op_f32, tiles + (3 * DT + FT + 1 + j))
                            settle()
                            act.activation(xa[:, bass.ds(tiles + j, 1), 0:S], tmp[:, 2], ACT.Copy).then_inc(op_hi, 1)

                with act.Fori(0, DT // 4 - 1) as i:
                    down(8 * i, 4 * i)
                down(2 * DT - 8, DT - 4)

            root(HEADS + 3)
            root(HEADS + 4)
            with act.Fori(0, 3 * HT // 4) as i:
                for j in range(4):
                    split(U_IN2 + j + 2, 4 * i)
                    mixed(T_IN2 + j, 4 * i, 4 * i + (U_IN2 + j + 1))
            for j in range(U_UQ - U_LAT):
                split(U_LAT + j + 2)
                mixed(T_LAT + j, 0, U_LAT + j + 1)
            for n, (a, b) in enumerate(((0, QT), (QT, QT + KVT))):
                act.wait_ge(lat_f32, b)
                act.activation(mix_sq[:, a:b], lat[:, a:b], ACT.Square).then_inc(lat_squared, 1)
            for n, (a, b) in enumerate(((0, QT), (QT, QT + KVT))):
                root(HEADS + 5 + n)
                act.wait_ge(lat_norm, n + 1)
                dst = cq_s if n == 0 else ckv_s
                act.activation(dst[:, :, 0:S], lat[:, a:b], ACT.Copy).then_inc(lat_hi, 1)
            t = T_UQ
            for u in range(U_UQ, U_UV):
                split(u + 2)
                for c in range(4):
                    mixed(t, 0, u + 1)
                    t += 1
            for u in range(U_UV, U_WO2):
                split(u + 2)
                for c in range(2):
                    act.wait_ge(lo_used, u + 1)
                    act.activation(v2[:, c, (u - U_UV) * 512:(u - U_UV + 1) * 512], acc[:, bank(t)], ACT.Copy)\
                       .then_inc(small_made, 2 if t == T_WO2 - 2 else 1)
                    t += 1
            act.sem_inc(attn_probt, 1)
            with act.Fori(0, NH // 2) as i:
                act.wait_ge(attn_out, 2 * i + 1)
                act.wait_ge(roped, 2)
                settle()
                act.activation(qh[:], q_n[:, bass.ds(2 * i, 2)], ACT.Copy).then_inc(head_q, 1)
                act.activation(kh[:], k_n[:, bass.ds(2 * i, 2)], ACT.Copy).then_inc(head_q, 1)
                for e in range(2):
                    act.wait_ge(attn_peak, 2 * i + (e + 1))
                    for c in range(2):
                        act.activation(prob[:, e, c], aux[:, e, c * S:(c + 1) * S], ACT.Exp, bias=peak[:, e, c:c + 1],
                                       scale=QK_SCALE, accum_out=rows[:, e, c:c + 1]).then_inc(attn_exp, 1)
                for e in range(2):
                    act.wait_ge(attn_turned, 2 * i + (e + 1))
                    act.activation(prob_t[:, e], aux[:, 2], ACT.Copy).then_inc(attn_probt, 1)
            for n in range(2):
                act.wait_ge(filt_arg, n + 1)
                act.activation(f_h[:, n], f_arg[:], ACT.Sin).then_inc(filt_sin, 1)
            for c in range(2):
                act.wait_ge(u_turned, c + 1)
                act.activation(u_tok[:, c], aux[:, 2 * c:2 * c + 2], ACT.Copy).then_inc(u_copied, 1)
            for n in range(4):
                src = aux if n % 2 == 0 else acc
                act.wait_ge(spec_made, n + 1)
                if n:
                    act.wait_ge(spec_used, n)
                act.activation(k_spec[:], src[:, 0:2], ACT.Copy).then_inc(k_copied, 1)
            for n, y in enumerate((xh[:, 2 * HT:3 * HT], q_n[:])):
                if n == 0:
                    act.wait_ge(conv_done, HT)
                else:
                    act.wait_ge(attn_read, NH + 1)
                act.activation(mix_sq2[:, n * HT:(n + 1) * HT], y, ACT.Square).then_inc(mix_squared, 1)
            root(HEADS + 7)
            root(HEADS + 8)
            for g in range(4):
                act.wait_ge(op_f32, V_MIX + 4 * g + 4)
                act.activation(xa[:, 4 * g:4 * g + 4, 0:S], mix_f[:, 4 * g:4 * g + 4], ACT.Copy).then_inc(op_hi, 4)
            with act.Fori(0, DT // 4) as i:
                for j in range(4):
                    split(U_WO2 + j + 2, 4 * i)
                    mixed(T_WO2 + j, 4 * i, 4 * i + (U_WO2 + j + 1))
            root(HEADS + 9)
            for g in range(4):
                act.wait_ge(op_f32, V_PRE + 4 * g + 4)
                act.activation(xa[:, 4 * g:4 * g + 4, 0:S], pre_a[:, 4 * g:4 * g + 4], ACT.Copy).then_inc(op_hi, 4)
            for g in range(4):
                act.wait_ge(x1_made, 4 + g + 1)
                act.activation(late_sqs[:, 4 * g:4 * g + 4], h[:, 4 * g:4 * g + 4], ACT.Square).then_inc(late_sq, 1)
            root(HEADS + 10)
            for g in range(GROUPS):
                u0, t0 = U_FF2 + g * FF_UNITS, T_FF2 + g * FF_TILES
                v0, g0 = V_FF2 + g * GT, G_FF2 + g * GT

                def gated(run, pairs):
                    for p in range(2):
                        u, t = u0 + 2 * p, t0 + 2 * p
                        split(u + 2, run)
                        split(u + 3, run)
                        mixed(t, run, run + (u + 2), 2)
                        act.wait_ge(gate_in, pairs + (g0 + 1 + p))
                        act.activation(tmp[:, 2], tmp[:, 2], ACT.Gelu_apprx_tanh).then_inc(gate_out, 1)
                        act.wait_ge(op_f32, pairs + (v0 + 1 + p))
                        settle()
                        act.activation(hid[:, bass.ds(pairs + p, 1), 0:S], tmp[:, 3], ACT.Copy).then_inc(op_hi, 1)

                with act.Fori(0, GT // 2 - 1) as i:
                    gated(4 * i, 2 * i)
                gated(2 * GT - 4, GT - 2)
                u1, t1 = u0 + 2 * GT, t0 + 2 * GT

                def down(run, tiles):
                    for j in range(4):
                        split(u1 + 2 * j + 2, run)
                        split(u1 + 2 * j + 3, run)
                        mixed(t1 + j, tiles, run + (u1 + 2 * j + 2))

                with act.Fori(0, DT // 4 - 1) as i:
                    down(8 * i, 4 * i)
                down(2 * DT - 8, DT - 4)
            root(HEADS + 11)

        @block.gpsimd
        def _(pool):
            pool.memset(ssum[:], 0.0).then_inc(pool_step, 1)
            with pool.Fori(0, DT) as i:
                pool.wait_ge(h_new, i + 1)
                pool.wait_ge(pool_step, 2 * i + 1)
                pool.tensor_tensor(sq[:], h[:, bass.ds(i, 1)], h[:, bass.ds(i, 1)], ALU.mult).then_inc(pool_step, 1)
                pool.wait_ge(pool_step, 2 * i + 2)
                pool.tensor_tensor(ssum[:], ssum[:], sq[:], ALU.add).then_inc(pool_step, 1)
            pool.wait_ge(sums_done, 2)
            pool.memset(ssum[:], 0.0).then_inc(pool_step, 1)
            pool.memset(ssum2[:], 0.0).then_inc(pool_step, 1)
            with pool.Fori(0, DT) as i:
                for k, (total, tile) in enumerate(((ssum, tmp[:, 3]), (ssum2, h[:, bass.ds(i, 1)]))):
                    pool.wait_ge(h_new, 2 * i + (2 * DT + 1 + k))
                    pool.wait_ge(pool_step, 4 * i + (POOL_WO + 2 + 2 * k))
                    pool.tensor_tensor(sq[:], tile, tile, ALU.mult).then_inc(pool_step, 1)
                    pool.wait_ge(pool_step, 4 * i + (POOL_WO + 3 + 2 * k))
                    pool.tensor_tensor(total[:], total[:], sq[:], ALU.add).then_inc(pool_step, 1)

            for base, first in ((POOL_FF1, 4 * DT), (POOL_WO2, 5 * DT)):
                pool.wait_ge(sums_done, 3 if base == POOL_FF1 else 4)
                pool.memset(ssum[:], 0.0).then_inc(pool_step, 1)
                source = branch if base == POOL_FF1 else ff_out
                with pool.Fori(0, DT) as i:
                    pool.wait_ge(h_new, i + (first + 1))
                    pool.wait_ge(pool_step, 2 * i + (base + 1))
                    pool.tensor_tensor(sq[:] if base == POOL_WO2 else sq2[:], source[:, bass.ds(i, 1)], source[:, bass.ds(i, 1)], ALU.mult).then_inc(pool_step, 1)
                    pool.wait_ge(pool_step, 2 * i + (base + 2))
                    pool.tensor_tensor(ssum[:], ssum[:], sq[:] if base == POOL_WO2 else sq2[:], ALU.add).then_inc(pool_step, 1)

        @block.vector
        def _(dve):
            step = Steps(dve, dve_step)

            def split(u, run=0):
                if k_blocks(u, run) is None:
                    return
                kt = k_blocks(u, run)
                dve.wait_ge(hi_made, run + (u + 1))
                if u >= SPLIT:
                    dve.wait_ge(lo_used, run + (u - 1))
                dve.tensor_tensor(w_lo[:, u % SPLIT, 0:kt * P], raw[:, u % RAW, 0:kt * P],
                                  w_hi[:, u % SPLIT, 0:kt * P], ALU.subtract).then_inc(lo_made, 1)

            def total(t, run, n=1):
                b = bank(t)
                if step.n:
                    step.wait()
                dve.wait_ge(small_made, run + (t + n))
                if n == 1:
                    dve.tensor_tensor(tmp[:, b % 2], acc[:, b, 0:S], small[:, b % 2], ALU.add).then_inc(acc_free, 1)
                else:
                    dve.tensor_tensor(tmp[:, 0:2], acc[:, b:b + 2, 0:S], small[:], ALU.add).then_inc(acc_free, 2)
                dve.wait_ge(acc_free, run + (t + n + 4))

            rstd2 = rstd[:].rearrange("p (a s) -> p a s", a=1).broadcast_to([P, 2, S])

            def scaled_pair():
                step(dve.tensor_tensor(tmp[:, 0:2], tmp[:, 0:2], rstd2, ALU.mult))
                step.wait()

            def norm(sums, number, source, width):
                dve.wait_ge(sums_done, sums)
                dve.tensor_scalar(scale2[:], source, 1.0 / width, EPS, ALU.mult, ALU.add).then_inc(var_made, 1)
                dve.wait_ge(std_made, number)

            dve.engine_nop().then_inc(acc_free, 4)
            dve.wait_ge(consts_loaded, 6 * 16)
            for g in range(4):
                dve.wait_ge(x_loaded[g], 16)
                for m in range(4 * g, 4 * g + 4):
                    dve.tensor_scalar(xf[:, m], h[:, m], column("mix_norm_w", m), None, ALU.mult).then_inc(op_f32, 1)
                if g < 2:
                    split(g)
                dve.wait_ge(op_hi, 4 * g + 4)
                dve.tensor_tensor(xa[:, 4 * g:4 * g + 4, S:2 * S], xf[:, 4 * g:4 * g + 4],
                                  xa[:, 4 * g:4 * g + 4, 0:S], ALU.subtract).then_inc(op_lo, 4)
            norm(1, 1, aux[:, 0, 0:S], D)
            step(dve.reciprocal(rstd[:], scale2[:]))

            total(0, 0)
            step.wait()
            step(dve.tensor_tensor(gkl[:], tmp[0:RANK, bank(0) % 2], rstd[0:RANK], ALU.mult))
            split(2)
            def gates(piece):
                if piece == 2:
                    for t in range(8):
                        if t % 2 == 0:
                            dve.wait_ge(gk_made, t // 2 + 1)
                        last = dve.tensor_scalar(e_nb[:, t], aux[:, t // 2, t % 2 * S:(t % 2 + 1) * S],
                                                 column("b_gk_up", t), None, ALU.add)
                        if t == 7:
                            last.then_inc(gate_in, 1)
                        else:
                            step(last)
                if piece == 6:
                    dve.wait_ge(gate_in, 1)
                    step.wait()
                    dve.wait_ge(gate_out, 1)
                    step(dve.scalar_tensor_tensor(e_end[:], e_nb[:], 0.0, e_b[:], ALU.min, ALU.subtract))
                if piece in (7, 8):
                    step.wait()
                    for t in range(4 * (piece - 7), 4 * (piece - 6)):
                        step(dve.tensor_tensor_scan(e_nb[:, t], reset[:], e_end[:, t], 0.0, ALU.mult, ALU.add))
                if piece == 9:
                    step.wait()
                    chunks = e_nb[:].rearrange("p t (n c) -> p (t n) c", c=CH)
                    ends = chunks[:, :, CH - 1:CH].broadcast_to([P, 8 * NCH, CH])
                    dve.tensor_tensor(e_end[:].rearrange("p t (n c) -> p (t n) c", c=CH), ends, chunks, ALU.subtract).then_inc(gate_in, 1)
                if piece == 14:
                    dve.wait_ge(gate_out, 2)
                    step.wait()
                    stage(0)

            def stage(hd):
                two, q, k = bass.ds(hd * 2, 2), bass.ds(hd * 4, 2), bass.ds(hd * 4 + 2, 2)
                dve.tensor_tensor(ke_s[:], qkv[:, k], e_end[:, two], ALU.mult).then_inc(staged, 1)
                dve.scalar_tensor_tensor(q_s[:], qkv[:, q], DK ** -0.5, e_b[:, two], ALU.mult, ALU.mult).then_inc(staged, 1)
                dve.tensor_tensor(k_s[:], qkv[:, k], e_nb[:, two], ALU.mult).then_inc(staged, 1)
                step(dve.tensor_copy(dec[:], e_b[:, two, CH - 1:S:CH]))

            def q_k_v(j, run):
                total(j, run)
                step.wait()
                step(dve.tensor_tensor(qkv[:, bass.ds(run + (j - 1), 1)], tmp[:, bank(j) % 2], rstd[:], ALU.mult))
                split(j + 2, run)

            for j in range(1, 17):
                q_k_v(j, 0)
                if j == 1:
                    step.wait()
                    dve.engine_nop().then_inc(gkl_made, 1)
                gates(j)
            with step.loop(4, 4) as i:
                for j in range(1, 5):
                    q_k_v(j + 16, 4 * i)
            step.wait()
            dve.engine_nop().then_inc(qkv_made, 1)

            def head_part(hd, slot, last):
                if slot == 1:
                    dve.wait_ge(scores_made, hd + 1)
                    causal = mask_s[:].rearrange("j (n i) -> j n i", n=1).broadcast_to([CH, NCH, CH])
                    dve.tensor_tensor(sc[:], aux[0:CH, 0, 0:S], causal, ALU.mult).then_inc(masked, 1)
                if 2 <= slot < 5:
                    n = slot - 2
                    dve.wait_ge(delta_made, hd * 3 + (n + 1))
                    if n == 0:
                        dve.tensor_copy(state[:], aux[:, 2:4]).then_inc(state_made, 2)
                    else:
                        dve.wait_ge(o_made, hd * NCH + (n + 1))
                        dve.wait_ge(state_made, hd * 6 + 2 * n)
                        for t in range(2):
                            dve.scalar_tensor_tensor(state[:, t], state[:, t], dec[:, t, n:n + 1], aux[:, 2 + t],
                                                     ALU.mult, ALU.add).then_inc(state_made, 1)
                if slot == 5 and not last:
                    dve.wait_ge(o_made, hd * NCH + NCH)
                    dve.wait_ge(state_made, hd * 6 + 6)
                    stage(hd + 1)
                if slot == 6:
                    dve.wait_ge(head_done, hd + 1)
                    dve.tensor_scalar(scale2[:], aux[:, 1, 0:S], 1.0 / DV, EPS, ALU.mult, ALU.add).then_inc(var_made, 1)
                if slot == 7:
                    dve.wait_ge(std_made, hd + 2)
                    step(dve.reciprocal(scale2[:], scale2[:]))
                    step.wait()
                    for t in range(4):
                        tile = bass.ds(hd * 4 + (16 + t), 1)
                        step(dve.scalar_tensor_tensor(qkv[:, tile], qkv[:, tile], column("gla_norm_w", t), scale2[:], ALU.mult, ALU.mult))

            def head(hd, last):
                run = 16 * hd
                for p in range(4):
                    u, i = U_CONV + 4 * p, 4 * hd + p
                    y = yb[:, bass.ds(i, 1)]
                    head_part(hd, 2 * p, last)
                    split(u + 2, run)
                    total(u, run, 2)
                    scaled_pair()
                    split(u + 3, run)
                    step(dve.tensor_tensor(tmp[:, 2], tmp[:, 0], tmp[:, 1], ALU.mult))
                    step.wait()
                    step(dve.tensor_scalar(y, tmp[:, 2], column("conv_w", i + 2 * DT), None, ALU.mult))
                    for back in (1, 2):
                        tail = yb[:, bass.ds(i, 1), back:S]
                        step.wait()
                        step(dve.scalar_tensor_tensor(tail, tmp[:, 2, 0:S - back], column("conv_w", i + (2 - back) * DT),
                                                      tail, ALU.mult, ALU.add))
                    head_part(hd, 2 * p + 1, last)
                    split(u + 4, run)
                    total(u + 2, run, 2)
                    step.wait()
                    dve.tensor_tensor(tmp[:, 0:2], tmp[:, 0:2], rstd2, ALU.mult).then_inc(gate_in, 1)
                    split(u + 5, run)
                    dve.wait_ge(gate_in, i + 3)
                    step(dve.tensor_tensor(y, y, tmp[:, 0], ALU.mult))
                    step.wait()
                    dve.wait_ge(gate_out, i + 3)
                    step(dve.tensor_tensor(y, y, tmp[:, 3], ALU.mult))
                    step.wait()

            with step.loop(HEADS - 1, 4 * 7 + 6) as hd:
                head(hd, False)
            head(HEADS - 1, True)

            with step.loop(DT // 2, 6) as i:
                for p in range(2):
                    u, m = U_OUT + 2 * p, bass.ds(2 * i + p, 1)
                    split(u + 2, 4 * i)
                    total(u, 4 * i, 2)
                    dve.tensor_tensor(tmp[:, 0:2], tmp[:, 0:2], rstd2, ALU.mult).then_inc(gate_in, 1)
                    split(u + 3, 4 * i)
                    dve.wait_ge(gate_out, 2 * i + (DT + 3 + p))
                    step(dve.tensor_tensor(tmp[:, 2], tmp[:, 2], tmp[:, 0], ALU.mult))
                    step.wait()
                    step(dve.tensor_tensor(tmp[:, 2], tmp[:, 2], tmp[:, 3], ALU.mult))
                    step.wait()
                    step(dve.tensor_tensor(tmp[:, 2], tmp[:, 2], qkv[:, bass.ds(2 * i + (16 + p), 1)], ALU.mult))
                    step.wait()
                    dve.tensor_tensor(yb[:, m], yb[:, m], tmp[:, 2], ALU.add).then_inc(op_f32, 1)
                    dve.wait_ge(op_hi, 2 * i + (DT + 1 + p))
                    dve.tensor_tensor(xb[:, m, S:2 * S], yb[:, m], xb[:, m, 0:S], ALU.subtract).then_inc(op_lo, 1)

            with step.loop(DT // 4, 0) as i:
                for j in range(4):
                    u, m = U_WO + j, bass.ds(4 * i + j, 1)
                    total(u, 4 * i)
                    dve.tensor_tensor(h[:, m], h[:, m], tmp[:, bank(u) % 2], ALU.add).then_inc(h_new, 1)
                    dve.wait_ge(h_new, 4 * i + (j + 1))
                    dve.tensor_scalar(tmp[:, 2], h[:, m], column("ffn_norm_w", 4 * i + j), None, ALU.mult).then_inc(op_f32, 1)
                    dve.wait_ge(op_hi, 4 * i + (2 * DT + 1 + j))
                    dve.tensor_tensor(xa[:, m, S:2 * S], tmp[:, 2], xa[:, m, 0:S], ALU.subtract).then_inc(op_lo, 1)
                    split(u + 2, 4 * i)

            for g in range(GROUPS):
                u0, t0 = U_FF1 + g * FF_UNITS, T_FF1 + g * FF_TILES
                v0, g0 = 3 * DT + g * GT, 2 * DT + 2 + g * GT

                def gated(run, pairs):
                    for p in range(2):
                        u, t, m = u0 + 2 * p, t0 + 2 * p, bass.ds(pairs + p, 1)
                        split(u + 2, run)
                        total(t, run, 2)
                        dve.tensor_tensor(tmp[:, 0:2], tmp[:, 0:2], rstd2, ALU.mult).then_inc(gate_in, 1)
                        split(u + 3, run)
                        dve.wait_ge(gate_out, pairs + (g0 + 1 + p))
                        dve.tensor_tensor(tmp[:, 3], tmp[:, 2], tmp[:, 1], ALU.mult).then_inc(op_f32, 1)
                        dve.wait_ge(op_hi, pairs + (v0 + 1 + p))
                        dve.tensor_tensor(hid[:, m, S:2 * S], tmp[:, 3], hid[:, m, 0:S], ALU.subtract).then_inc(op_lo, 1)

                if g == 0:
                    norm(2, HEADS + 2, aux[:, 0, 0:S], D)
                    step(dve.reciprocal(rstd[:], scale2[:]))
                    step.wait()
                with dve.Fori(0, GT // 2 - 1) as i:
                    gated(4 * i, 2 * i)
                gated(2 * GT - 4, GT - 2)

                u1, t1 = u0 + 2 * GT, t0 + 2 * GT

                def down(run, tiles):
                    for j in range(4):
                        t, m = t1 + j, bass.ds(tiles + j, 1)
                        split(u1 + 2 * j + 2, run)
                        total(t, tiles)
                        if g < GROUPS - 1:
                            dve.tensor_tensor(h[:, m], h[:, m], tmp[:, bank(t) % 2], ALU.add).then_inc(h_new, 1)
                        else:
                            dve.wait_ge(pool_step, 4 * tiles + (POOL_WO - 1 + 4 * j))
                            dve.tensor_tensor(tmp[:, 3], h[:, m], tmp[:, bank(t) % 2], ALU.add).then_inc(h_new, 1)
                            dve.wait_ge(h_new, 2 * tiles + (2 * DT + 1 + 2 * j))
                            dve.tensor_scalar(h[:, m], tmp[:, 3], column("final_norm_w", tiles + j), None, ALU.mult).then_inc(h_new, 1)
                            dve.wait_ge(h_new, 2 * tiles + (2 * DT + 2 + 2 * j))
                            dve.tensor_scalar(tmp[:, 2], h[:, m], column("pre_mix_gain", tiles + j), None, ALU.mult).then_inc(op_f32, 1)
                            dve.wait_ge(op_hi, tiles + (3 * DT + FT + 1 + j))
                            dve.tensor_tensor(xa[:, m, S:2 * S], tmp[:, 2], xa[:, m, 0:S], ALU.subtract).then_inc(op_lo, 1)
                        split(u1 + 2 * j + 3, run)

                with dve.Fori(0, DT // 4 - 1) as i:
                    down(8 * i, 4 * i)
                down(2 * DT - 8, DT - 4)

            def inverse_root(number, into):
                dve.wait_ge(std_made, number)
                step(dve.reciprocal(into[:], scale2[:]))
                step.wait()

            def over_tiles(row, n):
                return row[:].rearrange("p (a s) -> p a s", a=1).broadcast_to([P, n, S])

            dve.wait_ge(sums_done, 3)
            dve.tensor_scalar(scale2[:], aux[:, 0, 0:S], 1.0 / D, EPS, ALU.mult, ALU.add).then_inc(var_made, 1)
            inverse_root(HEADS + 3, rstd1)
            for n in range(2):
                source = aux[:, 0, S:2 * S] if n == 0 else tmp[:, 2]
                step(dve.tensor_tensor(tmp[:, 2], source, rstd1[:], ALU.mult))
                step.wait()
            dve.tensor_scalar(scale2[:], tmp[:, 2], 1.0 / D, EPS, ALU.mult, ALU.add).then_inc(var_made, 1)
            inverse_root(HEADS + 4, rstd)
            step(dve.tensor_tensor(rstd[:], rstd[:], rstd1[:], ALU.mult))
            with step.loop(3 * HT // 4, 16) as i:
                for j in range(4):
                    m, k = bass.ds(4 * i + j, 1), 4 * i + j
                    total(T_IN2 + j, 4 * i)
                    step(dve.tensor_tensor(tmp[:, 2], tmp[:, bank(T_IN2 + j) % 2], rstd[:], ALU.mult))
                    step.wait()
                    step(dve.tensor_scalar(xh[:, m], tmp[:, 2], column("hyena_conv_w", k + 3 * HT), column("hyena_conv_b", k),
                                           ALU.mult, ALU.add))
                    step.wait()
                    step(dve.scalar_tensor_tensor(xh[:, m, 1:S], tmp[:, 2, 0:S - 1], column("hyena_conv_w", k),
                                                  xh[:, m, 1:S], ALU.mult, ALU.add))
                    step.wait()
                    step(dve.scalar_tensor_tensor(xh[:, m, 0:S - 1], tmp[:, 2, 1:S], column("hyena_conv_w", k + 6 * HT),
                                                  xh[:, m, 0:S - 1], ALU.mult, ALU.add))
                    split(U_IN2 + j + 2, 4 * i)
            for j in range(U_UQ - U_LAT):
                total(T_LAT + j, 0)
                dst = lat[:, j] if j < QT + KVT else k_p[:, 0]
                dve.tensor_tensor(dst, tmp[:, bank(T_LAT + j) % 2], rstd[:], ALU.mult).then_inc(lat_f32, 1)
                dve.wait_ge(lat_f32, j + 1)
                split(U_LAT + j + 2)
            for g in range(4):
                hg = h[:, 4 * g:4 * g + 4]
                dve.tensor_tensor(hg, hg, over_tiles(rstd1, 4), ALU.mult).then_inc(x1_made, 1)
            for n, (a, b, gain, dst) in enumerate(((0, QT, "q_norm_gain", cq_s), (QT, QT + KVT, "kv_norm_gain", ckv_s))):
                dve.wait_ge(lat_summed, n + 1)
                dve.tensor_scalar(scale2[:], aux[:, n, 0:S], 1.0 / ((b - a) * P), EPS, ALU.mult, ALU.add).then_inc(var_made, 1)
                inverse_root(HEADS + 5 + n, tmp[:, 3])
                for k in range(a, b):
                    last = dve.scalar_tensor_tensor(lat[:, k], lat[:, k], column(gain, k - a), tmp[:, 3], ALU.mult, ALU.mult)
                    if k < b - 1:
                        step(last)
                last.then_inc(lat_norm, 1)
                dve.wait_ge(lat_hi, n + 1)
                step.wait()
                dve.tensor_tensor(dst[:, :, S:2 * S], lat[:, a:b], dst[:, :, 0:S], ALU.subtract).then_inc(lat_lo, 1)
            t = T_UQ
            for u in range(U_UQ, U_UV):
                for c in range(4):
                    n = t - T_UQ
                    dst = q_n[:, n] if n < 8 else q_p[:, n - 8] if n < 12 else k_n[:, n - 12]
                    dve.wait_ge(small_made, t + 1)
                    dve.tensor_tensor(dst, acc[:, bank(t), 0:S], small[:, bank(t) % 2], ALU.add).then_inc(acc_free, 1)
                    t += 1
                split(u + 2)
            for u in range(U_UV, U_WO2):
                split(u + 2)
            dve.wait_ge(small_made, T_WO2)
            dve.engine_nop().then_inc(acc_free, T_WO2 - T_UV)
            dve.wait_ge(tables_loaded, 32)
            dve.wait_ge(acc_free, T_WO2 + 4)
            dve.wait_ge(lat_f32, QT + KVT + 1)
            for n, x in enumerate((q_p, k_p)):
                tiles = NH // 2 if n == 0 else 1
                dve.wait_ge(rotated, n + 1)
                turned = aux[:, 0:2].rearrange("p b (a s) -> p (b a) s", s=S) if n == 0 else aux[:, 2:3, 0:S]
                cos, sin = (rope[:, a:a + 1].broadcast_to([P, tiles, S]) for a in range(2))
                step(dve.tensor_tensor(tmp[:, 0:tiles], turned, sin, ALU.mult))
                step(dve.tensor_tensor(x[:], x[:], cos, ALU.mult))
                step.wait()
                dve.tensor_tensor(x[:], x[:], tmp[:, 0:tiles], ALU.add).then_inc(roped, 1)
                dve.wait_ge(roped, n + 1)
            dve.engine_nop().then_inc(attn_read, 1)
            with step.loop(NH // 2, 6) as i:
                dve.wait_ge(attn_out, 2 * i + 1)
                step.wait()
                v_pair = v2[:, :, bass.ds(2 * P * i, 2 * P)]
                dve.tensor_copy(vh[:], v_pair).then_inc(head_kv, 1)
                dve.tensor_copy(qph[:], q_p[:, bass.ds(i, 1)]).then_inc(head_kv, 1)
                for e in range(2):
                    dve.wait_ge(attn_scores, 2 * i + (e + 1))
                    step(dve.tensor_reduce(peak[:, e], aux[:, e].rearrange("p (c s) -> p c s", c=2), AX.X, ALU.max))
                    step.wait()
                    dve.tensor_scalar(peak[:, e], peak[:, e], -QK_SCALE, None, ALU.mult).then_inc(attn_peak, 1)
                for e in range(2):
                    dve.wait_ge(attn_exp, 4 * i + (2 * e + 2))
                    step(dve.reciprocal(rows[:, e], rows[:, e]))
                    step.wait()
                    step(dve.tensor_scalar(prob[:, e, 0], prob[:, e, 0], rows[:, e, 0:1], None, ALU.mult))
                    step.wait()
                    dve.tensor_scalar(prob[:, e, 1], prob[:, e, 1], rows[:, e, 1:2], None, ALU.mult).then_inc(attn_prob, 1)
                dve.wait_ge(attn_out, 2 * i + 3)
                dve.tensor_copy(q_n[:, bass.ds(2 * i, 2)], aux[:, 3]).then_inc(attn_read, 2)
            dve.wait_ge(filt_loaded, 8 * 16)
            for n in range(2):
                dve.wait_ge(filt_in, n + 1)
                step(dve.tensor_scalar(f_arg[:], aux[0:FILT, n, 0:S], f_col[0:FILT, 2 * n:2 * n + 1],
                                       f_col[0:FILT, 2 * n + 1:2 * n + 2], ALU.add, ALU.mult))
                step.wait()
                step(dve.tensor_scalar(f_turn[:], f_arg[:], 1.0 / (2.0 * np.pi), ROUNDER, ALU.mult, ALU.add))
                step.wait()
                step(dve.tensor_scalar(f_turn[:], f_turn[:], -ROUNDER, None, ALU.add))
                for part_ in TURN:
                    step.wait()
                    step(dve.scalar_tensor_tensor(f_arg[:], f_turn[:], -part_, f_arg[:], ALU.mult, ALU.add))
                step.wait()
                dve.tensor_scalar(f_arg[:], f_arg[:], PI_BELOW, -PI_BELOW, ALU.min, ALU.max).then_inc(filt_arg, 1)
            for c in range(2):
                dve.wait_ge(filt_made, c + 1)
                win = window[:, c]
                step(dve.tensor_tensor(f_sum[:, c], aux[:, 0:2], win, ALU.mult))
                dve.scalar_tensor_tensor(f_dif[:, c], aux[:, 2:4], f_col[:, 4 + c:5 + c], win, ALU.mult, ALU.mult).then_inc(filt_win, 1)
                dve.wait_ge(filt_win, c + 1)
                step.wait()
                step(dve.tensor_tensor(tmp[:], f_sum[:, c], f_dif[:, c], ALU.subtract))
                step.wait()
                step(dve.tensor_tensor(f_sum[:, c], f_sum[:, c], f_dif[:, c], ALU.add))
                step.wait()
                step(dve.tensor_copy(f_dif[:, c], tmp[:]))
                step.wait()
            dve.tensor_tensor(xh[:, 2 * HT:3 * HT], xh[:, 2 * HT:3 * HT], xh[:, HT:2 * HT], ALU.mult).then_inc(u_ready, 1)
            for n in range(4):
                src = aux if n % 2 == 0 else acc
                f, c = n // 2, slice(n % 2 * 512, n % 2 * 512 + 512)
                dve.wait_ge(k_copied, n + 1)
                for r, op in enumerate((ALU.subtract, ALU.add)):
                    step.wait()
                    step(dve.tensor_tensor(part[:, 0], k_spec[:, 0], src[:, 2 + r], ALU.mult))
                    last = dve.tensor_tensor(part[:, 1], k_spec[:, 1], src[:, 3 - r], ALU.mult)
                    if r:
                        last.then_inc(spec_used, 1)
                        dve.wait_ge(spec_used, n + 1)
                    else:
                        step(last)
                    step.wait()
                    last = dve.tensor_tensor(spec[:, r, f, c], part[:, 0], part[:, 1], op)
                    if r:
                        last.then_inc(spec_ready, 1)
                        dve.wait_ge(spec_ready, n + 1)
                    else:
                        step(last)
            for c in range(HT):
                y = xh[:, 2 * HT + c]
                dve.wait_ge(conv_made, c + 1)
                step(dve.scalar_tensor_tensor(y, y, column("hyena_bias", c), aux[:, c % 4, 0:S], ALU.mult, ALU.add))
                step.wait()
                dve.tensor_tensor(y, y, xh[:, c], ALU.mult).then_inc(conv_done, 1)
            dve.wait_ge(conv_done, HT)
            for n, (gain, y) in enumerate((("hyena_out_gain", xh[:, 2 * HT:3 * HT]), ("attn_out_gain", q_n[:]))):
                dve.wait_ge(mix_summed, n + 1)
                dve.tensor_scalar(scale2[:], aux[:, n, 0:S], 1.0 / HY, EPS, ALU.mult, ALU.add).then_inc(var_made, 1)
                inverse_root(HEADS + 7 + n, tmp[:, n])
            for g in range(4):
                for m in range(4 * g, 4 * g + 4):
                    n, k = m // HT, m % HT
                    y = xh[:, 2 * HT + k] if n == 0 else q_n[:, k]
                    gain = column("attn_out_gain" if n else "hyena_out_gain", k)
                    dve.scalar_tensor_tensor(mix_f[:, m], y, gain, tmp[:, n], ALU.mult, ALU.mult).then_inc(op_f32, 1)
                dve.wait_ge(op_hi, V_MIX + 4 * g + 4)
                dve.tensor_tensor(xa[:, 4 * g:4 * g + 4, S:2 * S], mix_f[:, 4 * g:4 * g + 4],
                                  xa[:, 4 * g:4 * g + 4, 0:S], ALU.subtract).then_inc(op_lo, 4)
            dve.wait_ge(op_lo, V_MIX + DT)
            with step.loop(DT // 4, 8) as i:
                for j in range(4):
                    m, t, k = bass.ds(4 * i + j, 1), T_WO2 + j, 4 * i + j
                    total(t, 4 * i)
                    dve.tensor_copy(branch[:, m], tmp[:, bank(t) % 2]).then_inc(h_new, 1)
                    step(dve.tensor_scalar(pre_b[:, m], tmp[:, bank(t) % 2], column("post_mix_gain", k), column("pre_ffn_gain", k),
                                           ALU.mult, ALU.mult))
                    step(dve.tensor_scalar(pre_a[:, m], h[:, m], column("pre_ffn_gain", k), None, ALU.mult))
                    split(U_WO2 + j + 2, 4 * i)
            norm(4, HEADS + 9, aux[:, 0, 0:S], D)
            step(dve.reciprocal(r_post[:], scale2[:]))
            step.wait()
            for g in range(4):
                a, b = pre_a[:, 4 * g:4 * g + 4], pre_b[:, 4 * g:4 * g + 4]
                step(dve.tensor_tensor(b, b, over_tiles(r_post, 4), ALU.mult))
                step.wait()
                dve.tensor_tensor(a, a, b, ALU.add).then_inc(op_f32, 4)
                dve.wait_ge(op_hi, V_PRE + 4 * g + 4)
                dve.tensor_tensor(xa[:, 4 * g:4 * g + 4, S:2 * S], a, xa[:, 4 * g:4 * g + 4, 0:S], ALU.subtract).then_inc(op_lo, 4)
            for g in range(4):
                for m in range(4 * g, 4 * g + 4):
                    step(dve.scalar_tensor_tensor(branch[:, m], branch[:, m], column("post_mix_gain", m), r_post[:], ALU.mult, ALU.mult))
                step.wait()
                hg = h[:, 4 * g:4 * g + 4]
                dve.tensor_tensor(hg, hg, branch[:, 4 * g:4 * g + 4], ALU.add).then_inc(x1_made, 1)
            norm(5, HEADS + 10, aux[:, 0, 0:S], D)
            step(dve.reciprocal(rstd[:], scale2[:]))
            step.wait()
            for g in range(GROUPS):
                u0, t0 = U_FF2 + g * FF_UNITS, T_FF2 + g * FF_TILES
                v0, g0 = V_FF2 + g * GT, G_FF2 + g * GT

                def gated(run, pairs):
                    for p in range(2):
                        u, t, m, k = u0 + 2 * p, t0 + 2 * p, bass.ds(pairs + p, 1), pairs + (g * GT + p)
                        split(u + 2, run)
                        total(t, run, 2)
                        step(dve.tensor_tensor(tmp[:, 0:2], tmp[:, 0:2], rstd2, ALU.mult))
                        step.wait()
                        step(dve.tensor_scalar(tmp[:, 2], tmp[:, 0], column("ffn_conv_w", k + FT), column("ffn_conv_b", k), ALU.mult, ALU.add))
                        step.wait()
                        step(dve.scalar_tensor_tensor(tmp[:, 2, 1:S], tmp[:, 0, 0:S - 1], column("ffn_conv_w", k), tmp[:, 2, 1:S], ALU.mult, ALU.add))
                        step.wait()
                        dve.scalar_tensor_tensor(tmp[:, 2, 0:S - 1], tmp[:, 0, 1:S], column("ffn_conv_w", k + 2 * FT), tmp[:, 2, 0:S - 1],
                                                 ALU.mult, ALU.add).then_inc(gate_in, 1)
                        split(u + 3, run)
                        dve.wait_ge(gate_out, pairs + (g0 + 1 + p))
                        dve.tensor_tensor(tmp[:, 3], tmp[:, 2], tmp[:, 1], ALU.mult).then_inc(op_f32, 1)
                        dve.wait_ge(op_hi, pairs + (v0 + 1 + p))
                        dve.tensor_tensor(hid[:, m, S:2 * S], tmp[:, 3], hid[:, m, 0:S], ALU.subtract).then_inc(op_lo, 1)

                with step.loop(GT // 2 - 1, 6) as i:
                    gated(4 * i, 2 * i)
                gated(2 * GT - 4, GT - 2)
                u1, t1 = u0 + 2 * GT, t0 + 2 * GT

                def down(run, tiles):
                    for j in range(4):
                        t, m = t1 + j, bass.ds(tiles + j, 1)
                        split(u1 + 2 * j + 2, run)
                        if g == 0:
                            dve.wait_ge(small_made, tiles + (t + 1))
                            dve.tensor_tensor(ff_out[:, m], acc[:, bank(t), 0:S], small[:, bank(t) % 2], ALU.add).then_inc(acc_free, 1)
                        else:
                            total(t, tiles)
                            dve.tensor_tensor(ff_out[:, m], ff_out[:, m], tmp[:, bank(t) % 2], ALU.add).then_inc(h_new, 1)
                        split(u1 + 2 * j + 3, run)

                with dve.Fori(0, DT // 4 - 1) as i:
                    down(8 * i, 4 * i)
                down(2 * DT - 8, DT - 4)
            norm(6, HEADS + 11, aux[:, 0, 0:S], D)
            step(dve.reciprocal(rstd[:], scale2[:]))
            step.wait()
            for g in range(4):
                for m in range(4 * g, 4 * g + 4):
                    step(dve.scalar_tensor_tensor(ff_out[:, m], ff_out[:, m], column("post_ffn_gain", m), rstd[:], ALU.mult, ALU.mult))
                step.wait()
                hg = h[:, 4 * g:4 * g + 4]
                dve.tensor_tensor(hg, hg, ff_out[:, 4 * g:4 * g + 4], ALU.add).then_inc(fin_sum, 1)

        @block.tensor
        def _(pe):
            def high(u, run, bnk, x, kt, k0=0, first=True, ready=None):
                pe.wait_ge(hi_made, run + (u + 1))
                for k in range(kt):
                    if ready and k in ready:
                        pe.wait_ge(op_lo, ready[k])
                    last = pe.matmul(acc[:, bnk], w_hi[:, u % SPLIT, k * P:(k + 1) * P], x[:, k0 + k],
                                     start=first and k == 0, stop=False)
                last.then_inc(hi_used, 1)

            def low(u, run, bnk, x, kt, k0=0, final=True):
                pe.wait_ge(lo_made, run + (u + 1))
                for k in range(kt):
                    last = pe.matmul(acc[:, bnk, S:2 * S], w_lo[:, u % SPLIT, k * P:(k + 1) * P], x[:, k0 + k, 0:S],
                                     start=False, stop=final and k == kt - 1)
                last.then_inc(lo_used, 1)

            def unit(u, run, t, trun, x, ready=None):
                pe.wait_ge(acc_free, trun + (t + 1))
                high(u, run, bank(t), x, DT, ready=ready)
                low(u, run, bank(t), x, DT)

            def settle():
                pe.sem_inc(pe_settled, 1)

            def late(v0):
                return {0: v0 + 12, 12: v0 + 13, 13: v0 + 14, 14: v0 + 15, 15: v0 + 16}

            def sum_partitions(number):
                pe.wait_ge(sums_made, number)
                pe.matmul(aux[:, 0, 0:S], ones[:], ssum[:], start=True, stop=True).then_inc(sums_done, 1)

            pe.wait_ge(consts_loaded, 6 * 16)
            for g in range(4):
                pe.wait_ge(sums_made, g + 1)
                for m in range(4 * g, 4 * g + 4):
                    last = pe.matmul(aux[:, 0, 0:S], ones[:], sq_all[:, m], start=(m == 0), stop=(m == DT - 1))
            last.then_inc(sums_done, 1)
            unit(0, 0, 0, 0, xa, ready={4 * g: 4 * g + 4 for g in range(4)})
            unit(1, 0, 1, 0, xa)
            unit(2, 0, 2, 0, xa)
            pe.wait_ge(gkl_made, 1)
            for t in range(8):
                last = pe.matmul(aux[:, t // 2, t % 2 * S:(t % 2 + 1) * S], w_gk[:, t * P:(t + 1) * P], gkl[:],
                                 start=True, stop=True)
                if t % 2:
                    last.then_inc(gk_made, 1)

            unit(3, 0, 3, 0, xa)
            unit(4, 0, 4, 0, xa)
            with pe.Fori(1, 8) as i:
                for j in range(1, 5):
                    unit(j, 4 * i, j, 4 * i, xa)

            def turn_values(hd, half):
                for n in range(2):
                    for t in range(4):
                        c = (2 * half + n) * CH
                        last = pe.transpose(aux[0:CH, 2 + n, t * P:(t + 1) * P], v_s[:, t, c:c + CH], ident[:])
                last.then_inc(turned, 1)

            def head_part(hd, slot):
                if slot == 0:
                    pe.wait_ge(staged, hd * 3 + 3)
                    pe.wait_ge(var_made, hd + 1)
                    settle()
                    for n in range(NCH):
                        for t in range(2):
                            c = n % 2 * DK + t * P
                            last = pe.transpose(aux[0:CH, n // 2, c:c + P], ke_s[:, t, n * CH:(n + 1) * CH], ident[:])
                    last.then_inc(turned, 1)
                    pe.wait_ge(v_staged, hd + 1)
                    settle()
                    turn_values(hd, 0)
                if slot == 1:
                    pe.wait_ge(tok_made, hd * 3 + 2)
                    settle()
                    turn_values(hd, 1)
                    for n in range(NCH):
                        tok = slice(n * CH, (n + 1) * CH)
                        for t in range(2):
                            last = pe.matmul(aux[0:CH, 0, tok], k_s[:, t, tok], q_s[:, t, tok], start=(t == 0), stop=(t == 1))
                    last.then_inc(scores_made, 1)
                if 2 <= slot < 6:
                    n = slot - 2
                    tok = slice(n * CH, (n + 1) * CH)
                    if n:
                        pe.wait_ge(state_made, hd * 6 + 2 * n)
                    else:
                        pe.wait_ge(tok_made, hd * 3 + 3)
                    if n < NCH - 1:
                        for t in range(2):
                            last = pe.matmul(aux[:, 2 + t], ke_tok[:, n, t * P:(t + 1) * P], v_tok[:, n], start=True, stop=True)
                        last.then_inc(delta_made, 1)
                    if n == 0:
                        pe.wait_ge(masked, hd + 1)
                    elif n > 1:
                        pe.wait_ge(o_read, hd * NCH + (n - 1))
                    b = 1 - n % 2
                    for t in range(4):
                        for s_ in range(2 if n else 0):
                            pe.matmul(aux[:, b, t * CH:(t + 1) * CH], state[:, s_, t * P:(t + 1) * P], q_s[:, s_, tok],
                                      start=(s_ == 0), stop=False)
                        last = pe.matmul(aux[:, b, t * CH:(t + 1) * CH], v_tok[:, n, t * P:(t + 1) * P], sc[:, n],
                                         start=(n == 0), stop=True)
                    last.then_inc(o_made, 1)
                if slot == 6:
                    pe.wait_ge(o_squared, hd + 1)
                    for t in range(4):
                        last = pe.matmul(aux[:, 1, 0:S], ones[:], v_s[:, t], start=(t == 0), stop=(t == 3))
                    last.then_inc(head_done, 1)

            with pe.Fori(0, HEADS) as hd:
                for p in range(8):
                    head_part(hd, p)
                    for u in (U_CONV + 2 * p, U_CONV + 2 * p + 1):
                        unit(u, 16 * hd, u, 16 * hd, xa)

            with pe.Fori(0, DT // 2) as i:
                for j in range(4):
                    unit(U_OUT + j, 4 * i, U_OUT + j, 4 * i, xa)
            with pe.Fori(0, DT // 4) as i:
                for j in range(4):
                    unit(U_WO + j, 4 * i, U_WO + j, 4 * i, xb, ready=late(DT) if j == 0 else None)
            for g in range(GROUPS):
                u0, t0 = U_FF1 + g * FF_UNITS, T_FF1 + g * FF_TILES
                if g == 0:
                    for j in range(4):
                        unit(u0 + j, 0, t0 + j, 0, xa, ready=late(2 * DT) if j == 0 else None)
                        if j == 0:
                            pe.wait_ge(pool_step, POOL_WO)
                            pe.matmul(aux[:, 0, 0:S], ones[:], ssum[:], start=True, stop=True).then_inc(sums_done, 1)
                first = 1 if g == 0 else 0
                with pe.Fori(first, GT // 2) as i:
                    for j in range(4):
                        unit(u0 + j, 4 * i, t0 + j, 4 * i, xa)
                u1, t1, v1 = u0 + 2 * GT, t0 + 2 * GT, 3 * DT + g * GT
                with pe.Fori(0, DT // 4) as i:
                    for j in range(4):
                        u, b = u1 + 2 * j, bank(t1 + j)
                        pe.wait_ge(acc_free, 4 * i + (t1 + j + 1))
                        for half in range(2):
                            ready = {0: v1 + KD} if half == 0 else {0: v1 + 2 * KD - 1, KD - 1: v1 + 2 * KD}
                            high(u + half, 8 * i, b, hid, KD, half * KD, half == 0, ready if j == 0 else None)
                            low(u + half, 8 * i, b, hid, KD, half * KD, half == 1)

            def column_sums(dst, tiles):
                for k, tile in enumerate(tiles):
                    last = pe.matmul(dst, ones[:], tile, start=(k == 0), stop=(k == len(tiles) - 1))
                return last

            unit(U_IN2, 0, T_IN2, 0, xa, ready=late(V_IN2))
            pe.wait_ge(pool_step, POOL_FF1)
            column_sums(aux[:, 0, 0:S], [ssum[:]])
            column_sums(aux[:, 0, S:2 * S], [ssum2[:]]).then_inc(sums_done, 1)
            for j in range(1, 4):
                unit(U_IN2 + j, 0, T_IN2 + j, 0, xa)
            with pe.Fori(1, 3 * HT // 4) as i:
                for j in range(4):
                    unit(U_IN2 + j, 4 * i, T_IN2 + j, 4 * i, xa)
            for j in range(U_UQ - U_LAT):
                unit(U_LAT + j, 0, T_LAT + j, 0, xa)
            for n, (a, b) in enumerate(((0, QT), (QT, QT + KVT))):
                pe.wait_ge(lat_squared, n + 1)
                column_sums(aux[:, n, 0:S], [mix_sq[:, k] for k in range(a, b)]).then_inc(lat_summed, 1)
            t = T_UQ
            for u in range(U_UQ, U_UV):
                x, kt = (cq_s, QT) if u < U_UK else (ckv_s, KVT)
                pe.wait_ge(lat_lo, 1 if u < U_UK else 2)
                pe.wait_ge(acc_free, t + 4)
                pe.wait_ge(hi_made, u + 1)
                for c in range(4):
                    for k in range(kt):
                        w = slice(k * 512 + c * P, k * 512 + (c + 1) * P)
                        last = pe.matmul(acc[:, bank(t + c)], w_hi[:, u % SPLIT, w], x[:, k], start=(k == 0), stop=False)
                last.then_inc(hi_used, 1)
                pe.wait_ge(lo_made, u + 1)
                for c in range(4):
                    for k in range(kt):
                        w = slice(k * 512 + c * P, k * 512 + (c + 1) * P)
                        last = pe.matmul(acc[:, bank(t + c), S:2 * S], w_lo[:, u % SPLIT, w], x[:, k, 0:S], start=False, stop=(k == kt - 1))
                last.then_inc(lo_used, 1)
                t += 4
            for u in range(U_UV, U_WO2):
                pe.wait_ge(acc_free, t + 2)
                pe.wait_ge(hi_made, u + 1)
                for c in range(2):
                    for k in range(KVT):
                        for part_ in range(2):
                            x = ckv_s[:, k, part_ * S + c * P:part_ * S + (c + 1) * P]
                            last = pe.matmul(acc[:, bank(t + c)], x, w_hi[:, u % SPLIT, k * 512:(k + 1) * 512],
                                             start=(k == 0 and part_ == 0), stop=False)
                last.then_inc(hi_used, 1)
                pe.wait_ge(lo_made, u + 1)
                for c in range(2):
                    for k in range(KVT):
                        last = pe.matmul(acc[:, bank(t + c)], ckv_s[:, k, c * P:(c + 1) * P],
                                         w_lo[:, u % SPLIT, k * 512:(k + 1) * 512], start=False, stop=(k == KVT - 1))
                last.then_inc(lo_used, 1)
                t += 2
            pe.wait_ge(tables_loaded, 32)
            pe.wait_ge(acc_free, T_WO2 + 4)
            pe.wait_ge(lat_f32, QT + KVT + 1)
            for k in range(NH // 2):
                last = pe.matmul(aux[:, k // 2, k % 2 * S:(k % 2 + 1) * S], rot[:], q_p[:, k], start=True, stop=True)
            last.then_inc(rotated, 1)
            pe.matmul(aux[:, 2, 0:S], rot[:], k_p[:, 0], start=True, stop=True).then_inc(rotated, 1)
            pe.sem_inc(attn_out, 1)
            with pe.Fori(0, NH // 2) as i:
                pe.wait_ge(roped, 2)
                pe.wait_ge(head_q, 2 * i + 2)
                pe.wait_ge(head_kv, 2 * i + 2)
                pe.wait_ge(attn_read, 2 * i + 1)
                for e in range(2):
                    for c in range(2):
                        dst = aux[:, e, c * S:(c + 1) * S]
                        q, r = slice(c * P, (c + 1) * P), slice(e * ROPE, (e + 1) * ROPE)
                        pe.matmul(dst, qh[:, e, q], kh[:, e], start=True, stop=False)
                        last = pe.matmul(dst, qph[r, q], k_p[r, 0], start=False, stop=True)
                    last.then_inc(attn_scores, 1)
                for e in range(2):
                    pe.wait_ge(attn_prob, 2 * i + (e + 1))
                    pe.wait_ge(attn_probt, 2 * i + (e + 1))
                    settle()
                    for c in range(2):
                        for k in range(2):
                            last = pe.transpose(aux[:, 2, k * S + c * P:k * S + (c + 1) * P], prob[:, e, c, k * P:(k + 1) * P], ident[:])
                    last.then_inc(attn_turned, 1)
                    pe.wait_ge(attn_probt, 2 * i + (e + 2))
                    for k in range(2):
                        last = pe.matmul(aux[:, 3, e * S:(e + 1) * S], vh[:, k, e * P:(e + 1) * P], prob_t[:, e, k],
                                         start=(k == 0), stop=(k == 1))
                    last.then_inc(attn_out, 1)
            pe.wait_ge(filt_loaded, 8 * 16)
            pe.wait_ge(attn_read, NH + 1)
            pe.matmul(aux[0:FILT, 0, 0:S], w_f1[:], f_in[:], start=True, stop=True).then_inc(filt_in, 1)
            pe.wait_ge(filt_sin, 1)
            pe.matmul(aux[0:FILT, 1, 0:S], w_f2[:], f_h[:, 0], start=True, stop=True).then_inc(filt_in, 1)
            pe.wait_ge(filt_sin, 2)
            for c in range(2):
                if c:
                    pe.wait_ge(filt_win, 1)
                for n in range(4):
                    last = pe.matmul(aux[:, n], f_h[:, 1, c * P:(c + 1) * P], w_f3[:, n * 512:(n + 1) * 512], start=True, stop=True)
                last.then_inc(filt_made, 1)
            pe.wait_ge(filt_win, 2)
            pe.wait_ge(u_ready, 1)
            for c in range(2):
                for k in range(HT):
                    last = pe.transpose(aux[:, 2 * c + k // 4, k % 4 * P:(k % 4 + 1) * P],
                                        xh[:, 2 * HT + k, c * P:(c + 1) * P], ident[:])
                last.then_inc(u_turned, 1)
            pe.wait_ge(u_copied, 2)
            for n in range(4):
                dst = aux if n % 2 == 0 else acc
                f, cols = slice(n // 2 * P, (n // 2 + 1) * P), slice(n % 2 * 512, n % 2 * 512 + 512)
                if n >= 2:
                    pe.wait_ge(spec_used, n - 1)
                for q, (table, x) in enumerate(((0, f_sum), (1, f_dif), (0, u_tok), (1, u_tok))):
                    for c in range(2):
                        last = pe.matmul(dst[:, q], dft[:, table, c, f], x[:, c, cols], start=(c == 0), stop=(c == 1))
                last.then_inc(spec_made, 1)
            pe.wait_ge(spec_ready, 4)
            for c in range(HT):
                if c >= 4:
                    pe.wait_ge(conv_done, c - 3)
                for q in range(4):
                    r, f = q // 2, q % 2
                    last = pe.matmul(aux[:, c % 4, 0:S], spec[:, r, f, c * P:(c + 1) * P], idft[:, r, f], start=(q == 0), stop=(q == 3))
                last.then_inc(conv_made, 1)
            for n in range(2):
                pe.wait_ge(mix_squared, n + 1)
                pe.wait_ge(conv_done, HT)
                column_sums(aux[:, n, 0:S], [mix_sq2[:, n * HT + k] for k in range(HT)]).then_inc(mix_summed, 1)
            with pe.Fori(0, DT // 4) as i:
                for j in range(4):
                    unit(U_WO2 + j, 4 * i, T_WO2 + j, 4 * i, xa,
                         ready={4 * g: V_MIX + 4 * g + 4 for g in range(4)} if j == 0 else None)
            pe.wait_ge(pool_step, POOL_WO2)
            column_sums(aux[:, 0, 0:S], [ssum[:]]).then_inc(sums_done, 1)
            for g in range(GROUPS):
                u0, t0 = U_FF2 + g * FF_UNITS, T_FF2 + g * FF_TILES
                if g == 0:
                    for j in range(4):
                        unit(u0 + j, 0, t0 + j, 0, xa,
                             ready={4 * g_: V_PRE + 4 * g_ + 4 for g_ in range(4)} if j == 0 else None)
                        if j == 1:
                            pe.wait_ge(late_sq, 4)
                            column_sums(aux[:, 0, 0:S], [late_sqs[:, k] for k in range(DT)]).then_inc(sums_done, 1)
                with pe.Fori(1 - g, GT // 2) as i:
                    for j in range(4):
                        unit(u0 + j, 4 * i, t0 + j, 4 * i, xa)
                u1, t1, v1 = u0 + 2 * GT, t0 + 2 * GT, V_FF2 + g * GT
                with pe.Fori(0, DT // 4) as i:
                    for j in range(4):
                        u, b = u1 + 2 * j, bank(t1 + j)
                        pe.wait_ge(acc_free, 4 * i + (t1 + j + 1))
                        for half in range(2):
                            ready = {0: v1 + KD} if half == 0 else {0: v1 + 2 * KD - 1, KD - 1: v1 + 2 * KD}
                            high(u + half, 8 * i, b, hid, KD, half * KD, half == 0, ready if j == 0 else None)
                            low(u + half, 8 * i, b, hid, KD, half * KD, half == 1)
            pe.wait_ge(pool_step, POOL_WO2 + 1 + 2 * DT)
            column_sums(aux[:, 0, 0:S], [ssum[:]]).then_inc(sums_done, 1)


def _layout(i):
    f = np.ascontiguousarray
    def blocks(w, cols=P):
        k, c = w.shape
        w = w.reshape(k // P, P, c // cols, cols).transpose(2, 1, 0, 3)
        return f(w).reshape(c // cols, P, k // P * cols)
    def columns(*vs):
        return [v.reshape(-1, P).T for v in vs]
    def halves(w):
        w = w.reshape(GROUPS, 2, KD, P, DT, P).transpose(0, 4, 1, 3, 2, 5)
        return f(w).reshape(GROUPS, 2 * DT, P, KD * P)
    def paired(w):
        w = blocks(w)
        return f(np.stack([w[:FT], w[FT:]], 1)).reshape(GROUPS, 2 * GT, P, D)
    w = i["w_in"][0]
    ends = np.cumsum([0, 1024, 1024, D, D, RANK, D, D, D, D, D])
    q, k, v, g_out, gk, gate_b, gate_c, xc, merge_a, merge_b = (w[:, a:b] for a, b in zip(ends[:-1], ends[1:]))
    gk = np.pad(gk, ((0, 0), (0, P - RANK)))
    conv = np.stack([blocks(x) for x in (gate_c, xc, gate_b, merge_b)], 1).reshape(-1, P, D)
    outs = np.stack([blocks(x) for x in (g_out, merge_a)], 1).reshape(-1, P, D)
    qk = np.stack([blocks(x).reshape(HEADS, 2, P, D) for x in (q, k)], 1).reshape(-1, P, D)
    w2 = i["w_in_2"][0]
    w2 = np.concatenate([w2, w2[:, -ROPE:]], 1)
    uq = i["w_uq_2"][0].reshape(LQ, NH, P + ROPE)
    uq = np.concatenate([uq[:, :, :P].reshape(LQ, -1), uq[:, :, P:].reshape(LQ, -1)], 1)
    ukv = i["w_ukv_2"][0].reshape(LKV, NH, 2 * P)
    ukv = np.concatenate([ukv[:, :, :P].reshape(LKV, -1), ukv[:, :, P:].reshape(LKV, -1)], 1)
    f32 = np.float32
    tok = np.arange(S)
    inv_freq = (1.0 / (f32(10000.0) ** (np.arange(0, ROPE, 2, dtype=f32) / f32(ROPE)))).astype(f32)
    ang = tok.astype(f32)[:, None] * inv_freq[None, :]
    ang = np.tile(ang, (1, 4)).T
    rope = np.stack([np.cos(ang), np.sin(ang)], 1).astype(f32)
    rot = np.zeros((P, P), f32)
    for m in range(P):
        if m % ROPE < ROPE // 2:
            rot[m + ROPE // 2, m] = -1
        else:
            rot[m - ROPE // 2, m] = 1
    bands = (EMB - 1) // 2
    t = np.linspace(0.0, 1.0, S, dtype=f32)[:, None]
    wv = (f32(2.0 * np.pi) * tok.astype(f32) / f32(S)).astype(f32)
    fr = np.linspace(1e-4, bands - 1, bands, dtype=f32)
    za = wv[:, None] * fr[None, :]
    f_in = np.concatenate([t, np.cos(za), -np.sin(za)], 1).T.astype(f32)
    lo, hi = np.log(1e-2) / 1.5, np.log(1e-2) / 0.3
    deltas = np.abs(np.linspace(lo, hi, HY, dtype=f32))
    window = (np.exp(-t * deltas[None, :]) + f32(0.05)).astype(f32).reshape(2, P, HY).transpose(1, 0, 2)
    om = np.pi * (2 * np.arange(S) + 1) / (2 * S)
    table = np.stack([np.cos(tok[:, None] * om[None, :]), np.sin(tok[:, None] * om[None, :])])
    dft = table.reshape(2, 2, P, S).transpose(2, 0, 1, 3).astype(f32)
    idft = (table.transpose(0, 2, 1) / S).reshape(2, 2, P, S).transpose(2, 0, 1, 3).astype(f32)
    lag0 = np.ones((P, 2), f32)
    lag0[0, 0] = 0
    f_col = np.zeros((P, 4), f32)
    for n, name in enumerate(("filt_b1_2", "filt_freq1_2", "filt_b2_2", "filt_freq2_2")):
        f_col[:FILT, n] = i[name][0]
    reset = np.ones((P, S), f32)
    reset[:, ::CH] = 0
    return {
        "x": i["x"][0].T.reshape(DT, P, S).transpose(1, 0, 2),
        "w_in": np.concatenate([blocks(gk), qk, blocks(v), conv, outs]),
        "w_out": blocks(i["w_out"][0]),
        "w_gate_up": paired(i["w_gate_up"][0]), "w_down": halves(i["w_down"][0]),
        "w_gk_up": i["w_gk_up"][0],
        "w_in_2": blocks(w2), "w_uq": blocks(uq, 512), "w_ukv": blocks(ukv, 512),
        "w_out_2": blocks(i["w_out_2"][0]),
        "w_up": paired(i["w_up_2"][0]), "w_down_2": halves(i["w_down_2"][0]),
        "vec": np.concatenate(columns(*(i[n] for n in (
            "mix_norm_w", "ffn_norm_w", "final_norm_w", "gla_norm_w", "b_gk_up", "conv_w", "pre_mix_gain_2",
            "hyena_conv_w_2", "hyena_conv_b_2", "hyena_bias_2", "q_norm_gain_2", "kv_norm_gain_2", "hyena_out_gain_2",
            "attn_out_gain_2", "post_mix_gain_2", "pre_ffn_gain_2", "ffn_conv_w_2", "ffn_conv_b_2", "post_ffn_gain_2"))), 1),
        "ident": np.eye(P, dtype=f32), "ones": np.ones((P, P), f32),
        "mask": np.triu(np.ones((CH, CH), f32)), "reset": reset,
        "rope": rope, "rot": rot, "dft": dft, "idft": idft, "window": window, "f_in": f_in,
        "w_f1": i["filt_w1_2"][0], "w_f2": i["filt_w2_2"][0], "w_f3": i["filt_w3_2"][0],
        "f_col": np.concatenate([f_col, lag0], 1),
    }


def kernel(**inputs):
    import concourse.bacc as bacc
    from concourse.bass_utils import run_bass_kernel_spmd

    nc = bacc.Bacc("TRN2", target_bir_lowering=False, num_devices=1)
    arrays, aps = {}, {}
    for name, a in _layout({n: np.asarray(v) for n, v in inputs.items()}).items():
        a = np.ascontiguousarray(a)
        arrays[f"in_{name}"] = a
        aps[name] = nc.dram_tensor(f"in_{name}", a.shape, mybir.dt.from_np(a.dtype), kind="ExternalInput").ap()
    out = nc.dram_tensor("out", (P, DT, S), F32, kind="ExternalOutput").ap()
    build_program(nc, aps, out)
    result = run_bass_kernel_spmd(nc, [arrays], core_ids=[0]).results[0]["out"]
    return np.ascontiguousarray(np.asarray(result).transpose(2, 1, 0).reshape(1, S, D))
```

```python
from contextlib import ExitStack, contextmanager

import numpy as np

import concourse.bass as bass
from concourse import mybir

F32 = mybir.dt.float32
F32R = mybir.dt.float32r
ALU = mybir.AluOpType
ACT = mybir.ActivationFunctionType
AX = mybir.AxisListType

P = 128
D = 2048
S = 256
DT = D // P
EPS = 1e-6
FF = 5632
FT = FF // P
GROUPS = 2
GT = FT // GROUPS
KD = GT // 2
RAW = 4
SPLIT = 2
HEADS = 4
DK = 256
DV = 512
CH = 64
NCH = S // CH
RANK = 16

VEC = {}
_at = 0
for _name, _tiles in (
    ("mix_norm_w", 16), ("ffn_norm_w", 16), ("final_norm_w", 16), ("gla_norm_w", 4), ("b_gk_up", 8),
    ("conv_w", 48), ("pre_mix_gain", 16), ("hyena_conv_w", 72), ("hyena_conv_b", 24), ("hyena_bias", 8),
    ("q_norm_gain", 4), ("kv_norm_gain", 2), ("hyena_out_gain", 8), ("attn_out_gain", 8),
    ("post_mix_gain", 16), ("pre_ffn_gain", 16), ("ffn_conv_w", 132), ("ffn_conv_b", 44),
    ("post_ffn_gain", 16),
):
    VEC[_name] = _at
    _at += _tiles
NVEC = _at

U_QKV, N_QKV = 0, 33
U_CONV, N_CONV = 33, 64
U_OUT, N_OUT = 97, 32
U_WO = 129
U_FF1 = 145
FF_UNITS = 2 * GT + 2 * DT
T_FF1 = 145
FF_TILES = 2 * GT + DT


class Steps:

    def __init__(self, engine, sem):
        self.engine, self.sem, self.n, self.run = engine, sem, 0, 0

    def __call__(self, instruction):
        instruction.then_inc(self.sem, 1)
        self.n += 1
        return instruction

    def wait(self):
        self.engine.wait_ge(self.sem, self.n + self.run)

    @contextmanager
    def loop(self, count, per, start=0):
        with self.engine.Fori(start, start + count) as i:
            first, self.run = self.n, i * per + -start * per if start else i * per
            yield i
            assert self.n - first == per, (self.n - first, per)
        self.n, self.run = first + count * per, 0


def k_blocks(u, run=0):
    if isinstance(run, int):
        u += run
    if u >= N_UNITS:
        return None
    if U_UK <= u < U_HY2:
        return 8
    inside = u - (U_FF2 if u >= U_FF2 else U_FF1)
    return KD if 0 <= inside < GROUPS * FF_UNITS and inside % FF_UNITS >= 2 * GT else DT


ROUNDER = 1.5 * 2.0 ** 23
TURN = (6.28125, float(np.float32(2 * np.pi - 6.28125)))
PI_BELOW = 3.1415925
GATE_NORM = 16.0
POOL_WO = 1 + 2 * DT
POOL_FF1 = POOL_WO + 2 + 4 * DT
POOL_WO2 = POOL_FF1 + 1 + 2 * DT

HY = 1024
HT = HY // P
LQ, LKV = 512, 256
QT, KVT = LQ // P, LKV // P
NH = 8
ROPE = 64
QK_SCALE = (P + ROPE) ** -0.5
EMB, FILT = 33, 64
U_LAT = U_FF1 + GROUPS * FF_UNITS
U_HY = U_LAT + QT + KVT + 1
N_HY = 4
U_UQ = U_HY + N_HY
U_UK = U_UQ + 3
U_UV = U_UK + 2
U_HY2 = U_UV + 2
U_WO2 = U_HY2 + 3 * HT - N_HY
U_FF2 = U_WO2 + DT
N_UNITS = U_FF2 + GROUPS * FF_UNITS
T_LAT = T_FF1 + GROUPS * FF_TILES
T_HY = T_LAT + QT + KVT + 1
T_UQ = T_HY + N_HY
T_UK = T_UQ + 12
T_UV = T_UK + 8
T_HY2 = T_UV + 5
T_WO2 = T_HY2 + 3 * HT - N_HY
T_FF2 = T_WO2 + DT
V_LAT = 3 * DT + FT
V_MIX = V_LAT + DT
V_PRE = V_MIX + DT
V_FF2 = V_PRE + DT
G_FF2 = 2 * DT + 2 + FT


def build_program(nc, d, out):
    ctx = ExitStack()
    with ctx:
        base = -(-nc.sbuf_base // 32) * 32
        def at(name, offset, shape, dt=F32):
            return nc.alloc_sbuf_tensor_at(name, shape, dt, offset=base + offset)

        KB = 1024
        raw = at("raw", 0, [P, RAW, 2048])
        w_hi = at("w_hi", 32 * KB, [P, SPLIT, 2048], F32R)
        w_lo = at("w_lo", 48 * KB, [P, SPLIT, 2048], F32R)
        h = at("h", 64 * KB, [P, DT, S])
        xa = at("xa", 80 * KB, [P, DT, 2 * S], F32R)
        misc = 112 * KB
        small = at("small", misc, [P, 2, S])
        tmp = at("tmp", misc + 2 * KB, [P, 4, S])
        rstd = at("rstd", misc + 6 * KB, [P, S])
        scale2 = at("scale2", misc + 7 * KB, [P, S])
        ssum = at("ssum", misc + 8 * KB, [P, S])
        vec = at("vec", misc + 9 * KB, [P, NVEC])
        ident = at("ident", misc + 11 * KB, [P, P])
        ones = at("ones", misc + 11 * KB + 512, [P, P])
        A = misc + 12 * KB
        qkv = at("qkv", A, [P, 32, S])
        q_s = at("q_s", A + 32 * KB, [P, 2, S])
        k_s = at("k_s", A + 34 * KB, [P, 2, S])
        ke_s = at("ke_s", A + 36 * KB, [P, 2, S])
        v_s = at("v_s", A + 38 * KB, [P, 4, S])
        v_tok = at("v_tok", A + 42 * KB, [CH, NCH, DV])
        ke_tok = at("ke_tok", A + 50 * KB, [CH, NCH, DK])
        state = at("state", A + 54 * KB, [P, 2, DV])
        sc = at("sc", A + 58 * KB, [CH, NCH, CH])
        e_b = at("e_b", A + 59 * KB, [P, 8, S])
        e_nb = at("e_nb", A + 67 * KB, [P, 8, S])
        e_end = at("e_end", A + 75 * KB, [P, 8, S])
        yb = qkv[:, 0:DT]
        xb = at("xb", A + 32 * KB, [P, DT, 2 * S], F32R)
        xf = at("xf", A + 32 * KB, [P, DT, S])
        sq = at("sq", A + 66 * KB, [P, S])
        ssum2 = at("ssum2", A + 65 * KB, [P, S])
        dec = at("dec", A + 83 * KB, [P, 2, NCH])
        sq_all = at("sq_all", A + 59 * KB, [P, DT, S])
        gkl = at("gkl", A + 59 * KB, [RANK, S])
        w_gk = at("w_gk", A + 75 * KB, [RANK, 8 * P])
        mask_s = at("mask_s", A + 83 * KB + 32, [CH, CH])
        reset = at("reset", A + 48 * KB, [P, S])
        spare = at("spare", A + 83 * KB + 288, [P, 1])
        hid = at("hid", A, [P, GT, 2 * S], F32R)
        xh = at("xh", A, [P, 3 * HT, S])
        q_n = at("q_n", A + 24 * KB, [P, NH, S])
        q_p = at("q_p", A + 32 * KB, [P, NH // 2, S])
        k_p = at("k_p", A + 44 * KB, [P, 1, S])
        k_n = at("k_n", A + 36 * KB, [P, NH, S])
        v2 = at("v2", A + 45 * KB, [P, 2, NH * P])
        cq_s = at("cq_s", A + 53 * KB, [P, QT, 2 * S], F32R)
        ckv_s = at("ckv_s", A + 61 * KB, [P, KVT, 2 * S], F32R)
        lat = at("lat", A + 65 * KB, [P, QT + KVT, S])
        rope = at("rope", A + 71 * KB, [P, 2, S])
        rot = at("rot", A + 73 * KB, [P, P])
        rstd1 = at("rstd1", A + 73 * KB + 512, [P, S])
        B = A + 74 * KB + 512
        qh = at("qh", B, [P, 2, S])
        kh = at("kh", B + 2 * KB, [P, 2, S])
        vh = at("vh", B + 4 * KB, [P, 2, 2 * P])
        qph = at("qph", B + 6 * KB, [P, S])
        peak = at("peak", B + 7 * KB, [P, 2, 2])
        rows = at("rows", B + 7 * KB + 32, [P, 2, 2])
        XA = 80 * KB
        prob = at("prob", A + 63 * KB, [P, 2, 2, S])
        prob_t = at("prob_t", A + 67 * KB, [P, 2, 2, S])
        lat_r = at("lat_r", B + 6 * KB, [P, 2, S])
        w_f3 = at("w_f3", A + 53 * KB, [FILT, 2 * HY])
        f_in = at("f_in", A + 61 * KB, [EMB, S])
        w_f1 = at("w_f1", A + 62 * KB, [EMB, FILT])
        w_f2 = at("w_f2", A + 62 * KB + 256, [FILT, FILT])
        f_col = at("f_col", A + 62 * KB + 512, [P, 6])
        f_arg = at("f_arg", A + 71 * KB, [FILT, S])
        f_h = at("f_h", A + 72 * KB, [FILT, S])
        window = [at("window0", B, [P, HY]), at("window1", A + 63 * KB, [P, HY])]
        dft = at("dft", B + 4 * KB, [P, 2, 2, S])
        idft = at("idft", A + 48 * KB, [P, 2, 2, S])
        f_sum = at("f_sum", A + 32 * KB, [P, 2, HY])
        f_dif = at("f_dif", A + 40 * KB, [P, 2, HY])
        u_tok = at("u_tok", A + 32 * KB, [P, 2, HY])
        part = at("part", A + 40 * KB, [P, 4, 512])
        spec = at("spec", A + 53 * KB, [P, 2, 2, HY])
        mix_f = at("mix_f", A + 53 * KB, [P, DT, S])
        pre_a = at("pre_a", A, [P, DT, S])
        pre_b = at("pre_b", A + 16 * KB, [P, DT, S])
        branch = at("branch", A + 60 * KB, [P, DT, S])
        r_post = at("r_post", A + 77 * KB, [P, S])
        mix_sq = at("mix_sq", B, [P, QT + KVT, S])
        mix_sq2 = at("mix_sq2", A + 32 * KB, [P, DT, S])
        late_sqs = at("late_sqs", A + 16 * KB, [P, DT, S])
        ff_out = at("ff_out", A + 44 * KB, [P, DT, S])
        sq2 = at("sq2", A + 76 * KB, [P, S])
        USED_TOP = A + 83 * KB + 292
        assert base + USED_TOP <= nc.sbuf_usable_end, (base + USED_TOP, nc.sbuf_usable_end)

        acc = ctx.enter_context(nc.psum_tensor("acc", [P, 4, 512], F32))
        aux = ctx.enter_context(nc.psum_tensor("aux", [P, 4, 512], F32))

        def sem(name):
            return ctx.enter_context(nc.semaphore(name))

        vec_loaded = sem("vec_loaded")
        consts_loaded = sem("consts_loaded")
        x_loaded = [sem(f"x_loaded{g}") for g in range(4)]
        raw_loaded = [sem(f"raw_loaded{r}") for r in range(RAW)]
        hi_made = sem("hi_made")
        lo_made = sem("lo_made")
        hi_used = sem("hi_used")
        lo_used = sem("lo_used")
        small_made = sem("small_made")
        acc_free = sem("acc_free")
        op_f32 = sem("op_f32")
        op_hi = sem("op_hi")
        op_lo = sem("op_lo")
        gate_in = sem("gate_in")
        gate_out = sem("gate_out")
        sums_made = sem("sums_made")
        sums_done = sem("sums_done")
        var_made = sem("var_made")
        std_made = sem("std_made")
        dve_step = sem("dve_step")
        act_step = sem("act_step")
        pool_step = sem("pool_step")
        h_new = sem("h_new")
        staged = sem("staged")
        v_staged = sem("v_staged")
        turned = sem("turned")
        tok_made = sem("tok_made")
        scores_made = sem("scores_made")
        masked = sem("masked")
        delta_made = sem("delta_made")
        state_made = sem("state_made")
        o_made = sem("o_made")
        o_read = sem("o_read")
        o_squared = sem("o_squared")
        head_done = sem("head_done")
        act_settled = sem("act_settled")
        pe_settled = sem("pe_settled")
        gkl_made = sem("gkl_made")
        v_made = sem("v_made")
        gk_made = sem("gk_made")
        out_stored = sem("out_stored")

        rstd1_made = sem("rstd1_made")
        x1_made = sem("x1_made")
        lat_f32 = sem("lat_f32")
        lat_squared = sem("lat_squared")
        lat_summed = sem("lat_summed")
        lat_norm = sem("lat_norm")
        lat_hi = sem("lat_hi")
        lat_lo = sem("lat_lo")
        tables_loaded = sem("tables_loaded")
        quarter_made = sem("quarter_made")
        rotated = sem("rotated")
        roped = sem("roped")
        head_q = sem("head_q")
        head_rot = sem("head_rot")
        head_v = sem("head_v")
        attn_scores = sem("attn_scores")
        attn_peak = sem("attn_peak")
        attn_exp = sem("attn_exp")
        attn_prob = sem("attn_prob")
        attn_turned = sem("attn_turned")
        attn_probt = sem("attn_probt")
        attn_out = sem("attn_out")
        attn_read = sem("attn_read")
        filt_loaded = sem("filt_loaded")
        win_loaded = [sem("win_loaded0"), sem("win_loaded1")]
        dft_loaded = sem("dft_loaded")
        filt_in = sem("filt_in")
        filt_arg = sem("filt_arg")
        filt_sin = sem("filt_sin")
        filt_made = sem("filt_made")
        filt_win = sem("filt_win")
        k_spec_made = sem("k_spec_made")
        k_copied = sem("k_copied")
        u_ready = sem("u_ready")
        u_turned = sem("u_turned")
        u_copied = sem("u_copied")
        u_spec_made = sem("u_spec_made")
        spec_used = sem("spec_used")
        spec_ready = sem("spec_ready")
        conv_made = sem("conv_made")
        conv_biased = sem("conv_biased")
        conv_done = sem("conv_done")
        attn_gained = sem("attn_gained")
        attn_factor = sem("attn_factor")
        attn_normed = sem("attn_normed")
        mix_squared = sem("mix_squared")
        mix_summed = sem("mix_summed")
        post_ready = sem("post_ready")
        pre_pool = sem("pre_pool")
        x1_pool = sem("x1_pool")
        branch_gained = sem("branch_gained")
        late_sq = sem("late_sq")
        folded = sem("folded")
        out_gained = sem("out_gained")
        out_factor = sem("out_factor")
        fin_sum = sem("fin_sum")
        fin_pool = sem("fin_pool")

        def column(name, tile):
            return vec[:, bass.ds(VEC[name] + tile, 1)]

        def bank(t):
            return (t + 3) % 4

        def hyena_unit(n):
            u, t = (U_HY + n, T_HY + n) if n < N_HY else (U_HY2 + n - N_HY, T_HY2 + n - N_HY)
            return u, t, n + HT if n < 2 * HT else n - 2 * HT

        LATENTS = ((0, QT), (QT, QT + KVT))

        block = ctx.enter_context(nc.Block())

        @block.sync
        def _(sp):
            sp.dma_start(vec[:], d["vec"]).then_inc(vec_loaded, 16)

            def load_x(g):
                sp.dma_start(h[:, 4 * g:4 * g + 4], d["x"][:, 4 * g:4 * g + 4]).then_inc(x_loaded[g], 16)

            def unit(u, run, src, index, width):
                if u >= RAW:
                    sp.wait_ge(lo_made, run + (u - (RAW - 1)))
                sp.dma_start(raw[:, u % RAW, 0:width], src[index]).then_inc(raw_loaded[u % RAW], 16)

            def load(u0, src, n, width):
                with sp.Fori(0, n // 4) as i:
                    for j in range(4):
                        unit(u0 + j, 4 * i, src, 4 * i + j, width)

            load_x(0)
            for u in range(5):
                unit(u, 0, d["w_in"], u, 2048)
                if u == 0:
                    for g in range(1, 4):
                        load_x(g)
            load(5, d["w_in"][5:], 124, 2048)
            load(U_WO, d["w_out"], 16, 2048)
            for g in range(GROUPS):
                load(U_FF1 + g * FF_UNITS, d["w_gate_up"][g], 2 * GT, 2048)
                load(U_FF1 + g * FF_UNITS + 2 * GT, d["w_down"][g], 2 * DT, KD * P)
            sp.wait_ge(op_lo, 2 * DT)
            sp.dma_start(rope[:], d["rope"]).then_inc(tables_loaded, 16)
            sp.dma_start(rot[:], d["rot"]).then_inc(tables_loaded, 16)
            for n in range(QT + KVT + 1 + N_HY):
                unit(U_LAT + n, 0, d["w_in_2"], n, 2048)
            for u in range(U_UQ, U_UK):
                unit(u, 0, d["w_uq"], u - U_UQ, 2048)
            for u in range(U_UK, U_HY2):
                unit(u, 0, d["w_ukv"], u - U_UK, 1024)
            rest = d["w_in_2"][U_UQ - U_LAT:]
            load(U_HY2, rest, 8, 2048)
            sp.wait_ge(lo_used, U_HY2)
            for buffer, name in ((f_in, "f_in"), (w_f1, "w_f1"), (w_f2, "w_f2"), (f_col, "f_col"), (w_f3, "w_f3")):
                sp.dma_start(buffer[:], d[name]).then_inc(filt_loaded, 16)
            load(U_HY2 + 8, rest[8:], 4, 2048)
            sp.wait_ge(attn_scores, NH)
            sp.dma_start(window[0][:], d["window"][:, 0]).then_inc(win_loaded[0], 16)
            unit(U_HY2 + 12, 0, rest, 12, 2048)
            unit(U_HY2 + 13, 0, rest, 13, 2048)
            sp.wait_ge(attn_read, NH)
            sp.wait_ge(filt_sin, 2)
            sp.dma_start(window[1][:], d["window"][:, 1]).then_inc(win_loaded[1], 16)
            sp.dma_start(dft[:], d["dft"]).then_inc(dft_loaded, 16)
            sp.dma_start(idft[:], d["idft"]).then_inc(dft_loaded, 16)
            for n in range(14, 20):
                unit(U_HY2 + n, 0, rest, n, 2048)
            for u in range(U_WO2, U_WO2 + 4):
                unit(u, 0, d["w_out_2"], u - U_WO2, 2048)
            load(U_WO2 + 4, d["w_out_2"][4:], 12, 2048)
            for g in range(GROUPS):
                load(U_FF2 + g * FF_UNITS, d["w_up"][g], 2 * GT, 2048)
                load(U_FF2 + g * FF_UNITS + 2 * GT, d["w_down_2"][g], 2 * DT, KD * P)
            for g, made, number in ((1, fin_sum, 1), (2, fin_sum, 2), (0, fin_pool, 2), (3, fin_sum, 3)):
                sp.wait_ge(made, number)
                sp.dma_start(out[:, 4 * g:4 * g + 4], h[:, 4 * g:4 * g + 4]).then_inc(out_stored, 16)
            sp.wait_ge(out_stored, 64)

        @block.scalar
        def _(act):
            step = Steps(act, act_step)
            act.dma_start(ones[:], d["ones"]).then_inc(consts_loaded, 16)
            act.dma_start(ident[:], d["ident"]).then_inc(consts_loaded, 16)
            act.dma_start(w_gk[:], d["w_gk_up"]).then_inc(consts_loaded, 16)
            act.dma_start(mask_s[:], d["mask"]).then_inc(consts_loaded, 16)
            act.dma_start(reset[:], d["reset"]).then_inc(consts_loaded, 16)

            def settle():
                act.sem_inc(act_settled, 1)

            def split(u, run=0):
                if k_blocks(u, run) is None:
                    return
                kt = k_blocks(u, run)
                act.wait_ge(raw_loaded[u % RAW], run * 4 + 16 * (u // RAW + 1))
                if u >= SPLIT:
                    act.wait_ge(hi_used, run + (u - 1))
                    act.wait_ge(lo_made, run + (u - 1))
                act.activation(w_hi[:, u % SPLIT, 0:kt * P], raw[:, u % RAW, 0:kt * P], ACT.Copy).then_inc(hi_made, 1)

            def mixed(t, run, done, n=1):
                b = bank(t)
                act.wait_ge(lo_used, done)
                act.wait_ge(acc_free, run + (t + (3 if n == 1 else 4)))
                if n == 1:
                    act.activation(small[:, b % 2], acc[:, b, S:2 * S], ACT.Copy).then_inc(small_made, 1)
                else:
                    act.activation(small[:], acc[:, b:b + 2, S:2 * S], ACT.Copy).then_inc(small_made, 2)

            def prepare(function):
                step.wait()
                step(act.activation(spare[:], vec[:, 0:1], function))

            def root(number):
                act.wait_ge(var_made, number)
                act.activation(scale2[:], scale2[:], ACT.Sqrt).then_inc(std_made, 1)

            for g in range(4):
                act.wait_ge(op_f32, 4 * g + 4)
                act.activation(xa[:, 4 * g:4 * g + 4, 0:S], xf[:, 4 * g:4 * g + 4], ACT.Copy).then_inc(op_hi, 4)
                if g in (0, 3):
                    split(g // 3)
            for g in range(4):
                act.activation(sq_all[:, 4 * g:4 * g + 4], h[:, 4 * g:4 * g + 4], ACT.Square).then_inc(sums_made, 1)

            def gates(piece):
                if piece == 3:
                    act.wait_ge(gate_in, 1)
                    step(act.activation(e_b[:], e_nb[:], ACT.Abs))
                if piece == 4:
                    step.wait()
                    step(act.activation(e_b[:], e_b[:], ACT.Exp, scale=-1.0))
                if piece == 5:
                    step.wait()
                    act.activation(e_b[:], e_b[:], ACT.Ln, bias=1.0).then_inc(gate_out, 1)
                if piece == 10:
                    act.wait_ge(gate_in, 2)
                    step(act.activation(e_b[:], e_nb[:], ACT.Exp, scale=1.0 / GATE_NORM))
                if piece == 11:
                    step(act.activation(e_end[:], e_end[:], ACT.Exp, scale=1.0 / GATE_NORM))
                if piece == 12:
                    step.wait()
                    act.activation(e_nb[:], e_nb[:], ACT.Exp, scale=-1.0 / GATE_NORM).then_inc(gate_out, 1)

            split(2)
            mixed(0, 0, 1)
            root(1)
            for j in range(1, 17):
                split(j + 2)
                mixed(j, 0, j + 1)
                gates(j)
            with act.Fori(4, 8) as i:
                for j in range(1, 5):
                    split(j + 2, 4 * i)
                    mixed(j, 4 * i, 4 * i + (j + 1))

            def stage_values(hd):
                settle()
                act.activation(v_s[:], qkv[:, bass.ds(hd * 4 + 16, 4)], ACT.Copy).then_inc(v_staged, 1)

            def head_part(hd, slot, last):
                if slot == 0:
                    act.wait_ge(turned, hd * 3 + 1)
                    act.activation(ke_tok[:], aux[0:CH, 0:2], ACT.Copy).then_inc(tok_made, 1)
                if slot < 2:
                    act.wait_ge(turned, hd * 3 + (slot + 2))
                    act.activation(v_tok[:, 2 * slot:2 * slot + 2], aux[0:CH, 2:4], ACT.Copy).then_inc(tok_made, 1)
                if 2 <= slot < 6:
                    n = slot - 2
                    act.wait_ge(o_made, hd * NCH + (n + 1))
                    settle()
                    act.activation(qkv[:, bass.ds(hd * 4 + 16, 4), n * CH:(n + 1) * CH],
                                   aux[:, 1 - n % 2, 0:4 * CH], ACT.Copy).then_inc(o_read, 1)
                if slot == 5:
                    act.wait_ge(o_read, hd * NCH + NCH)
                    settle()
                    act.activation(v_s[:], qkv[:, bass.ds(hd * 4 + 16, 4)], ACT.Square).then_inc(o_squared, 1)
                if slot == 6 and not last:
                    act.wait_ge(head_done, hd + 1)
                    act.wait_ge(v_made, DT)
                    stage_values(hd + 1)
                if slot == 7:
                    act.wait_ge(var_made, hd + 2)
                    act.activation(scale2[:], scale2[:], ACT.Sqrt).then_inc(std_made, 1)

            def head(hd, last):
                for p in range(8):
                    u = U_CONV + 2 * p
                    head_part(hd, p, last)
                    split(u + 2, 16 * hd)
                    split(u + 3, 16 * hd)
                    mixed(u, 16 * hd, 16 * hd + (u + 2), 2)
                    if p % 2:
                        act.wait_ge(gate_in, 4 * hd + (3 + p // 2))
                        act.activation(tmp[:, 3], tmp[:, 1], ACT.Sigmoid).then_inc(gate_out, 1)

            act.wait_ge(v_made, 4)
            stage_values(0)
            prepare(ACT.Sigmoid)
            with act.Fori(0, HEADS - 1) as hd:
                head(hd, False)
            head(HEADS - 1, True)

            with act.Fori(0, DT // 2) as i:
                for p in range(2):
                    u = U_OUT + 2 * p
                    split(u + 2, 4 * i)
                    split(u + 3, 4 * i)
                    mixed(u, 4 * i, 4 * i + (u + 2), 2)
                    act.wait_ge(gate_in, 2 * i + (DT + 3 + p))
                    act.activation(tmp[:, 2:4], tmp[:, 0:2], ACT.Sigmoid).then_inc(gate_out, 1)
                    act.wait_ge(op_f32, 2 * i + (DT + 1 + p))
                    settle()
                    act.activation(xb[:, bass.ds(2 * i + p, 1), 0:S], yb[:, bass.ds(2 * i + p, 1)], ACT.Copy).then_inc(op_hi, 1)

            with act.Fori(0, DT // 4) as i:
                for j in range(4):
                    u = U_WO + j
                    split(u + 2, 4 * i)
                    mixed(u, 4 * i, 4 * i + (u + 1))
                    act.wait_ge(op_f32, 4 * i + (2 * DT + 1 + j))
                    settle()
                    act.activation(xa[:, bass.ds(4 * i + j, 1), 0:S], tmp[:, 2], ACT.Copy).then_inc(op_hi, 1)

            for g in range(GROUPS):
                u0, t0 = U_FF1 + g * FF_UNITS, T_FF1 + g * FF_TILES
                v0, g0 = 3 * DT + g * GT, 2 * DT + 2 + g * GT

                def gated(run, pairs, ahead=0):
                    for p in range(2):
                        u, t = u0 + 2 * p, t0 + 2 * p
                        if p or ahead < 1:
                            split(u + 2, run)
                        if p or ahead < 2:
                            split(u + 3, run)
                        mixed(t, run, run + (u + 2), 2)
                        act.wait_ge(gate_in, pairs + (g0 + 1 + p))
                        act.activation(tmp[:, 2], tmp[:, 0], ACT.Silu).then_inc(gate_out, 1)
                        act.wait_ge(op_f32, pairs + (v0 + 1 + p))
                        settle()
                        act.activation(hid[:, bass.ds(pairs + p, 1), 0:S], tmp[:, 3], ACT.Copy).then_inc(op_hi, 1)

                if g == 0:
                    split(u0 + 2)
                    root(HEADS + 2)
                if g == 0:
                    gated(0, 0, ahead=1)
                with act.Fori(1 - g, GT // 2 - 1) as i:
                    gated(4 * i, 2 * i)
                gated(2 * GT - 4, GT - 2)

                u1, t1 = u0 + 2 * GT, t0 + 2 * GT

                def down(run, tiles):
                    for j in range(4):
                        split(u1 + 2 * j + 2, run)
                        split(u1 + 2 * j + 3, run)
                        mixed(t1 + j, tiles, run + (u1 + 2 * j + 2))
                        if g == GROUPS - 1:
                            act.wait_ge(op_f32, tiles + (3 * DT + FT + 1 + j))
                            settle()
                            act.activation(xa[:, bass.ds(tiles + j, 1), 0:S], tmp[:, 2], ACT.Copy).then_inc(op_hi, 1)

                with act.Fori(0, DT // 4 - 1) as i:
                    down(8 * i, 4 * i)
                down(2 * DT - 8, DT - 4)

            split(U_LAT + 2)
            root(HEADS + 3)
            split(U_LAT + 3)
            root(HEADS + 4)
            for j in range(U_HY - U_LAT):
                if j >= 2:
                    split(U_LAT + j + 2)
                mixed(T_LAT + j, 0, U_LAT + j + 1)
                if j:
                    act.wait_ge(lat_f32, j)
                    act.activation(mix_sq[:, j - 1], lat[:, j - 1], ACT.Square).then_inc(lat_squared, 1)

            def stage_heads(i):
                act.activation(qh[:], q_n[:, 2 * i:2 * i + 2], ACT.Copy).then_inc(head_q, 1)
                act.activation(kh[:], k_n[:, 2 * i:2 * i + 2], ACT.Copy).then_inc(head_q, 1)

            def mixer_part(s):
                if s == 0:
                    act.wait_ge(var_made, HEADS + 6)
                    act.activation(lat_r[:], lat_r[:], ACT.Sqrt).then_inc(std_made, 2)
                if s == 2:
                    for n, (a, b) in enumerate(LATENTS):
                        act.wait_ge(lat_norm, n + 1)
                        act.activation((cq_s if n == 0 else ckv_s)[:, :, 0:S], lat[:, a:b], ACT.Copy).then_inc(lat_hi, 1)
                if s == 4:
                    act.wait_ge(acc_free, T_UV + 4)
                    stage_heads(0)
                if 5 <= s < 13:
                    i = (s - 5) // 2
                    for e in range(2):
                        if s % 2:
                            act.wait_ge(attn_peak, 2 * i + (e + 1))
                            for c in range(2):
                                act.activation(prob[:, e, c], aux[:, e, c * S:(c + 1) * S], ACT.Exp, bias=peak[:, e, c:c + 1],
                                               scale=QK_SCALE, accum_out=rows[:, e, c:c + 1]).then_inc(attn_exp, 1)
                        else:
                            act.wait_ge(attn_turned, 2 * i + (e + 1))
                            act.activation(prob_t[:, e], aux[:, 2 - 2 * e], ACT.Copy).then_inc(attn_probt, 1)
                    if s % 2 == 0 and i < NH // 2 - 1:
                        act.wait_ge(attn_scores, 2 * i + 2)
                        stage_heads(i + 1)
                if s in (9, 11):
                    act.wait_ge(filt_arg, (s - 7) // 2)
                    act.activation(f_h[:], f_arg[:], ACT.Sin).then_inc(filt_sin, 1)
                if s in (16, 17):
                    for n in (2 * (s - 16), 2 * (s - 16) + 1):
                        act.wait_ge(k_spec_made, n + 1)
                        act.activation(spec[:, :, n // 2, n % 2 * 512:n % 2 * 512 + 512], aux[:, n % 2 * 2:n % 2 * 2 + 2],
                                       ACT.Copy).then_inc(k_copied, 1)
                if s == 18:
                    for c in range(2):
                        act.wait_ge(u_turned, c + 1)
                        act.activation(u_tok[:, c], aux[:, 2 * c:2 * c + 2], ACT.Copy).then_inc(u_copied, 1)
                if s == 21:
                    act.wait_ge(spec_ready, 4)
                    act.activation(mix_sq2[:, HT:2 * HT], q_n[:], ACT.Square).then_inc(mix_squared, 1)
                if s == 22:
                    root(HEADS + 7)
                    for k in range(HT):
                        act.wait_ge(mix_squared, 1)
                        act.activation(q_n[:, k], q_n[:, k], ACT.Copy, scale=column("attn_out_gain", k)).then_inc(attn_gained, 1)
                if s == 23:
                    act.wait_ge(conv_done, 1)
                    act.activation(mix_sq2[:, 0:6], xh[:, 2 * HT:2 * HT + 6], ACT.Square).then_inc(mix_squared, 1)
                if s == 24:
                    act.wait_ge(conv_done, 2)
                    act.activation(mix_sq2[:, 6:8], xh[:, 2 * HT + 6:3 * HT], ACT.Square).then_inc(mix_squared, 1)
                    act.wait_ge(lo_used, U_WO2)
                    for g in range(4):
                        if g == 1:
                            root(HEADS + 8)
                        if g < 2:
                            act.wait_ge(attn_normed, g + 1)
                        else:
                            act.wait_ge(op_f32, V_MIX + 4 * g + 4)
                        act.activation(xa[:, 4 * g:4 * g + 4, 0:S], mix_f[:, 4 * g:4 * g + 4], ACT.Copy).then_inc(op_hi, 4)

            for n in range(3 * HT):
                u, t, _ = hyena_unit(n)
                mixer_part(n)
                split(u + 2)
                mixed(t, 0, u + 1)
                if n == N_HY - 1:
                    t = T_UQ
                    for u in range(U_UQ, U_UV):
                        split(u + 2)
                        for c in range(4):
                            if c < 3:
                                act.wait_ge(quarter_made, 3 * (u - U_UQ) + c + 1)
                            mixed(t, 0, u + 1 if c == 3 else u)
                            t += 1
                    for u in range(U_UV, U_HY2):
                        split(u + 2)
                        for c in range(2):
                            act.wait_ge(lo_used, u + 1)
                            act.activation(v2[:, c, (u - U_UV) * 512:(u - U_UV + 1) * 512], acc[:, bank(t)], ACT.Copy)\
                               .then_inc(small_made, 2 if t == T_HY2 - 2 else 1)
                            t += 1
            mixer_part(3 * HT)
            with act.Fori(0, DT // 4) as i:
                for j in range(4):
                    split(U_WO2 + j + 2, 4 * i)
                    mixed(T_WO2 + j, 4 * i, 4 * i + (U_WO2 + j + 1))
            def gain_branch(a, b):
                for m in range(a, b):
                    act.wait_ge(pool_step, POOL_FF1 + 2 * m + 2)
                    act.activation(branch[:, m], branch[:, m], ACT.Copy, scale=column("post_mix_gain", m)).then_inc(branch_gained, 1)

            gain_branch(0, 10)
            root(HEADS + 9)
            gain_branch(10, DT)
            for g in range(4):
                act.wait_ge(op_f32, V_PRE + 4 * g + 4)
                act.activation(xa[:, 4 * g:4 * g + 4, 0:S], pre_a[:, 4 * g:4 * g + 4], ACT.Copy).then_inc(op_hi, 4)
            for g, made, number in ((3, x1_pool, 1), (2, x1_pool, 2), (0, x1_made, 5), (1, x1_made, 6)):
                if g == 1:
                    split(U_FF2 + 2)
                act.wait_ge(made, number)
                act.activation(late_sqs[:, 4 * g:4 * g + 4], h[:, 4 * g:4 * g + 4], ACT.Square).then_inc(late_sq, 1)
            split(U_FF2 + 3)
            root(HEADS + 10)
            prepare(ACT.Gelu_apprx_tanh)
            for g in range(GROUPS):
                u0, t0 = U_FF2 + g * FF_UNITS, T_FF2 + g * FF_TILES
                v0, g0 = V_FF2 + g * GT, G_FF2 + g * GT

                def gated(run, pairs, ahead=1, last=False):
                    for p in range(2):
                        u, t = u0 + 2 * p, t0 + 2 * p
                        if p or ahead < 2:
                            split(u + 3, run)
                        mixed(t, run, run + (u + 2), 2)
                        act.wait_ge(gate_in, pairs + (g0 + 1 + p))
                        act.activation(tmp[:, 2], tmp[:, 2], ACT.Gelu_apprx_tanh).then_inc(gate_out, 1)
                        if not (last and p):
                            split(u + 4, run)
                        act.wait_ge(op_f32, pairs + (v0 + 1 + p))
                        settle()
                        act.activation(hid[:, bass.ds(pairs + p, 1), 0:S], tmp[:, 3], ACT.Copy).then_inc(op_hi, 1)

                if g == 0:
                    gated(0, 0, ahead=2)
                else:
                    split(u0 + 2)
                with act.Fori(1 - g, GT // 2 - 1) as i:
                    gated(4 * i, 2 * i)
                gated(2 * GT - 4, GT - 2, last=True)
                u1, t1 = u0 + 2 * GT, t0 + 2 * GT

                def down(run, tiles):
                    for j in range(4):
                        split(u1 + 2 * j + 2, run)
                        split(u1 + 2 * j + 3, run)
                        mixed(t1 + j, tiles, run + (u1 + 2 * j + 2))

                with act.Fori(0, DT // 4 - 1) as i:
                    down(8 * i, 4 * i)
                down(2 * DT - 8, DT - 4)
            def gain_output(a, b):
                for m in range(a, b):
                    act.wait_ge(pool_step, POOL_WO2 + 2 * m + 2)
                    act.activation(ff_out[:, m], ff_out[:, m], ACT.Copy, scale=column("post_ffn_gain", m)).then_inc(out_gained, 1)

            gain_output(0, 9)
            root(HEADS + 11)
            gain_output(9, DT)

        @block.gpsimd
        def _(pool):
            def sums_of_squares(free, base, first, source, square):
                pool.wait_ge(sums_done, free)
                pool.memset(ssum[:], 0.0).then_inc(pool_step, 1)
                with pool.Fori(0, DT) as i:
                    pool.wait_ge(h_new, i + (first + 1))
                    pool.wait_ge(pool_step, 2 * i + (base + 1))
                    pool.tensor_tensor(square[:], source[:, bass.ds(i, 1)], source[:, bass.ds(i, 1)], ALU.mult).then_inc(pool_step, 1)
                    pool.wait_ge(pool_step, 2 * i + (base + 2))
                    pool.tensor_tensor(ssum[:], ssum[:], square[:], ALU.add).then_inc(pool_step, 1)

            def fold(tiles, made, number, order):
                into = tiles[:, 4 * order[0]:4 * order[0] + 4]
                for n, g in enumerate(order[1:]):
                    pool.wait_ge(made, n + 2)
                    if n:
                        pool.wait_ge(folded, number + n)
                    pool.tensor_tensor(into, into, tiles[:, 4 * g:4 * g + 4], ALU.add).then_inc(folded, 1)

            fold(sq_all, sums_made, 0, (0, 1, 2, 3))
            pool.memset(ssum[:], 0.0).then_inc(pool_step, 1)
            with pool.Fori(0, DT) as i:
                pool.wait_ge(h_new, i + 1)
                pool.wait_ge(pool_step, 2 * i + 1)
                pool.tensor_tensor(sq[:], h[:, bass.ds(i, 1)], h[:, bass.ds(i, 1)], ALU.mult).then_inc(pool_step, 1)
                pool.wait_ge(pool_step, 2 * i + 2)
                pool.tensor_tensor(ssum[:], ssum[:], sq[:], ALU.add).then_inc(pool_step, 1)
            pool.wait_ge(sums_done, 2)
            pool.memset(ssum[:], 0.0).then_inc(pool_step, 1)
            pool.memset(ssum2[:], 0.0).then_inc(pool_step, 1)
            with pool.Fori(0, DT) as i:
                for k, (total, tile) in enumerate(((ssum, tmp[:, 3]), (ssum2, h[:, bass.ds(i, 1)]))):
                    pool.wait_ge(h_new, 2 * i + (2 * DT + 1 + k))
                    pool.wait_ge(pool_step, 4 * i + (POOL_WO + 2 + 2 * k))
                    pool.tensor_tensor(sq[:], tile, tile, ALU.mult).then_inc(pool_step, 1)
                    pool.wait_ge(pool_step, 4 * i + (POOL_WO + 3 + 2 * k))
                    pool.tensor_tensor(total[:], total[:], sq[:], ALU.add).then_inc(pool_step, 1)

            pool.wait_ge(rstd1_made, 1)
            for g in range(4):
                hg = h[:, 4 * g:4 * g + 4]
                factor = rstd1[:].rearrange("p (a s) -> p a s", a=1).broadcast_to([P, 4, S])
                pool.tensor_tensor(hg, hg, factor, ALU.mult).then_inc(x1_made, 1)
            pool.wait_ge(attn_factor, 1)
            pool.wait_ge(attn_gained, HT)
            pool.wait_ge(conv_made, HT)
            for g in range(2):
                tiles = slice(4 * g, 4 * g + 4)
                factor = rstd1[:].rearrange("p (a s) -> p a s", a=1).broadcast_to([P, 4, S])
                pool.tensor_tensor(mix_f[:, tiles], q_n[:, tiles], factor, ALU.mult).then_inc(attn_normed, 1)
            sums_of_squares(3, POOL_FF1, 4 * DT, branch, sq2)
            pool.wait_ge(post_ready, 1)
            a, b = pre_a[:, 12:16], pre_b[:, 12:16]
            pool.tensor_tensor(b, b, r_post[:].rearrange("p (a s) -> p a s", a=1).broadcast_to([P, 4, S]), ALU.mult).then_inc(pre_pool, 1)
            pool.wait_ge(pre_pool, 1)
            pool.tensor_tensor(a, a, b, ALU.add).then_inc(pre_pool, 1)
            pool.wait_ge(branch_gained, DT)
            for n, g in enumerate((3, 2)):
                hg, bg = h[:, 4 * g:4 * g + 4], branch[:, 4 * g:4 * g + 4]
                pool.tensor_tensor(bg, bg, r_post[:].rearrange("p (a s) -> p a s", a=1).broadcast_to([P, 4, S]), ALU.mult).then_inc(pre_pool, 1)
                pool.wait_ge(pre_pool, n + 3)
                pool.tensor_tensor(hg, hg, bg, ALU.add).then_inc(x1_pool, 1)
            fold(late_sqs, late_sq, 3, (3, 2, 0, 1))
            sums_of_squares(4, POOL_WO2, 5 * DT, ff_out, sq)
            pool.wait_ge(out_factor, 1)
            pool.wait_ge(out_gained, 4)
            hg, bg = h[:, 0:4], ff_out[:, 0:4]
            pool.tensor_tensor(bg, bg, rstd[:].rearrange("p (a s) -> p a s", a=1).broadcast_to([P, 4, S]), ALU.mult).then_inc(fin_pool, 1)
            pool.wait_ge(fin_pool, 1)
            pool.tensor_tensor(hg, hg, bg, ALU.add).then_inc(fin_pool, 1)

        @block.vector
        def _(dve):
            step = Steps(dve, dve_step)

            def split(u, run=0):
                if k_blocks(u, run) is None:
                    return
                kt = k_blocks(u, run)
                dve.wait_ge(hi_made, run + (u + 1))
                if u >= SPLIT:
                    dve.wait_ge(lo_used, run + (u - 1))
                dve.tensor_tensor(w_lo[:, u % SPLIT, 0:kt * P], raw[:, u % RAW, 0:kt * P],
                                  w_hi[:, u % SPLIT, 0:kt * P], ALU.subtract).then_inc(lo_made, 1)

            def total(t, run, n=1):
                b = bank(t)
                if step.n:
                    step.wait()
                dve.wait_ge(small_made, run + (t + n))
                if n == 1:
                    dve.tensor_tensor(tmp[:, b % 2], acc[:, b, 0:S], small[:, b % 2], ALU.add).then_inc(acc_free, 1)
                else:
                    dve.tensor_tensor(tmp[:, 0:2], acc[:, b:b + 2, 0:S], small[:], ALU.add).then_inc(acc_free, 2)
                dve.wait_ge(acc_free, run + (t + n + 4))

            rstd2 = rstd[:].rearrange("p (a s) -> p a s", a=1).broadcast_to([P, 2, S])

            def scaled_pair():
                step(dve.tensor_tensor(tmp[:, 0:2], tmp[:, 0:2], rstd2, ALU.mult))
                step.wait()

            def norm(sums, number, source, width):
                dve.wait_ge(sums_done, sums)
                dve.tensor_scalar(scale2[:], source, 1.0 / width, EPS, ALU.mult, ALU.add).then_inc(var_made, 1)
                dve.wait_ge(std_made, number)

            dve.engine_nop().then_inc(acc_free, 4)
            dve.wait_ge(vec_loaded, 16)
            def gained(g):
                dve.wait_ge(x_loaded[g], 16)
                for m in range(4 * g, 4 * g + 4):
                    dve.tensor_scalar(xf[:, m], h[:, m], column("mix_norm_w", m), None, ALU.mult).then_inc(op_f32, 1)

            gained(0)
            for g in range(4):
                if g < 3:
                    gained(g + 1)
                dve.wait_ge(op_hi, 4 * g + 4)
                dve.tensor_tensor(xa[:, 4 * g:4 * g + 4, S:2 * S], xf[:, 4 * g:4 * g + 4],
                                  xa[:, 4 * g:4 * g + 4, 0:S], ALU.subtract).then_inc(op_lo, 4)
                if g in (0, 3):
                    split(g // 3)
            split(2)
            norm(1, 1, aux[:, 0, 0:S], D)
            step(dve.reciprocal(rstd[:], scale2[:]))

            total(0, 0)
            step.wait()
            step(dve.tensor_tensor(gkl[:], tmp[0:RANK, bank(0) % 2], rstd[0:RANK], ALU.mult))
            def gates(piece):
                if piece == 2:
                    for t in range(8):
                        if t % 2 == 0:
                            dve.wait_ge(gk_made, t // 2 + 1)
                        last = dve.tensor_scalar(e_nb[:, t], aux[:, t // 2, t % 2 * S:(t % 2 + 1) * S],
                                                 column("b_gk_up", t), None, ALU.add)
                        if t == 7:
                            last.then_inc(gate_in, 1)
                        else:
                            step(last)
                if piece == 6:
                    dve.wait_ge(gate_in, 1)
                    step.wait()
                    dve.wait_ge(gate_out, 1)
                    step(dve.scalar_tensor_tensor(e_end[:], e_nb[:], 0.0, e_b[:], ALU.min, ALU.subtract))
                if piece in (7, 8):
                    dve.wait_ge(consts_loaded, 5 * 16)
                    step.wait()
                    for t in range(4 * (piece - 7), 4 * (piece - 6)):
                        step(dve.tensor_tensor_scan(e_nb[:, t], reset[:], e_end[:, t], 0.0, ALU.mult, ALU.add))
                if piece == 9:
                    step.wait()
                    chunks = e_nb[:].rearrange("p t (n c) -> p (t n) c", c=CH)
                    ends = chunks[:, :, CH - 1:CH].broadcast_to([P, 8 * NCH, CH])
                    dve.tensor_tensor(e_end[:].rearrange("p t (n c) -> p (t n) c", c=CH), ends, chunks, ALU.subtract).then_inc(gate_in, 1)
                if piece == 14:
                    dve.wait_ge(gate_out, 2)
                    step.wait()
                    stage(0)

            def stage(hd):
                two, q, k = bass.ds(hd * 2, 2), bass.ds(hd * 4, 2), bass.ds(hd * 4 + 2, 2)
                dve.tensor_tensor(ke_s[:], qkv[:, k], e_end[:, two], ALU.mult).then_inc(staged, 1)
                dve.scalar_tensor_tensor(q_s[:], qkv[:, q], DK ** -0.5, e_b[:, two], ALU.mult, ALU.mult).then_inc(staged, 1)
                dve.tensor_tensor(k_s[:], qkv[:, k], e_nb[:, two], ALU.mult).then_inc(staged, 1)
                step(dve.tensor_copy(dec[:], e_b[:, two, CH - 1:S:CH]))

            def q_k_v(j, run, values=False):
                total(j, run)
                step.wait()
                last = dve.tensor_tensor(qkv[:, bass.ds(run + (j - 1), 1)], tmp[:, bank(j) % 2], rstd[:], ALU.mult)
                if values:
                    last.then_inc(v_made, 1)
                else:
                    step(last)
                split(j + 2, run)

            for j in range(1, 17):
                q_k_v(j, 0)
                if j == 1:
                    step.wait()
                    dve.engine_nop().then_inc(gkl_made, 1)
                gates(j)
            with dve.Fori(0, 4) as i:
                for j in range(1, 5):
                    q_k_v(j + 16, 4 * i, values=True)
                    dve.wait_ge(v_made, 4 * i + j)

            def head_part(hd, slot, last):
                if slot == 1:
                    dve.wait_ge(scores_made, hd + 1)
                    causal = mask_s[:].rearrange("j (n i) -> j n i", n=1).broadcast_to([CH, NCH, CH])
                    dve.tensor_tensor(sc[:], aux[0:CH, 0, 0:S], causal, ALU.mult).then_inc(masked, 1)
                if 2 <= slot < 5:
                    n = slot - 2
                    dve.wait_ge(delta_made, hd * 3 + (n + 1))
                    if n == 0:
                        dve.tensor_copy(state[:], aux[:, 2:4]).then_inc(state_made, 2)
                    else:
                        dve.wait_ge(o_made, hd * NCH + (n + 1))
                        dve.wait_ge(state_made, hd * 6 + 2 * n)
                        for t in range(2):
                            dve.scalar_tensor_tensor(state[:, t], state[:, t], dec[:, t, n:n + 1], aux[:, 2 + t],
                                                     ALU.mult, ALU.add).then_inc(state_made, 1)
                if slot == 5 and not last:
                    dve.wait_ge(o_made, hd * NCH + NCH)
                    dve.wait_ge(state_made, hd * 6 + 6)
                    stage(hd + 1)
                if slot == 6:
                    dve.wait_ge(head_done, hd + 1)
                    dve.tensor_scalar(scale2[:], aux[:, 1, 0:S], 1.0 / DV, EPS, ALU.mult, ALU.add).then_inc(var_made, 1)
                if slot == 7:
                    dve.wait_ge(std_made, hd + 2)
                    step(dve.reciprocal(scale2[:], scale2[:]))
                    step.wait()
                    for t in range(4):
                        tile = bass.ds(hd * 4 + (16 + t), 1)
                        step(dve.scalar_tensor_tensor(qkv[:, tile], qkv[:, tile], column("gla_norm_w", t), scale2[:], ALU.mult, ALU.mult))

            def head(hd, last):
                run = 16 * hd
                for p in range(4):
                    u, i = U_CONV + 4 * p, 4 * hd + p
                    y = yb[:, bass.ds(i, 1)]
                    head_part(hd, 2 * p, last)
                    split(u + 2, run)
                    total(u, run, 2)
                    scaled_pair()
                    split(u + 3, run)
                    step(dve.tensor_tensor(tmp[:, 2], tmp[:, 0], tmp[:, 1], ALU.mult))
                    step.wait()
                    step(dve.tensor_scalar(y, tmp[:, 2], column("conv_w", i + 2 * DT), None, ALU.mult))
                    for back in (1, 2):
                        tail = yb[:, bass.ds(i, 1), back:S]
                        step.wait()
                        step(dve.scalar_tensor_tensor(tail, tmp[:, 2, 0:S - back], column("conv_w", i + (2 - back) * DT),
                                                      tail, ALU.mult, ALU.add))
                    head_part(hd, 2 * p + 1, last)
                    split(u + 4, run)
                    total(u + 2, run, 2)
                    step.wait()
                    dve.tensor_tensor(tmp[:, 0:2], tmp[:, 0:2], rstd2, ALU.mult).then_inc(gate_in, 1)
                    split(u + 5, run)
                    dve.wait_ge(gate_in, i + 3)
                    step(dve.tensor_tensor(y, y, tmp[:, 0], ALU.mult))
                    step.wait()
                    dve.wait_ge(gate_out, i + 3)
                    step(dve.tensor_tensor(y, y, tmp[:, 3], ALU.mult))
                    step.wait()

            with step.loop(HEADS - 1, 4 * 7 + 6) as hd:
                head(hd, False)
            head(HEADS - 1, True)

            with step.loop(DT // 2, 6) as i:
                for p in range(2):
                    u, m = U_OUT + 2 * p, bass.ds(2 * i + p, 1)
                    split(u + 2, 4 * i)
                    total(u, 4 * i, 2)
                    dve.tensor_tensor(tmp[:, 0:2], tmp[:, 0:2], rstd2, ALU.mult).then_inc(gate_in, 1)
                    split(u + 3, 4 * i)
                    dve.wait_ge(gate_out, 2 * i + (DT + 3 + p))
                    step(dve.tensor_tensor(tmp[:, 2], tmp[:, 2], tmp[:, 0], ALU.mult))
                    step.wait()
                    step(dve.tensor_tensor(tmp[:, 2], tmp[:, 2], tmp[:, 3], ALU.mult))
                    step.wait()
                    step(dve.tensor_tensor(tmp[:, 2], tmp[:, 2], qkv[:, bass.ds(2 * i + (16 + p), 1)], ALU.mult))
                    step.wait()
                    dve.tensor_tensor(yb[:, m], yb[:, m], tmp[:, 2], ALU.add).then_inc(op_f32, 1)
                    dve.wait_ge(op_hi, 2 * i + (DT + 1 + p))
                    dve.tensor_tensor(xb[:, m, S:2 * S], yb[:, m], xb[:, m, 0:S], ALU.subtract).then_inc(op_lo, 1)

            with step.loop(DT // 4, 0) as i:
                for j in range(4):
                    u, m = U_WO + j, bass.ds(4 * i + j, 1)
                    total(u, 4 * i)
                    dve.tensor_tensor(h[:, m], h[:, m], tmp[:, bank(u) % 2], ALU.add).then_inc(h_new, 1)
                    dve.wait_ge(h_new, 4 * i + (j + 1))
                    dve.tensor_scalar(tmp[:, 2], h[:, m], column("ffn_norm_w", 4 * i + j), None, ALU.mult).then_inc(op_f32, 1)
                    dve.wait_ge(op_hi, 4 * i + (2 * DT + 1 + j))
                    dve.tensor_tensor(xa[:, m, S:2 * S], tmp[:, 2], xa[:, m, 0:S], ALU.subtract).then_inc(op_lo, 1)
                    split(u + 2, 4 * i)

            for g in range(GROUPS):
                u0, t0 = U_FF1 + g * FF_UNITS, T_FF1 + g * FF_TILES
                v0, g0 = 3 * DT + g * GT, 2 * DT + 2 + g * GT

                def gated(run, pairs, ahead=0):
                    for p in range(2):
                        u, t, m = u0 + 2 * p, t0 + 2 * p, bass.ds(pairs + p, 1)
                        if p or ahead < 1:
                            split(u + 2, run)
                        total(t, run, 2)
                        dve.tensor_tensor(tmp[:, 0:2], tmp[:, 0:2], rstd2, ALU.mult).then_inc(gate_in, 1)
                        if p or ahead < 2:
                            split(u + 3, run)
                        dve.wait_ge(gate_out, pairs + (g0 + 1 + p))
                        dve.tensor_tensor(tmp[:, 3], tmp[:, 2], tmp[:, 1], ALU.mult).then_inc(op_f32, 1)
                        dve.wait_ge(op_hi, pairs + (v0 + 1 + p))
                        dve.tensor_tensor(hid[:, m, S:2 * S], tmp[:, 3], hid[:, m, 0:S], ALU.subtract).then_inc(op_lo, 1)

                if g == 0:
                    split(u0 + 2)
                    norm(2, HEADS + 2, aux[:, 0, 0:S], D)
                    step(dve.reciprocal(rstd[:], scale2[:]))
                    step.wait()
                if g == 0:
                    gated(0, 0, ahead=1)
                with dve.Fori(1 - g, GT // 2 - 1) as i:
                    gated(4 * i, 2 * i)
                gated(2 * GT - 4, GT - 2)

                u1, t1 = u0 + 2 * GT, t0 + 2 * GT

                def down(run, tiles):
                    for j in range(4):
                        t, m = t1 + j, bass.ds(tiles + j, 1)
                        split(u1 + 2 * j + 2, run)
                        total(t, tiles)
                        if g < GROUPS - 1:
                            dve.tensor_tensor(h[:, m], h[:, m], tmp[:, bank(t) % 2], ALU.add).then_inc(h_new, 1)
                        else:
                            dve.wait_ge(pool_step, 4 * tiles + (POOL_WO - 1 + 4 * j))
                            dve.tensor_tensor(tmp[:, 3], h[:, m], tmp[:, bank(t) % 2], ALU.add).then_inc(h_new, 1)
                            dve.wait_ge(h_new, 2 * tiles + (2 * DT + 1 + 2 * j))
                            dve.tensor_scalar(h[:, m], tmp[:, 3], column("final_norm_w", tiles + j), None, ALU.mult).then_inc(h_new, 1)
                            dve.wait_ge(h_new, 2 * tiles + (2 * DT + 2 + 2 * j))
                            dve.tensor_scalar(tmp[:, 2], h[:, m], column("pre_mix_gain", tiles + j), None, ALU.mult).then_inc(op_f32, 1)
                            dve.wait_ge(op_hi, tiles + (3 * DT + FT + 1 + j))
                            dve.tensor_tensor(xa[:, m, S:2 * S], tmp[:, 2], xa[:, m, 0:S], ALU.subtract).then_inc(op_lo, 1)
                        split(u1 + 2 * j + 3, run)

                with dve.Fori(0, DT // 4 - 1) as i:
                    down(8 * i, 4 * i)
                down(2 * DT - 8, DT - 4)

            def inverse_root(number, into):
                dve.wait_ge(std_made, number)
                step(dve.reciprocal(into[:], scale2[:]))
                step.wait()

            def over_tiles(row, n):
                return row[:].rearrange("p (a s) -> p a s", a=1).broadcast_to([P, n, S])

            split(U_LAT + 2)
            dve.wait_ge(sums_done, 3)
            dve.tensor_scalar(scale2[:], aux[:, 0, 0:S], 1.0 / D, EPS, ALU.mult, ALU.add).then_inc(var_made, 1)
            inverse_root(HEADS + 3, rstd1)
            dve.engine_nop().then_inc(rstd1_made, 1)
            for n in range(2):
                source = aux[:, 0, S:2 * S] if n == 0 else tmp[:, 2]
                step(dve.tensor_tensor(tmp[:, 2], source, rstd1[:], ALU.mult))
                step.wait()
            dve.tensor_scalar(scale2[:], tmp[:, 2], 1.0 / D, EPS, ALU.mult, ALU.add).then_inc(var_made, 1)
            split(U_LAT + 3)
            inverse_root(HEADS + 4, rstd)
            step(dve.tensor_tensor(rstd[:], rstd[:], rstd1[:], ALU.mult))
            for j in range(U_HY - U_LAT):
                total(T_LAT + j, 0)
                dst = lat[:, j] if j < QT + KVT else k_p[:, 0]
                dve.tensor_tensor(dst, tmp[:, bank(T_LAT + j) % 2], rstd[:], ALU.mult).then_inc(lat_f32, 1)
                dve.wait_ge(lat_f32, j + 1)
                if j >= 2:
                    split(U_LAT + j + 2)

            def latent_projections():
                t = T_UQ
                for u in range(U_UQ, U_UV):
                    for c in range(4):
                        n = t - T_UQ
                        dst = q_n[:, n] if n < 8 else q_p[:, n - 8] if n < 12 else k_n[:, n - 12]
                        dve.wait_ge(small_made, t + 1)
                        dve.tensor_tensor(dst, acc[:, bank(t), 0:S], small[:, bank(t) % 2], ALU.add).then_inc(acc_free, 1)
                        t += 1
                    split(u + 2)
                for u in range(U_UV, U_HY2):
                    split(u + 2)
                dve.wait_ge(small_made, T_HY2)
                dve.engine_nop().then_inc(acc_free, T_HY2 - T_UV)

            def rotary():
                dve.wait_ge(tables_loaded, 32)
                for n, x in enumerate((q_p, k_p)):
                    tiles = NH // 2 if n == 0 else 1
                    dve.wait_ge(rotated, n + 1)
                    turned = aux[:, 0:2].rearrange("p b (a s) -> p (b a) s", s=S) if n == 0 else aux[:, 2:3, 0:S]
                    cos, sin = (rope[:, a:a + 1].broadcast_to([P, tiles, S]) for a in range(2))
                    step.wait()
                    step(dve.tensor_tensor(tmp[:, 0:tiles], turned, sin, ALU.mult))
                    step(dve.tensor_tensor(x[:], x[:], cos, ALU.mult))
                    step.wait()
                    dve.tensor_tensor(x[:], x[:], tmp[:, 0:tiles], ALU.add).then_inc(roped, 1)
                    dve.wait_ge(roped, n + 1)

            def stage_rotary(i):
                dve.tensor_copy(qph[:], q_p[:, i]).then_inc(head_rot, 1)

            def stage_values(i):
                dve.tensor_copy(vh[:], v2[:, :, 2 * P * i:2 * P * (i + 1)]).then_inc(head_v, 1)

            def read_heads(i):
                dve.wait_ge(attn_out, 2 * i + 2)
                dve.tensor_copy(q_n[:, 2 * i:2 * i + 2], aux[:, 3]).then_inc(attn_read, 2)

            def softmax(i):
                for e in range(2):
                    dve.wait_ge(attn_scores, 2 * i + (e + 1))
                    step(dve.tensor_reduce(peak[:, e], aux[:, e].rearrange("p (c s) -> p c s", c=2), AX.X, ALU.max))
                    step.wait()
                    dve.tensor_scalar(peak[:, e], peak[:, e], -QK_SCALE, None, ALU.mult).then_inc(attn_peak, 1)
                if i:
                    read_heads(i - 1)
                    stage_values(i)
                for e in range(2):
                    dve.wait_ge(attn_exp, 4 * i + (2 * e + 2))
                    step(dve.reciprocal(rows[:, e], rows[:, e]))
                    step.wait()
                    step(dve.tensor_scalar(prob[:, e, 0], prob[:, e, 0], rows[:, e, 0:1], None, ALU.mult))
                    step.wait()
                    dve.tensor_scalar(prob[:, e, 1], prob[:, e, 1], rows[:, e, 1:2], None, ALU.mult).then_inc(attn_prob, 1)

            def sine_argument(n):
                if n == 0:
                    dve.wait_ge(filt_loaded, 5 * 16)
                dve.wait_ge(filt_in, n + 1)
                step(dve.tensor_scalar(f_arg[:], aux[0:FILT, 1, 0:S], f_col[0:FILT, 2 * n:2 * n + 1],
                                       f_col[0:FILT, 2 * n + 1:2 * n + 2], ALU.add, ALU.mult))
                step.wait()
                step(dve.tensor_scalar(f_h[:], f_arg[:], 1.0 / (2.0 * np.pi), ROUNDER, ALU.mult, ALU.add))
                step.wait()
                step(dve.tensor_scalar(f_h[:], f_h[:], -ROUNDER, None, ALU.add))
                for part_ in TURN:
                    step.wait()
                    step(dve.scalar_tensor_tensor(f_arg[:], f_h[:], -part_, f_arg[:], ALU.mult, ALU.add))
                step.wait()
                dve.tensor_scalar(f_arg[:], f_arg[:], PI_BELOW, -PI_BELOW, ALU.min, ALU.max).then_inc(filt_arg, 1)

            def windowed(c):
                dve.wait_ge(filt_made, c + 1)
                dve.wait_ge(win_loaded[c], 16)
                step.wait()
                step(dve.tensor_tensor(f_sum[:, c], aux[:, 0:2], window[c][:], ALU.mult))
                step(dve.scalar_tensor_tensor(tmp[:], aux[:, 2:4], f_col[:, 4 + c:5 + c], window[c][:], ALU.mult, ALU.mult))
                step.wait()
                step(dve.tensor_tensor(f_dif[:, c], f_sum[:, c], tmp[:], ALU.subtract))
                step.wait()
                dve.tensor_tensor(f_sum[:, c], f_sum[:, c], tmp[:], ALU.add).then_inc(filt_win, 1)
                dve.wait_ge(filt_win, c + 1)

            def spectra(n):
                k, b = spec[:, :, n // 2, n % 2 * 512:n % 2 * 512 + 512], n % 2 * 2
                dve.wait_ge(k_copied, 4)
                dve.wait_ge(u_spec_made, n + 1)
                if n:
                    dve.wait_ge(spec_ready, n)
                step(dve.tensor_tensor(part[:, 0:2], k, aux[:, b:b + 2], ALU.mult))
                step(dve.tensor_tensor(part[:, 2], k[:, 0], aux[:, b + 1], ALU.mult))
                dve.tensor_tensor(part[:, 3], k[:, 1], aux[:, b], ALU.mult).then_inc(spec_used, 1)
                step.wait()
                step(dve.tensor_tensor(k[:, 0], part[:, 0], part[:, 1], ALU.subtract))
                dve.wait_ge(spec_used, n + 1)
                dve.tensor_tensor(k[:, 1], part[:, 2], part[:, 3], ALU.add).then_inc(spec_ready, 1)

            def convolved(c):
                dve.wait_ge(conv_made, c // 2 * 2 + 2)
                y = xh[:, 2 * HT + c]
                dve.scalar_tensor_tensor(y, y, column("hyena_bias", c), aux[:, c // 2, c % 2 * S:(c % 2 + 1) * S],
                                         ALU.mult, ALU.add).then_inc(conv_biased, 1)

            def gated_conv(a, b):
                step.wait()
                y = xh[:, 2 * HT + a:2 * HT + b]
                dve.tensor_tensor(y, y, xh[:, a:b], ALU.mult).then_inc(conv_done, 1)

            def half_variance(n):
                dve.wait_ge(mix_summed, n + 1)
                dve.tensor_scalar(scale2[:], aux[:, n, 0:S], 1.0 / HY, EPS, ALU.mult, ALU.add).then_inc(var_made, 1)

            def normed(g):
                for m in range(4 * g, 4 * g + 4):
                    dve.scalar_tensor_tensor(mix_f[:, m], xh[:, HT + m], column("hyena_out_gain", m - HT), tmp[:, 2],
                                             ALU.mult, ALU.mult).then_inc(op_f32, 1)

            def normed_low(g):
                dve.wait_ge(op_hi, V_MIX + 4 * g + 4)
                dve.wait_ge(op_f32, V_MIX + 4 * g + 4)
                dve.tensor_tensor(xa[:, 4 * g:4 * g + 4, S:2 * S], mix_f[:, 4 * g:4 * g + 4],
                                  xa[:, 4 * g:4 * g + 4, 0:S], ALU.subtract).then_inc(op_lo, 4)

            def mixer_part(s):
                if s == 0:
                    for n, (a, b) in enumerate(LATENTS):
                        dve.wait_ge(lat_summed, n + 1)
                        dve.tensor_scalar(lat_r[:, n], aux[:, n, 0:S], 1.0 / ((b - a) * P), EPS, ALU.mult, ALU.add).then_inc(var_made, 1)
                    dve.wait_ge(std_made, HEADS + 6)
                    step(dve.reciprocal(lat_r[:], lat_r[:]))
                if s == 1:
                    step.wait()
                    for n, (a, b) in enumerate(LATENTS):
                        for k in range(a, b):
                            gain = column("kv_norm_gain" if n else "q_norm_gain", k - a)
                            last = dve.scalar_tensor_tensor(lat[:, k], lat[:, k], gain, lat_r[:, n], ALU.mult, ALU.mult)
                            if k < b - 1:
                                step(last)
                        last.then_inc(lat_norm, 1)
                if s == 2:
                    for n, (a, b) in enumerate(LATENTS):
                        dst = ckv_s if n else cq_s
                        dve.wait_ge(lat_hi, n + 1)
                        step.wait()
                        dve.tensor_tensor(dst[:, :, S:2 * S], lat[:, a:b], dst[:, :, 0:S], ALU.subtract).then_inc(lat_lo, 1)
                if s == 4:
                    rotary()
                    stage_rotary(0)
                    stage_values(0)
                if 5 <= s < 13 and s % 2:
                    softmax((s - 5) // 2)
                if s in (6, 8, 10):
                    dve.wait_ge(attn_scores, s - 4)
                    stage_rotary((s - 4) // 2)
                if s in (8, 10):
                    sine_argument((s - 8) // 2)
                if s == 13:
                    read_heads(NH // 2 - 1)
                if s in (14, 15):
                    windowed(s - 14)
                if s == 16:
                    step.wait()
                    u = xh[:, 2 * HT:3 * HT]
                    dve.tensor_tensor(u, u, xh[:, HT:2 * HT], ALU.mult).then_inc(u_ready, 1)
                if s in (19, 20):
                    spectra(2 * (s - 19))
                    spectra(2 * (s - 19) + 1)
                if s in (21, 22):
                    if s == 21:
                        dve.wait_ge(u_ready, 1)
                    for c in range(4 * (s - 21), 4 * (s - 20)):
                        convolved(c)
                if s == 22:
                    dve.wait_ge(conv_biased, HT)
                    gated_conv(0, 6)
                    half_variance(0)
                if s == 23:
                    dve.wait_ge(x1_made, 4)
                    inverse_root(HEADS + 7, rstd1)
                    dve.engine_nop().then_inc(attn_factor, 1)
                if s == 24:
                    gated_conv(6, 8)
                    split(U_WO2 + 1)
                    dve.wait_ge(attn_normed, 2)
                    dve.engine_nop().then_inc(op_f32, HT)
                    normed_low(0)
                    half_variance(1)
                    normed_low(1)
                    dve.wait_ge(conv_done, 2)
                    inverse_root(HEADS + 8, tmp[:, 2])
                    normed(2)
                    normed(3)
                    normed_low(2)
                    normed_low(3)

            for n in range(3 * HT):
                u, t, k = hyena_unit(n)
                mixer_part(n)
                if n < 3 * HT - 1:
                    split(u + 2)
                total(t, 0)
                step(dve.tensor_tensor(tmp[:, 2], tmp[:, bank(t) % 2], rstd[:], ALU.mult))
                step.wait()
                step(dve.tensor_scalar(xh[:, k], tmp[:, 2], column("hyena_conv_w", k + 3 * HT), column("hyena_conv_b", k),
                                       ALU.mult, ALU.add))
                step.wait()
                step(dve.scalar_tensor_tensor(xh[:, k, 1:S], tmp[:, 2, 0:S - 1], column("hyena_conv_w", k),
                                              xh[:, k, 1:S], ALU.mult, ALU.add))
                step.wait()
                step(dve.scalar_tensor_tensor(xh[:, k, 0:S - 1], tmp[:, 2, 1:S], column("hyena_conv_w", k + 6 * HT),
                                              xh[:, k, 0:S - 1], ALU.mult, ALU.add))
                if n == N_HY - 1:
                    latent_projections()
            mixer_part(3 * HT)
            dve.wait_ge(op_lo, V_MIX + DT)
            dve.wait_ge(x1_made, 4)
            with step.loop(DT // 4, 8) as i:
                for j in range(4):
                    m, t, k = bass.ds(4 * i + j, 1), T_WO2 + j, 4 * i + j
                    total(t, 4 * i)
                    dve.tensor_copy(branch[:, m], tmp[:, bank(t) % 2]).then_inc(h_new, 1)
                    step(dve.tensor_scalar(pre_b[:, m], tmp[:, bank(t) % 2], column("post_mix_gain", k), column("pre_ffn_gain", k),
                                           ALU.mult, ALU.mult))
                    step(dve.tensor_scalar(pre_a[:, m], h[:, m], column("pre_ffn_gain", k), None, ALU.mult))
                    split(U_WO2 + j + 2, 4 * i)
            norm(4, HEADS + 9, aux[:, 0, 0:S], D)
            step(dve.reciprocal(r_post[:], scale2[:]))
            step.wait()
            dve.engine_nop().then_inc(post_ready, 1)
            def branch_scaled(g):
                b = pre_b[:, 4 * g:4 * g + 4]
                step(dve.tensor_tensor(b, b, over_tiles(r_post, 4), ALU.mult))

            def branch_added(g):
                step.wait()
                a, b = pre_a[:, 4 * g:4 * g + 4], pre_b[:, 4 * g:4 * g + 4]
                dve.tensor_tensor(a, a, b, ALU.add).then_inc(op_f32, 4)

            def second_low(g):
                dve.wait_ge(op_hi, V_PRE + 4 * g + 4)
                dve.wait_ge(op_f32, V_PRE + 4 * g + 4)
                dve.tensor_tensor(xa[:, 4 * g:4 * g + 4, S:2 * S], pre_a[:, 4 * g:4 * g + 4],
                                  xa[:, 4 * g:4 * g + 4, 0:S], ALU.subtract).then_inc(op_lo, 4)

            branch_scaled(0)
            branch_added(0)
            branch_scaled(1)
            second_low(0)
            branch_added(1)
            branch_scaled(2)
            second_low(1)
            branch_added(2)
            dve.wait_ge(pre_pool, 2)
            dve.engine_nop().then_inc(op_f32, 4)
            second_low(2)
            second_low(3)
            dve.wait_ge(branch_gained, DT)
            for g in range(2):
                hg, bg = h[:, 4 * g:4 * g + 4], branch[:, 4 * g:4 * g + 4]
                step(dve.tensor_tensor(bg, bg, over_tiles(r_post, 4), ALU.mult))
                step.wait()
                dve.tensor_tensor(hg, hg, bg, ALU.add).then_inc(x1_made, 1)
            split(U_FF2 + 2)
            split(U_FF2 + 3)
            norm(5, HEADS + 10, aux[:, 0, 0:S], D)
            step(dve.reciprocal(rstd[:], scale2[:]))
            step.wait()
            for g in range(GROUPS):
                u0, t0 = U_FF2 + g * FF_UNITS, T_FF2 + g * FF_TILES
                v0, g0 = V_FF2 + g * GT, G_FF2 + g * GT

                def gated(run, pairs, ahead=0):
                    for p in range(2):
                        u, t, m, k = u0 + 2 * p, t0 + 2 * p, bass.ds(pairs + p, 1), pairs + (g * GT + p)
                        if p or ahead < 1:
                            split(u + 2, run)
                        total(t, run, 2)
                        step(dve.tensor_tensor(tmp[:, 0:2], tmp[:, 0:2], rstd2, ALU.mult))
                        step.wait()
                        step(dve.tensor_scalar(tmp[:, 2], tmp[:, 0], column("ffn_conv_w", k + FT), column("ffn_conv_b", k), ALU.mult, ALU.add))
                        step.wait()
                        step(dve.scalar_tensor_tensor(tmp[:, 2, 1:S], tmp[:, 0, 0:S - 1], column("ffn_conv_w", k), tmp[:, 2, 1:S], ALU.mult, ALU.add))
                        step.wait()
                        dve.scalar_tensor_tensor(tmp[:, 2, 0:S - 1], tmp[:, 0, 1:S], column("ffn_conv_w", k + 2 * FT), tmp[:, 2, 0:S - 1],
                                                 ALU.mult, ALU.add).then_inc(gate_in, 1)
                        if p or ahead < 2:
                            split(u + 3, run)
                        dve.wait_ge(gate_out, pairs + (g0 + 1 + p))
                        dve.tensor_tensor(tmp[:, 3], tmp[:, 2], tmp[:, 1], ALU.mult).then_inc(op_f32, 1)
                        dve.wait_ge(op_hi, pairs + (v0 + 1 + p))
                        dve.tensor_tensor(hid[:, m, S:2 * S], tmp[:, 3], hid[:, m, 0:S], ALU.subtract).then_inc(op_lo, 1)

                if g == 0:
                    gated(0, 0, ahead=2)
                with step.loop(GT // 2 - 2 + g, 6, start=1 - g) as i:
                    gated(4 * i, 2 * i)
                gated(2 * GT - 4, GT - 2)
                u1, t1 = u0 + 2 * GT, t0 + 2 * GT

                def down(run, tiles):
                    for j in range(4):
                        t, m = t1 + j, bass.ds(tiles + j, 1)
                        split(u1 + 2 * j + 2, run)
                        if g == 0:
                            dve.wait_ge(small_made, tiles + (t + 1))
                            dve.tensor_tensor(ff_out[:, m], acc[:, bank(t), 0:S], small[:, bank(t) % 2], ALU.add).then_inc(acc_free, 1)
                        else:
                            total(t, tiles)
                            dve.tensor_tensor(ff_out[:, m], ff_out[:, m], tmp[:, bank(t) % 2], ALU.add).then_inc(h_new, 1)
                        split(u1 + 2 * j + 3, run)

                with dve.Fori(0, DT // 4 - 1) as i:
                    down(8 * i, 4 * i)
                down(2 * DT - 8, DT - 4)
            norm(6, HEADS + 11, aux[:, 0, 0:S], D)
            step(dve.reciprocal(rstd[:], scale2[:]))
            step.wait()
            dve.engine_nop().then_inc(out_factor, 1)
            for g in range(1, 4):
                dve.wait_ge(out_gained, 4 * g + 4)
                hg, bg = h[:, 4 * g:4 * g + 4], ff_out[:, 4 * g:4 * g + 4]
                step(dve.tensor_tensor(bg, bg, over_tiles(rstd, 4), ALU.mult))
                step.wait()
                dve.tensor_tensor(hg, hg, bg, ALU.add).then_inc(fin_sum, 1)

        @block.tensor
        def _(pe):
            def high(u, run, bnk, x, kt, k0=0, first=True, ready=None):
                pe.wait_ge(hi_made, run + (u + 1))
                for k in range(kt):
                    if ready and k in ready:
                        pe.wait_ge(op_lo, ready[k])
                    last = pe.matmul(acc[:, bnk], w_hi[:, u % SPLIT, k * P:(k + 1) * P], x[:, k0 + k],
                                     start=first and k == 0, stop=False)
                last.then_inc(hi_used, 1)

            def low(u, run, bnk, x, kt, k0=0, final=True):
                pe.wait_ge(lo_made, run + (u + 1))
                for k in range(kt):
                    last = pe.matmul(acc[:, bnk, S:2 * S], w_lo[:, u % SPLIT, k * P:(k + 1) * P], x[:, k0 + k, 0:S],
                                     start=False, stop=final and k == kt - 1)
                last.then_inc(lo_used, 1)

            def unit(u, run, t, trun, x, ready=None):
                pe.wait_ge(acc_free, trun + (t + 1))
                high(u, run, bank(t), x, DT, ready=ready)
                low(u, run, bank(t), x, DT)

            def first_two(u, t, x, v0, groups):
                for start, end in groups:
                    pe.wait_ge(op_lo, v0 + end)
                    for j in range(2):
                        if start == 0:
                            pe.wait_ge(acc_free, t + j + 1)
                            pe.wait_ge(hi_made, u + j + 1)
                        for k in range(start, end):
                            last = pe.matmul(acc[:, bank(t + j)], w_hi[:, (u + j) % SPLIT, k * P:(k + 1) * P], x[:, k],
                                             start=(k == 0), stop=False)
                        if end == DT:
                            last.then_inc(hi_used, 1)
                        if start == 0:
                            pe.wait_ge(lo_made, u + j + 1)
                        for k in range(start, end):
                            last = pe.matmul(acc[:, bank(t + j), S:2 * S], w_lo[:, (u + j) % SPLIT, k * P:(k + 1) * P],
                                             x[:, k, 0:S], start=False, stop=(k == DT - 1))
                        if end == DT:
                            last.then_inc(lo_used, 1)

            QUARTERS = ((0, 4), (4, 8), (8, 12), (12, 16))
            SINGLES = ((0, 12), (12, 14), (14, 15), (15, 16))

            def settle():
                pe.sem_inc(pe_settled, 1)

            def late(v0):
                return {0: v0 + 12, 12: v0 + 13, 13: v0 + 14, 14: v0 + 15, 15: v0 + 16}

            def column_sums(dst, tiles):
                for k, tile in enumerate(tiles):
                    last = pe.matmul(dst, ones[:], tile, start=(k == 0), stop=(k == len(tiles) - 1))
                return last

            unit(0, 0, 0, 0, xa, ready={4 * g: 4 * g + 4 for g in range(4)})
            unit(1, 0, 1, 0, xa)
            pe.wait_ge(consts_loaded, 5 * 16)
            pe.wait_ge(folded, 3)
            column_sums(aux[:, 0, 0:S], [sq_all[:, m] for m in range(4)]).then_inc(sums_done, 1)
            unit(2, 0, 2, 0, xa)
            pe.wait_ge(gkl_made, 1)
            for t in range(8):
                last = pe.matmul(aux[:, t // 2, t % 2 * S:(t % 2 + 1) * S], w_gk[:, t * P:(t + 1) * P], gkl[:],
                                 start=True, stop=True)
                if t % 2:
                    last.then_inc(gk_made, 1)

            unit(3, 0, 3, 0, xa)
            unit(4, 0, 4, 0, xa)
            with pe.Fori(1, 8) as i:
                for j in range(1, 5):
                    unit(j, 4 * i, j, 4 * i, xa)

            def turn_values(hd, half):
                for n in range(2):
                    for t in range(4):
                        c = (2 * half + n) * CH
                        last = pe.transpose(aux[0:CH, 2 + n, t * P:(t + 1) * P], v_s[:, t, c:c + CH], ident[:])
                last.then_inc(turned, 1)

            def head_part(hd, slot):
                if slot == 0:
                    pe.wait_ge(staged, hd * 3 + 3)
                    pe.wait_ge(var_made, hd + 1)
                    settle()
                    for n in range(NCH):
                        for t in range(2):
                            c = n % 2 * DK + t * P
                            last = pe.transpose(aux[0:CH, n // 2, c:c + P], ke_s[:, t, n * CH:(n + 1) * CH], ident[:])
                    last.then_inc(turned, 1)
                    pe.wait_ge(v_staged, hd + 1)
                    settle()
                    turn_values(hd, 0)
                if slot == 1:
                    pe.wait_ge(tok_made, hd * 3 + 2)
                    settle()
                    turn_values(hd, 1)
                    for n in range(NCH):
                        tok = slice(n * CH, (n + 1) * CH)
                        for t in range(2):
                            last = pe.matmul(aux[0:CH, 0, tok], k_s[:, t, tok], q_s[:, t, tok], start=(t == 0), stop=(t == 1))
                    last.then_inc(scores_made, 1)
                if 2 <= slot < 6:
                    n = slot - 2
                    tok = slice(n * CH, (n + 1) * CH)
                    if n:
                        pe.wait_ge(state_made, hd * 6 + 2 * n)
                    else:
                        pe.wait_ge(tok_made, hd * 3 + 3)
                    if n < NCH - 1:
                        for t in range(2):
                            last = pe.matmul(aux[:, 2 + t], ke_tok[:, n, t * P:(t + 1) * P], v_tok[:, n], start=True, stop=True)
                        last.then_inc(delta_made, 1)
                    if n == 0:
                        pe.wait_ge(masked, hd + 1)
                    elif n > 1:
                        pe.wait_ge(o_read, hd * NCH + (n - 1))
                    b = 1 - n % 2
                    for t in range(4):
                        for s_ in range(2 if n else 0):
                            pe.matmul(aux[:, b, t * CH:(t + 1) * CH], state[:, s_, t * P:(t + 1) * P], q_s[:, s_, tok],
                                      start=(s_ == 0), stop=False)
                        last = pe.matmul(aux[:, b, t * CH:(t + 1) * CH], v_tok[:, n, t * P:(t + 1) * P], sc[:, n],
                                         start=(n == 0), stop=True)
                    last.then_inc(o_made, 1)
                if slot == 6:
                    pe.wait_ge(o_squared, hd + 1)
                    for t in range(4):
                        last = pe.matmul(aux[:, 1, 0:S], ones[:], v_s[:, t], start=(t == 0), stop=(t == 3))
                    last.then_inc(head_done, 1)

            with pe.Fori(0, HEADS) as hd:
                for p in range(8):
                    head_part(hd, p)
                    for u in (U_CONV + 2 * p, U_CONV + 2 * p + 1):
                        unit(u, 16 * hd, u, 16 * hd, xa)

            with pe.Fori(0, DT // 2) as i:
                for j in range(4):
                    unit(U_OUT + j, 4 * i, U_OUT + j, 4 * i, xa)
            first_two(U_WO, U_WO, xb, DT, SINGLES)
            unit(U_WO + 2, 0, U_WO + 2, 0, xb)
            unit(U_WO + 3, 0, U_WO + 3, 0, xb)
            with pe.Fori(1, DT // 4) as i:
                for j in range(4):
                    unit(U_WO + j, 4 * i, U_WO + j, 4 * i, xb)
            for g in range(GROUPS):
                u0, t0 = U_FF1 + g * FF_UNITS, T_FF1 + g * FF_TILES
                if g == 0:
                    for j in range(4):
                        unit(u0 + j, 0, t0 + j, 0, xa, ready=late(2 * DT) if j == 0 else None)
                        if j == 0:
                            pe.wait_ge(pool_step, POOL_WO)
                            pe.matmul(aux[:, 0, 0:S], ones[:], ssum[:], start=True, stop=True).then_inc(sums_done, 1)
                first = 1 if g == 0 else 0
                with pe.Fori(first, GT // 2) as i:
                    for j in range(4):
                        unit(u0 + j, 4 * i, t0 + j, 4 * i, xa)
                u1, t1, v1 = u0 + 2 * GT, t0 + 2 * GT, 3 * DT + g * GT
                with pe.Fori(0, DT // 4) as i:
                    for j in range(4):
                        u, b = u1 + 2 * j, bank(t1 + j)
                        pe.wait_ge(acc_free, 4 * i + (t1 + j + 1))
                        for half in range(2):
                            ready = {0: v1 + KD} if half == 0 else {0: v1 + 2 * KD - 1, KD - 1: v1 + 2 * KD}
                            high(u + half, 8 * i, b, hid, KD, half * KD, half == 0, ready if j == 0 else None)
                            low(u + half, 8 * i, b, hid, KD, half * KD, half == 1)

            for j in range(U_HY - U_LAT):
                unit(U_LAT + j, 0, T_LAT + j, 0, xa, ready=None if j else late(V_LAT))
                if j == 0:
                    pe.wait_ge(pool_step, POOL_FF1)
                    column_sums(aux[:, 0, 0:S], [ssum[:]])
                    column_sums(aux[:, 0, S:2 * S], [ssum2[:]]).then_inc(sums_done, 1)

            def latent_projections():
                t = T_UQ
                for u in range(U_UQ, U_UV):
                    x, kt = (cq_s, QT) if u < U_UK else (ckv_s, KVT)
                    pe.wait_ge(lat_lo, 1 if u < U_UK else 2)
                    pe.wait_ge(hi_made, u + 1)
                    for c in range(4):
                        pe.wait_ge(acc_free, t + c + 1)
                        for k in range(kt):
                            w = slice(k * 512 + c * P, k * 512 + (c + 1) * P)
                            last = pe.matmul(acc[:, bank(t + c)], w_hi[:, u % SPLIT, w], x[:, k], start=(k == 0), stop=False)
                    last.then_inc(hi_used, 1)
                    pe.wait_ge(lo_made, u + 1)
                    for c in range(4):
                        for k in range(kt):
                            w = slice(k * 512 + c * P, k * 512 + (c + 1) * P)
                            last = pe.matmul(acc[:, bank(t + c), S:2 * S], w_lo[:, u % SPLIT, w], x[:, k, 0:S],
                                             start=False, stop=(k == kt - 1))
                        last.then_inc(lo_used if c == 3 else quarter_made, 1)
                    t += 4
                for u in range(U_UV, U_HY2):
                    pe.wait_ge(acc_free, t + 2)
                    pe.wait_ge(hi_made, u + 1)
                    for c in range(2):
                        for k in range(KVT):
                            for half in range(2):
                                x = ckv_s[:, k, half * S + c * P:half * S + (c + 1) * P]
                                last = pe.matmul(acc[:, bank(t + c)], x, w_hi[:, u % SPLIT, k * 512:(k + 1) * 512],
                                                 start=(k == 0 and half == 0), stop=False)
                    last.then_inc(hi_used, 1)
                    pe.wait_ge(lo_made, u + 1)
                    for c in range(2):
                        for k in range(KVT):
                            last = pe.matmul(acc[:, bank(t + c)], ckv_s[:, k, c * P:(c + 1) * P],
                                             w_lo[:, u % SPLIT, k * 512:(k + 1) * 512], start=False, stop=(k == KVT - 1))
                    last.then_inc(lo_used, 1)
                    t += 2

            def rotation():
                pe.wait_ge(tables_loaded, 32)
                pe.wait_ge(acc_free, T_UK + 4)
                pe.wait_ge(lat_f32, QT + KVT + 1)
                for k in range(NH // 2):
                    last = pe.matmul(aux[:, k // 2, k % 2 * S:(k % 2 + 1) * S], rot[:], q_p[:, k], start=True, stop=True)
                last.then_inc(rotated, 1)
                pe.matmul(aux[:, 2, 0:S], rot[:], k_p[:, 0], start=True, stop=True).then_inc(rotated, 1)

            def scores(i):
                pe.wait_ge(roped, 2)
                pe.wait_ge(head_q, 2 * i + 2)
                pe.wait_ge(head_rot, i + 1)
                if i >= 2:
                    pe.wait_ge(filt_arg, i - 1)
                for e in range(2):
                    for c in range(2):
                        dst = aux[:, e, c * S:(c + 1) * S]
                        q, r = slice(c * P, (c + 1) * P), slice(e * ROPE, (e + 1) * ROPE)
                        pe.matmul(dst, qh[:, e, q], kh[:, e], start=True, stop=False)
                        last = pe.matmul(dst, qph[r, q], k_p[r, 0], start=False, stop=True)
                    last.then_inc(attn_scores, 1)

            def turn_probabilities(i):
                for e in range(2):
                    pe.wait_ge(attn_prob, 2 * i + (e + 1))
                    for c in range(2):
                        for k in range(2):
                            last = pe.transpose(aux[:, 2 - 2 * e, k * S + c * P:k * S + (c + 1) * P],
                                                prob[:, e, c, k * P:(k + 1) * P], ident[:])
                    last.then_inc(attn_turned, 1)

            def weighted_values(i):
                pe.wait_ge(head_v, i + 1)
                if i:
                    pe.wait_ge(attn_read, 2 * i)
                for e in range(2):
                    pe.wait_ge(attn_probt, 2 * i + (e + 1))
                    for k in range(2):
                        last = pe.matmul(aux[:, 3, e * S:(e + 1) * S], vh[:, k, e * P:(e + 1) * P], prob_t[:, e, k],
                                         start=(k == 0), stop=(k == 1))
                    last.then_inc(attn_out, 1)

            def spectrum(n, inputs, made):
                f, cols = slice(n // 2 * P, (n // 2 + 1) * P), slice(n % 2 * 512, n % 2 * 512 + 512)
                for table, x in enumerate(inputs):
                    for c in range(2):
                        last = pe.matmul(aux[:, n % 2 * 2 + table], dft[:, table, c, f], x[:, c, cols], start=(c == 0), stop=(c == 1))
                last.then_inc(made, 1)

            def mixer_part(s):
                if s == 0:
                    for n, (a, b) in enumerate(LATENTS):
                        pe.wait_ge(lat_squared, b)
                        column_sums(aux[:, n, 0:S], [mix_sq[:, k] for k in range(a, b)]).then_inc(lat_summed, 1)
                if s == 4:
                    rotation()
                if 7 <= s <= 13 and s % 2:
                    weighted_values((s - 7) // 2)
                if 5 <= s < 13:
                    if s % 2:
                        scores((s - 5) // 2)
                    else:
                        turn_probabilities((s - 6) // 2)
                if s == 8:
                    pe.wait_ge(filt_loaded, 5 * 16)
                    pe.matmul(aux[0:FILT, 1, 0:S], w_f1[:], f_in[:], start=True, stop=True).then_inc(filt_in, 1)
                if s == 10:
                    pe.wait_ge(filt_sin, 1)
                    pe.matmul(aux[0:FILT, 1, 0:S], w_f2[:], f_h[:], start=True, stop=True).then_inc(filt_in, 1)
                if s in (14, 15):
                    c = s - 14
                    if c == 0:
                        pe.wait_ge(filt_sin, 2)
                        pe.wait_ge(attn_read, NH)
                    else:
                        pe.wait_ge(filt_win, 1)
                    for n in range(4):
                        last = pe.matmul(aux[:, n], f_h[:, c * P:(c + 1) * P], w_f3[:, n * 512:(n + 1) * 512], start=True, stop=True)
                    last.then_inc(filt_made, 1)
                if s in (16, 17):
                    for n in (2 * (s - 16), 2 * (s - 16) + 1):
                        if s == 16:
                            pe.wait_ge(filt_win, 2)
                            pe.wait_ge(dft_loaded, 32)
                        else:
                            pe.wait_ge(k_copied, n - 1)
                        spectrum(n, (f_sum, f_dif), k_spec_made)
                if s == 18:
                    pe.wait_ge(k_copied, 4)
                    pe.wait_ge(u_ready, 1)
                    for c in range(2):
                        for k in range(HT):
                            last = pe.transpose(aux[:, 2 * c + k // 4, k % 4 * P:(k % 4 + 1) * P],
                                                xh[:, 2 * HT + k, c * P:(c + 1) * P], ident[:])
                        last.then_inc(u_turned, 1)
                if s in (19, 20):
                    for n in (2 * (s - 19), 2 * (s - 19) + 1):
                        if s == 19:
                            pe.wait_ge(u_copied, 2)
                        else:
                            pe.wait_ge(spec_used, n - 1)
                        spectrum(n, (u_tok, u_tok), u_spec_made)
                if s in (21, 22):
                    pe.wait_ge(spec_ready, 4)
                    for c in range(4 * (s - 21), 4 * (s - 20)):
                        for q in range(4):
                            r, f = q // 2, q % 2
                            last = pe.matmul(aux[:, c // 2, c % 2 * S:(c % 2 + 1) * S], spec[:, r, f, c * P:(c + 1) * P],
                                             idft[:, r, f], start=(q == 0), stop=(q == 3))
                        last.then_inc(conv_made, 1)
                if s == 22:
                    pe.wait_ge(conv_biased, 4)
                    pe.wait_ge(mix_squared, 1)
                    column_sums(aux[:, 0, 0:S], [mix_sq2[:, HT + k] for k in range(HT)]).then_inc(mix_summed, 1)
                if s == 24:
                    for k in range(HT):
                        pe.wait_ge(mix_squared, 2 if k < 6 else 3)
                        last = pe.matmul(aux[:, 1, 0:S], ones[:], mix_sq2[:, k], start=(k == 0), stop=(k == HT - 1))
                    last.then_inc(mix_summed, 1)

            for n in range(3 * HT):
                u, t, _ = hyena_unit(n)
                mixer_part(n)
                unit(u, 0, t, 0, xa)
                if n == N_HY - 1:
                    latent_projections()
            mixer_part(3 * HT)
            first_two(U_WO2, T_WO2, xa, V_MIX, QUARTERS)
            unit(U_WO2 + 2, 0, T_WO2 + 2, 0, xa)
            unit(U_WO2 + 3, 0, T_WO2 + 3, 0, xa)
            with pe.Fori(1, DT // 4) as i:
                for j in range(4):
                    unit(U_WO2 + j, 4 * i, T_WO2 + j, 4 * i, xa)
            pe.wait_ge(pool_step, POOL_WO2)
            column_sums(aux[:, 0, 0:S], [ssum[:]]).then_inc(sums_done, 1)
            for g in range(GROUPS):
                u0, t0 = U_FF2 + g * FF_UNITS, T_FF2 + g * FF_TILES
                if g == 0:
                    first_two(u0, t0, xa, V_PRE, QUARTERS)
                    unit(u0 + 2, 0, t0 + 2, 0, xa)
                    pe.wait_ge(folded, 6)
                    column_sums(aux[:, 0, 0:S], [late_sqs[:, k] for k in range(12, 16)]).then_inc(sums_done, 1)
                    unit(u0 + 3, 0, t0 + 3, 0, xa)
                with pe.Fori(1 - g, GT // 2) as i:
                    for j in range(4):
                        unit(u0 + j, 4 * i, t0 + j, 4 * i, xa)
                u1, t1, v1 = u0 + 2 * GT, t0 + 2 * GT, V_FF2 + g * GT
                with pe.Fori(0, DT // 4) as i:
                    for j in range(4):
                        u, b = u1 + 2 * j, bank(t1 + j)
                        pe.wait_ge(acc_free, 4 * i + (t1 + j + 1))
                        for half in range(2):
                            ready = {0: v1 + KD} if half == 0 else {0: v1 + 2 * KD - 1, KD - 1: v1 + 2 * KD}
                            high(u + half, 8 * i, b, hid, KD, half * KD, half == 0, ready if j == 0 else None)
                            low(u + half, 8 * i, b, hid, KD, half * KD, half == 1)
            pe.wait_ge(pool_step, POOL_WO2 + 1 + 2 * DT)
            column_sums(aux[:, 0, 0:S], [ssum[:]]).then_inc(sums_done, 1)


def _layout(i):
    f = np.ascontiguousarray
    def blocks(w, cols=P):
        k, c = w.shape
        w = w.reshape(k // P, P, c // cols, cols).transpose(2, 1, 0, 3)
        return f(w).reshape(c // cols, P, k // P * cols)
    def columns(*vs):
        return [v.reshape(-1, P).T for v in vs]
    def halves(w):
        w = w.reshape(GROUPS, 2, KD, P, DT, P).transpose(0, 4, 1, 3, 2, 5)
        return f(w).reshape(GROUPS, 2 * DT, P, KD * P)
    def paired(w):
        w = blocks(w)
        return f(np.stack([w[:FT], w[FT:]], 1)).reshape(GROUPS, 2 * GT, P, D)
    w = i["w_in"][0]
    ends = np.cumsum([0, 1024, 1024, D, D, RANK, D, D, D, D, D])
    q, k, v, g_out, gk, gate_b, gate_c, xc, merge_a, merge_b = (w[:, a:b] for a, b in zip(ends[:-1], ends[1:]))
    gk = np.pad(gk, ((0, 0), (0, P - RANK)))
    conv = np.stack([blocks(x) for x in (gate_c, xc, gate_b, merge_b)], 1).reshape(-1, P, D)
    outs = np.stack([blocks(x) for x in (g_out, merge_a)], 1).reshape(-1, P, D)
    qk = np.stack([blocks(x).reshape(HEADS, 2, P, D) for x in (q, k)], 1).reshape(-1, P, D)
    w2 = i["w_in_2"][0]
    w2 = np.concatenate([w2[:, 3 * HY:], w2[:, -ROPE:], w2[:, HY:3 * HY], w2[:, :HY]], 1)
    uq = i["w_uq_2"][0].reshape(LQ, NH, P + ROPE)
    uq = np.concatenate([uq[:, :, :P].reshape(LQ, -1), uq[:, :, P:].reshape(LQ, -1)], 1)
    ukv = i["w_ukv_2"][0].reshape(LKV, NH, 2 * P)
    ukv = np.concatenate([ukv[:, :, :P].reshape(LKV, -1), ukv[:, :, P:].reshape(LKV, -1)], 1)
    f32 = np.float32
    tok = np.arange(S)
    inv_freq = (1.0 / (f32(10000.0) ** (np.arange(0, ROPE, 2, dtype=f32) / f32(ROPE)))).astype(f32)
    ang = tok.astype(f32)[:, None] * inv_freq[None, :]
    ang = np.tile(ang, (1, 4)).T
    rope = np.stack([np.cos(ang), np.sin(ang)], 1).astype(f32)
    rot = np.zeros((P, P), f32)
    for m in range(P):
        if m % ROPE < ROPE // 2:
            rot[m + ROPE // 2, m] = -1
        else:
            rot[m - ROPE // 2, m] = 1
    bands = (EMB - 1) // 2
    t = np.linspace(0.0, 1.0, S, dtype=f32)[:, None]
    wv = (f32(2.0 * np.pi) * tok.astype(f32) / f32(S)).astype(f32)
    fr = np.linspace(1e-4, bands - 1, bands, dtype=f32)
    za = wv[:, None] * fr[None, :]
    f_in = np.concatenate([t, np.cos(za), -np.sin(za)], 1).T.astype(f32)
    lo, hi = np.log(1e-2) / 1.5, np.log(1e-2) / 0.3
    deltas = np.abs(np.linspace(lo, hi, HY, dtype=f32))
    window = (np.exp(-t * deltas[None, :]) + f32(0.05)).astype(f32).reshape(2, P, HY).transpose(1, 0, 2)
    om = np.pi * (2 * np.arange(S) + 1) / (2 * S)
    table = np.stack([np.cos(tok[:, None] * om[None, :]), np.sin(tok[:, None] * om[None, :])])
    dft = table.reshape(2, 2, P, S).transpose(2, 0, 1, 3).astype(f32)
    idft = (table.transpose(0, 2, 1) / S).reshape(2, 2, P, S).transpose(2, 0, 1, 3).astype(f32)
    lag0 = np.ones((P, 2), f32)
    lag0[0, 0] = 0
    f_col = np.zeros((P, 4), f32)
    for n, name in enumerate(("filt_b1_2", "filt_freq1_2", "filt_b2_2", "filt_freq2_2")):
        f_col[:FILT, n] = i[name][0]
    reset = np.ones((P, S), f32)
    reset[:, ::CH] = 0
    return {
        "x": i["x"][0].T.reshape(DT, P, S).transpose(1, 0, 2),
        "w_in": np.concatenate([blocks(gk), qk, blocks(v), conv, outs]),
        "w_out": blocks(i["w_out"][0]),
        "w_gate_up": paired(i["w_gate_up"][0]), "w_down": halves(i["w_down"][0]),
        "w_gk_up": i["w_gk_up"][0],
        "w_in_2": blocks(w2), "w_uq": blocks(uq, 512), "w_ukv": blocks(ukv, 512),
        "w_out_2": blocks(np.concatenate([i["w_out_2"][0][HY:], i["w_out_2"][0][:HY]])),
        "w_up": paired(i["w_up_2"][0]), "w_down_2": halves(i["w_down_2"][0]),
        "vec": np.concatenate(columns(*(i[n] for n in (
            "mix_norm_w", "ffn_norm_w", "final_norm_w", "gla_norm_w", "b_gk_up", "conv_w", "pre_mix_gain_2",
            "hyena_conv_w_2", "hyena_conv_b_2", "hyena_bias_2", "q_norm_gain_2", "kv_norm_gain_2", "hyena_out_gain_2",
            "attn_out_gain_2", "post_mix_gain_2", "pre_ffn_gain_2", "ffn_conv_w_2", "ffn_conv_b_2", "post_ffn_gain_2"))), 1),
        "ident": np.eye(P, dtype=f32), "ones": np.ones((P, P), f32),
        "mask": np.triu(np.ones((CH, CH), f32)), "reset": reset,
        "rope": rope, "rot": rot, "dft": dft, "idft": idft, "window": window, "f_in": f_in,
        "w_f1": i["filt_w1_2"][0], "w_f2": i["filt_w2_2"][0], "w_f3": i["filt_w3_2"][0],
        "f_col": np.concatenate([f_col, lag0], 1),
    }


def kernel(**inputs):
    import concourse.bacc as bacc
    from concourse.bass_utils import run_bass_kernel_spmd

    nc = bacc.Bacc("TRN2", target_bir_lowering=False, num_devices=1)
    arrays, aps = {}, {}
    for name, a in _layout({n: np.asarray(v) for n, v in inputs.items()}).items():
        a = np.ascontiguousarray(a)
        arrays[f"in_{name}"] = a
        aps[name] = nc.dram_tensor(f"in_{name}", a.shape, mybir.dt.from_np(a.dtype), kind="ExternalInput").ap()
    out = nc.dram_tensor("out", (P, DT, S), F32, kind="ExternalOutput").ap()
    build_program(nc, aps, out)
    result = run_bass_kernel_spmd(nc, [arrays], core_ids=[0]).results[0]["out"]
    return np.ascontiguousarray(np.asarray(result).transpose(2, 1, 0).reshape(1, S, D))
```
